# Optimizing a Trainium2 kernel written in Bass

```python
import math
import jax, jax.numpy as jnp
from jax import lax
import numpy as np

D_MODEL = 1024
BATCH = 1
SEQ = 256
DEPTH = 2

N_MIXERS = 2
N_META = 16
GDN_HEADS = 8
GDN_HEAD_DIM = 128
GDN_WIDTH = GDN_HEADS * GDN_HEAD_DIM
GDN_CONV = 4
CHUNK = 64
META_PAD = (-N_META) % CHUNK
SC_WIDTH = D_MODEL
SC_CONV = 3
D_FF = 2816
FFN_CONV = 3
N_LAYERS_A = (DEPTH + 1) // 2
N_LAYERS_B = DEPTH // 2
ALPHA = (2.0 * DEPTH) ** 0.25
BETA_INIT = (8.0 * DEPTH) ** -0.25
LN_EPS = 1e-5
RMS_EPS = 1e-6
L2_EPS = 1e-6


def causal_dwconv(x, w):
    width, ch = w.shape
    return lax.conv_general_dilated(
        x, w[:, None, :].astype(x.dtype), window_strides=(1,), padding=[(width - 1, 0)],
        dimension_numbers=("NWC", "WIO", "NWC"), feature_group_count=ch)

def layer_norm(x, g, b):
    xf = x.astype(jnp.float32)
    mu = jnp.mean(xf, axis=-1, keepdims=True)
    var = jnp.mean(jnp.square(xf - mu), axis=-1, keepdims=True)
    y = (xf - mu) * lax.rsqrt(var + LN_EPS) * g.astype(jnp.float32) + b.astype(jnp.float32)
    return y.astype(x.dtype)

def l2norm(x):
    return x * lax.rsqrt(jnp.sum(x * x, axis=-1, keepdims=True) + L2_EPS)

def chunk_gated_delta_rule(q, k, v, g, beta):
    bsz, t_len, h, dk = q.shape
    n = t_len // CHUNK

    def to_chunks(t):
        return jnp.transpose(t.reshape(bsz, n, CHUNK, h, -1), (0, 3, 1, 2, 4))

    q, k, v = to_chunks(q), to_chunks(k), to_chunks(v)
    g = jnp.transpose(g.reshape(bsz, n, CHUNK, h), (0, 3, 1, 2))
    beta = jnp.transpose(beta.reshape(bsz, n, CHUNK, h), (0, 3, 1, 2))
    g = jnp.cumsum(g, axis=-1)

    causal = jnp.tril(jnp.ones((CHUNK, CHUNK), dtype=bool))
    strict = jnp.tril(jnp.ones((CHUNK, CHUNK), dtype=bool), -1)
    decay = jnp.exp(jnp.where(causal, g[..., :, None] - g[..., None, :], -jnp.inf))

    k_beta = k * beta[..., None]
    v_beta = v * beta[..., None]
    m = jnp.where(strict, jnp.einsum("bhnid,bhnjd->bhnij", k_beta, k) * decay, 0.0)
    a_mat = jnp.eye(CHUNK, dtype=q.dtype) + m
    u = lax.linalg.triangular_solve(a_mat, v_beta, left_side=True, lower=True)
    w = lax.linalg.triangular_solve(a_mat, k_beta * jnp.exp(g)[..., None], left_side=True, lower=True)

    qk = jnp.einsum("bhnid,bhnjd->bhnij", q, k) * decay
    q_g = q * jnp.exp(g)[..., None]
    g_last = g[..., -1]
    k_dec = k * jnp.exp(g_last[..., None] - g)[..., None]

    def step(state, inp):
        qg_i, kd_i, u_i, w_i, qk_i, gl_i = inp
        v_new = u_i - jnp.einsum("bhcd,bhde->bhce", w_i, state)
        o_i = jnp.einsum("bhcd,bhde->bhce", qg_i, state) + jnp.einsum("bhij,bhje->bhie", qk_i, v_new)
        state = state * jnp.exp(gl_i)[..., None, None] + jnp.einsum("bhcd,bhce->bhde", kd_i, v_new)
        return state, o_i

    xs = tuple(jnp.moveaxis(t, 2, 0) for t in (q_g, k_dec, u, w, qk, g_last))
    state0 = jnp.zeros((bsz, h, dk, v.shape[-1]), dtype=q.dtype)
    _, o = lax.scan(step, state0, xs)
    return jnp.transpose(o, (1, 0, 3, 2, 4)).reshape(bsz, t_len, h, -1)

def gated_deltanet(h, w_in, conv_w, a_log, dt_bias, norm_w, w_out):
    bsz, seq_len, _ = h.shape
    proj = h @ w_in
    qkv, z, b_raw, a_raw = jnp.split(
        proj, [3 * GDN_WIDTH, 4 * GDN_WIDTH, 4 * GDN_WIDTH + GDN_HEADS], axis=-1)
    qkv = jax.nn.silu(causal_dwconv(qkv, conv_w))
    q, k, v = [t.reshape(bsz, seq_len, GDN_HEADS, GDN_HEAD_DIM).astype(jnp.float32)
               for t in jnp.split(qkv, 3, axis=-1)]
    q = l2norm(q) * (GDN_HEAD_DIM ** -0.5)
    k = l2norm(k)
    beta = jax.nn.sigmoid(b_raw.astype(jnp.float32))
    g = -jnp.exp(a_log.astype(jnp.float32)) * jax.nn.softplus(
        a_raw.astype(jnp.float32) + dt_bias.astype(jnp.float32))
    pad4 = ((0, 0), (META_PAD, 0), (0, 0), (0, 0))
    pad3 = ((0, 0), (META_PAD, 0), (0, 0))
    o = chunk_gated_delta_rule(jnp.pad(q, pad4), jnp.pad(k, pad4), jnp.pad(v, pad4),
                               jnp.pad(g, pad3), jnp.pad(beta, pad3))[:, META_PAD:]
    o = o * lax.rsqrt(jnp.mean(o * o, axis=-1, keepdims=True) + RMS_EPS) * norm_w.astype(jnp.float32)
    o = o * jax.nn.silu(z.reshape(bsz, seq_len, GDN_HEADS, GDN_HEAD_DIM).astype(jnp.float32))
    return o.reshape(bsz, seq_len, GDN_WIDTH).astype(h.dtype) @ w_out

def short_conv_mixer(h, w_in, conv_w, w_out):
    b_gate, c_gate, xv = jnp.split(h @ w_in, 3, axis=-1)
    u = causal_dwconv(c_gate * xv, conv_w)
    return (b_gate * u) @ w_out

def conv_ffn(h, w_up, conv_w, w_down):
    u, gate = jnp.split(h @ w_up, 2, axis=-1)
    u = causal_dwconv(u, conv_w)
    return (jax.nn.silu(u) * gate) @ w_down

def first_inputs(seed: int = 0) -> dict:
    key = jax.random.key(seed)
    ks = iter(jax.random.split(key, 32))
    f32 = jnp.float32

    def nrm(shape, scale):
        return jax.random.normal(next(ks), shape, f32) * scale

    a_in_cols = 4 * GDN_WIDTH + 2 * GDN_HEADS
    dt = jnp.exp(jax.random.uniform(next(ks), (N_LAYERS_A, GDN_HEADS), f32,
                                    math.log(1e-3), math.log(1e-1)))
    return {
        "x": nrm((BATCH, SEQ, D_MODEL), 1.0),
        "meta": nrm((N_META, D_MODEL), 1.0),
        "a_w_in": nrm((N_LAYERS_A, D_MODEL, a_in_cols), D_MODEL ** -0.5),
        "a_conv": nrm((N_LAYERS_A, GDN_CONV, 3 * GDN_WIDTH), GDN_CONV ** -0.5),
        "a_log": jnp.log(jax.random.uniform(next(ks), (N_LAYERS_A, GDN_HEADS), f32, 1.0, 16.0)),
        "a_dt_bias": dt + jnp.log(-jnp.expm1(-dt)),
        "a_norm": 1.0 + nrm((N_LAYERS_A, GDN_HEAD_DIM), 0.02),
        "a_w_out": nrm((N_LAYERS_A, GDN_WIDTH, D_MODEL), BETA_INIT * GDN_WIDTH ** -0.5),
        "b_w_in": nrm((N_LAYERS_B, D_MODEL, 3 * SC_WIDTH), D_MODEL ** -0.5),
        "b_conv": nrm((N_LAYERS_B, SC_CONV, SC_WIDTH), SC_CONV ** -0.5),
        "b_w_out": nrm((N_LAYERS_B, SC_WIDTH, D_MODEL), BETA_INIT * SC_WIDTH ** -0.5),
        "ln_mix_g": 1.0 + nrm((DEPTH, D_MODEL), 0.02),
        "ln_mix_b": nrm((DEPTH, D_MODEL), 0.02),
        "ffn_w_up": nrm((DEPTH, D_MODEL, 2 * D_FF), D_MODEL ** -0.5),
        "ffn_conv": nrm((DEPTH, FFN_CONV, D_FF), FFN_CONV ** -0.5),
        "ffn_w_down": nrm((DEPTH, D_FF, D_MODEL), BETA_INIT * D_FF ** -0.5),
        "ln_ffn_g": 1.0 + nrm((DEPTH, D_MODEL), 0.02),
        "ln_ffn_b": nrm((DEPTH, D_MODEL), 0.02),
    }

def first_block(x, meta, a_w_in, a_conv, a_log, a_dt_bias, a_norm, a_w_out,
              b_w_in, b_conv, b_w_out, ln_mix_g, ln_mix_b,
              ffn_w_up, ffn_conv, ffn_w_down, ln_ffn_g, ln_ffn_b):
    bsz = x.shape[0]
    h = jnp.concatenate(
        [jnp.broadcast_to(meta.astype(x.dtype)[None], (bsz, N_META, D_MODEL)), x], axis=1)
    for i in range(DEPTH):
        j = i // N_MIXERS
        if i % N_MIXERS == 0:
            mix = gated_deltanet(h, a_w_in[j], a_conv[j], a_log[j], a_dt_bias[j], a_norm[j], a_w_out[j])
        else:
            mix = short_conv_mixer(h, b_w_in[j], b_conv[j], b_w_out[j])
        h = layer_norm(ALPHA * h + mix, ln_mix_g[i], ln_mix_b[i])
        h = layer_norm(ALPHA * h + conv_ffn(h, ffn_w_up[i], ffn_conv[i], ffn_w_down[i]),
                       ln_ffn_g[i], ln_ffn_b[i])
    return h[:, N_META:]


Q_BLOCK = 128
P_DIM = 256
MLA_HEADS = 8
MLA_NOPE = 64
MLA_ROPE = 32
MLA_V = 64
Q_LORA = 256
KV_LORA = 256
ROPE_BASE = 10000.0
SB_HEADS = 8
SB_DIM = 64
FOX_HEADS = 16
FOX_DIM = 64
D_FF_2 = ((-(-8 * D_MODEL // 3)) + 255) // 256 * 256
DEEPNORM_ALPHA = (2.0 * DEPTH) ** 0.25
DEEPNORM_BETA = (8.0 * DEPTH) ** -0.25
N_EVEN = (DEPTH + 1) // 2
N_ODD = DEPTH // 2
IN_A = Q_LORA + KV_LORA + MLA_ROPE
IN_B = 3 * SB_HEADS * SB_DIM
IN_C = 3 * FOX_HEADS * FOX_DIM + FOX_HEADS
MIX_A = MLA_HEADS * MLA_V + SB_HEADS * SB_DIM
MIX_C = FOX_HEADS * FOX_DIM


def layer_norm_2(x, g, b, eps=1e-5):
    xf = x.astype(jnp.float32)
    mu = jnp.mean(xf, -1, keepdims=True)
    var = jnp.mean(jnp.square(xf - mu), -1, keepdims=True)
    return ((xf - mu) * lax.rsqrt(var + eps) * g + b).astype(x.dtype)

def rms_norm(x, g, eps=1e-6):
    xf = x.astype(jnp.float32)
    return (xf * lax.rsqrt(jnp.mean(jnp.square(xf), -1, keepdims=True) + eps) * g).astype(x.dtype)

def rope_tables(seq, dim):
    inv = 1.0 / (ROPE_BASE ** (jnp.arange(0, dim, 2, dtype=jnp.float32) / dim))
    ang = jnp.arange(seq, dtype=jnp.float32)[:, None] * inv[None, :]
    return jnp.cos(ang), jnp.sin(ang)

def apply_rope(x, cos, sin):
    x1, x2 = jnp.split(x, 2, axis=-1)
    return jnp.concatenate([x1 * cos - x2 * sin, x1 * sin + x2 * cos], -1).astype(x.dtype)

def sweep_query_blocks(block_fn, q):
    b, h, s, d = q.shape
    nb = s // Q_BLOCK
    q_blocks = q.reshape(b, h, nb, Q_BLOCK, d).transpose(2, 0, 1, 3, 4)
    out = lax.map(lambda a: block_fn(a[0], a[1]), (q_blocks, jnp.arange(nb)))
    dv = out.shape[-1]
    return out.transpose(1, 0, 3, 2, 4).reshape(b, s, h * dv)

def mla_block(q_blk, blk, k, v):
    t = blk * Q_BLOCK + jnp.arange(Q_BLOCK)
    s = jnp.arange(k.shape[2])
    allowed = (s[None, :] // CHUNK) <= (t[:, None] // CHUNK)
    logits = jnp.einsum('bhqd,bhkd->bhqk', q_blk, k).astype(jnp.float32) * (MLA_NOPE + MLA_ROPE) ** -0.5
    w = jax.nn.softmax(jnp.where(allowed, logits, -jnp.inf), axis=-1)
    return jnp.einsum('bhqk,bhkd->bhqd', w.astype(v.dtype), v)

def stick_breaking_block(q_blk, blk, k, v):
    t = blk * Q_BLOCK + jnp.arange(Q_BLOCK)
    s = jnp.arange(k.shape[2])
    past = s[None, :] < t[:, None]
    z = jnp.einsum('bhqd,bhkd->bhqk', q_blk, k).astype(jnp.float32) * SB_DIM ** -0.5
    log_beta = jax.nn.log_sigmoid(z)
    log_rem = jnp.where(past, jax.nn.log_sigmoid(-z), 0.0)
    between = lax.cumsum(log_rem, axis=3, reverse=True) - log_rem
    att = jnp.where(past, jnp.exp(log_beta + between), 0.0)
    return jnp.einsum('bhqk,bhkd->bhqd', att.astype(v.dtype), v)

def forgetting_block(q_blk, blk, k, v, dcum):
    t = blk * Q_BLOCK + jnp.arange(Q_BLOCK)
    s = jnp.arange(k.shape[2])
    causal = s[None, :] <= t[:, None]
    d_t = lax.dynamic_slice_in_dim(dcum, blk * Q_BLOCK, Q_BLOCK, axis=2)
    logits = (jnp.einsum('bhqd,bhkd->bhqk', q_blk, k).astype(jnp.float32) * FOX_DIM ** -0.5
              + d_t[..., :, None] - dcum[..., None, :])
    w = jax.nn.softmax(jnp.where(causal, logits, -jnp.inf), axis=-1)
    return jnp.einsum('bhqk,bhkd->bhqd', w.astype(v.dtype), v)

def mixer_mla_sb(x, w_in, q_norm_g, w_uq, kv_norm_g, w_ukv, w_out, cos, sin):
    b, s, _ = x.shape
    h = x @ w_in
    c_q, c_kv, k_rope, sb_qkv = jnp.split(h, [Q_LORA, Q_LORA + KV_LORA, IN_A], axis=-1)
    q = (rms_norm(c_q, q_norm_g) @ w_uq).reshape(b, s, MLA_HEADS, MLA_NOPE + MLA_ROPE).transpose(0, 2, 1, 3)
    q_nope, q_rope = jnp.split(q, [MLA_NOPE], axis=-1)
    q = jnp.concatenate([q_nope, apply_rope(q_rope, cos, sin)], -1)
    kv = (rms_norm(c_kv, kv_norm_g) @ w_ukv).reshape(b, s, MLA_HEADS, MLA_NOPE + MLA_V).transpose(0, 2, 1, 3)
    k_nope, v_a = jnp.split(kv, [MLA_NOPE], axis=-1)
    k_rope = apply_rope(k_rope[:, None], cos, sin)
    k_a = jnp.concatenate([k_nope, jnp.broadcast_to(k_rope, (b, MLA_HEADS, s, MLA_ROPE))], -1)
    o_a = sweep_query_blocks(lambda qb, i: mla_block(qb, i, k_a, v_a), q)
    q_b, k_b, v_b = sb_qkv.reshape(b, s, 3, SB_HEADS, SB_DIM).transpose(2, 0, 3, 1, 4)
    o_b = sweep_query_blocks(lambda qb, i: stick_breaking_block(qb, i, k_b, v_b), q_b)
    return jnp.concatenate([o_a, o_b], -1) @ w_out

def mixer_fox(x, w_in, b_f, w_out):
    b, s, _ = x.shape
    h = x @ w_in
    qkv, f_logit = jnp.split(h, [3 * FOX_HEADS * FOX_DIM], axis=-1)
    q, k, v = qkv.reshape(b, s, 3, FOX_HEADS, FOX_DIM).transpose(2, 0, 3, 1, 4)
    log_f = jax.nn.log_sigmoid((f_logit + b_f).astype(jnp.float32))
    dcum = lax.cumsum(log_f, axis=1).transpose(0, 2, 1)
    o = sweep_query_blocks(lambda qb, i: forgetting_block(qb, i, k, v, dcum), q)
    return o @ w_out

def swiglu(x, w1, w3, w2):
    return (jax.nn.silu(x @ w1) * (x @ w3)) @ w2

def second_inputs(seed: int = 0) -> dict:
    key = jax.random.key(seed)
    ks = iter(jax.random.split(key, 32))

    def dense(shape, fan_in, scale=1.0):
        return jax.random.normal(next(ks), shape, jnp.float32) * (fan_in ** -0.5) * scale

    def gain(shape):
        return 1.0 + 0.02 * jax.random.normal(next(ks), shape, jnp.float32)

    def bias(shape):
        return 0.02 * jax.random.normal(next(ks), shape, jnp.float32)

    return {
        "x": jax.random.normal(next(ks), (BATCH, SEQ, D_MODEL), jnp.float32),
        "p": jax.random.normal(next(ks), (DEPTH, BATCH, SEQ, P_DIM), jnp.float32),
        "a_w_in": dense((N_EVEN, D_MODEL, IN_A + IN_B), D_MODEL),
        "a_q_norm": gain((N_EVEN, Q_LORA)),
        "a_w_uq": dense((N_EVEN, Q_LORA, MLA_HEADS * (MLA_NOPE + MLA_ROPE)), Q_LORA),
        "a_kv_norm": gain((N_EVEN, KV_LORA)),
        "a_w_ukv": dense((N_EVEN, KV_LORA, MLA_HEADS * (MLA_NOPE + MLA_V)), KV_LORA),
        "a_w_out": dense((N_EVEN, MIX_A, D_MODEL), MIX_A, DEEPNORM_BETA),
        "c_w_in": dense((N_ODD, D_MODEL, IN_C), D_MODEL),
        "c_b_f": jax.random.uniform(next(ks), (N_ODD, FOX_HEADS), jnp.float32, 1.0, 4.0),
        "c_w_out": dense((N_ODD, MIX_C, D_MODEL), MIX_C, DEEPNORM_BETA),
        "ffn_w1": dense((DEPTH, D_MODEL, D_FF_2), D_MODEL),
        "ffn_w3": dense((DEPTH, D_MODEL, D_FF_2), D_MODEL),
        "ffn_w2": dense((DEPTH, D_FF_2, D_MODEL), D_FF_2, DEEPNORM_BETA),
        "ln1_g": gain((DEPTH, D_MODEL)),
        "ln1_b": bias((DEPTH, D_MODEL)),
        "ln2_g": gain((DEPTH, D_MODEL)),
        "ln2_b": bias((DEPTH, D_MODEL)),
        "ple_w_proj": dense((DEPTH, P_DIM, D_MODEL), P_DIM),
        "ple_w_gate": dense((DEPTH, D_MODEL, D_MODEL), D_MODEL),
        "ple_b_gate": bias((DEPTH, D_MODEL)),
    }

def second_block(x, p, a_w_in, a_q_norm, a_w_uq, a_kv_norm, a_w_ukv, a_w_out,
              c_w_in, c_b_f, c_w_out, ffn_w1, ffn_w3, ffn_w2,
              ln1_g, ln1_b, ln2_g, ln2_b, ple_w_proj, ple_w_gate, ple_b_gate):
    cos, sin = rope_tables(x.shape[1], MLA_ROPE)
    for i in range(DEPTH):
        j = i // 2
        if i % 2 == 0:
            mix = mixer_mla_sb(x, a_w_in[j], a_q_norm[j], a_w_uq[j], a_kv_norm[j],
                               a_w_ukv[j], a_w_out[j], cos, sin)
        else:
            mix = mixer_fox(x, c_w_in[j], c_b_f[j], c_w_out[j])
        x = layer_norm_2(DEEPNORM_ALPHA * x + mix, ln1_g[i], ln1_b[i])
        x = layer_norm_2(DEEPNORM_ALPHA * x + swiglu(x, ffn_w1[i], ffn_w3[i], ffn_w2[i]), ln2_g[i], ln2_b[i])
        x = x + jax.nn.sigmoid(x @ ple_w_gate[i] + ple_b_gate[i]) * (p[i] @ ple_w_proj[i])
    return x


def setup_inputs(seed=0):
    out = dict(first_inputs(seed))
    for name, value in second_inputs(seed + 1).items():
        if name != "x":
            out[name + "_2"] = value
    return out


def reference(
    x, meta, a_w_in, a_conv, a_log, a_dt_bias, a_norm, a_w_out, b_w_in, b_conv, b_w_out,
    ln_mix_g, ln_mix_b, ffn_w_up, ffn_conv, ffn_w_down, ln_ffn_g, ln_ffn_b, p_2, a_w_in_2,
    a_q_norm_2, a_w_uq_2, a_kv_norm_2, a_w_ukv_2, a_w_out_2, c_w_in_2, c_b_f_2, c_w_out_2,
    ffn_w1_2, ffn_w3_2, ffn_w2_2, ln1_g_2, ln1_b_2, ln2_g_2, ln2_b_2, ple_w_proj_2,
    ple_w_gate_2, ple_b_gate_2,
):
    x = first_block(
        x, meta, a_w_in, a_conv, a_log, a_dt_bias, a_norm, a_w_out, b_w_in, b_conv, b_w_out,
        ln_mix_g, ln_mix_b, ffn_w_up, ffn_conv, ffn_w_down, ln_ffn_g, ln_ffn_b,
    )
    return second_block(
        x, p_2, a_w_in_2, a_q_norm_2, a_w_uq_2, a_kv_norm_2, a_w_ukv_2, a_w_out_2, c_w_in_2,
        c_b_f_2, c_w_out_2, ffn_w1_2, ffn_w3_2, ffn_w2_2, ln1_g_2, ln1_b_2, ln2_g_2, ln2_b_2,
        ple_w_proj_2, ple_w_gate_2, ple_b_gate_2,
    )


_drawn_inputs = setup_inputs


def setup_inputs(seed=0):
    import zlib

    import numpy as np

    out = dict(_drawn_inputs(seed))
    spreads = {}
    factors = {'a_norm': 8.0, 'a_q_norm_2': 8.0, 'a_kv_norm_2': 8.0, 'ple_b_gate_2': 8.0}
    for name, (base, spread) in spreads.items():
        noise = np.random.default_rng([zlib.crc32(name.encode()), seed]).standard_normal(out[name].shape)
        drawn = base * np.exp(spread * noise) if base else spread * noise
        out[name] = __import__('jax').numpy.asarray(drawn.astype(out[name].dtype))
    for name, factor in factors.items():
        out[name] = (out[name] * factor).astype(out[name].dtype)
    return out
```

```python
from contextlib import ExitStack

import numpy as np

import concourse.bass as bass
from concourse import mybir

F32 = mybir.dt.float32
F32R = mybir.dt.float32r
ALU = mybir.AluOpType
ACT = mybir.ActivationFunctionType
AX = mybir.AxisListType.X

P = 128
D = 1024
KT = D // P
SEQ, META = 256, 16
L = SEQ + META
FF = 2816
FT = FF // P
HEADS_A = 8
CH = 64
PAD = CH - META
LP = L + PAD
NCH = LP // CH
NPAIR = 3
ALPHA = 4.0 ** 0.25
RING = 4
N_MIX, N_FFN0, N_B, N_FFN1 = SEQ + 6, SEQ + 4, SEQ + 2, SEQ
OFF_MIX = L - N_MIX

_SIZES = [("ba", 1), ("kqv", 24), ("z", 8), ("a_out", 8), ("up0", 2 * FT), ("down0", FT), ("b_in", 24), ("b_out", 8),
          ("up1", 2 * FT), ("down1", FT), ("m_in", 5), ("m_sbqk", 8), ("m_sbv", 4), ("m_uq", 2), ("m_ukn", 1), ("m_ukv", 1),
          ("m_out", 8), ("up2", 2 * FT), ("down2", FT), ("proj0", 2), ("gate0", 8), ("f_f", 1), ("f_qk", 16), ("f_v", 8),
          ("f_out", 8), ("up3", 2 * FT), ("down3", FT), ("proj1", 2), ("gate1", 8)]
U = {}
NU = 0
for _n, _c in _SIZES:
    U[_n] = NU
    NU += _c

_PARAMS = [("a_conv", 24 * 4), ("b_conv", 8 * 3), ("f_conv0", FT * 3), ("f_conv1", FT * 3), ("a_norm", 1),
           ("q_norm", 2), ("kv_norm", 2), ("ple_b0", 8), ("ple_b1", 8), ("b_f", 1), ("a_log", 8), ("dt_bias", 8)]
_PARAMS += [(f"ln_g{i}", 8) for i in range(8)] + [(f"ln_b{i}", 8) for i in range(8)]
PC = {}
NPC = 0
for _n, _c in _PARAMS:
    PC[_n] = NPC
    NPC += _c

_CONST_A = [("ident", P), ("ones", P), ("half_ones", P), ("half_tri", P), ("tri64", CH), ("eye64", CH), ("incl", CH),
            ("strict", CH), ("levels", 6 * CH), ("live0", 1)]
_CONST_B = [("mla_mask", 384), ("fox_mask", 384), ("sb_mask", 384), ("sb_past", 384), ("neg_tri", P), ("neg_ones", P),
            ("rope", SEQ), ("sel", 16 * P)]


def _columns(names):
    at, n = {}, 0
    for name, c in names:
        at[name] = n
        n += c
    return at, n


CA, NCA = _columns(_CONST_A)
CB, NCB = _columns(_CONST_B)
NEG = -1.0e30


def build(nc, w, h0, par, ca, cb, pin, out):
    with ExitStack() as ctx:
        sems = {}

        def S(name):
            if name not in sems:
                sems[name] = ctx.enter_context(nc.semaphore(name))
            return sems[name]

        def sb(name, shape, dt=F32, where=ctx):
            return where.enter_context(nc.sbuf_tensor(name, shape, dt))

        raw = sb("raw", [P, RING, D])
        w_hi = sb("w_hi", [P, RING, D], F32R)
        w_lo = sb("w_lo", [P, RING, D], F32R)
        h = sb("h", [P, KT, L])
        r = sb("r", [P, KT, L])
        sq = sb("sq", [P, KT, L])
        x_hi = sb("x_hi", [P, KT, L], F32R)
        x_lo = sb("x_lo", [P, KT, L], F32R)
        prm = sb("prm", [P, NPC])
        con = sb("con", [P, NCA])
        std = sb("std", [P, 2, LP])
        rstd = sb("rstd", [P, 2, LP])
        eps = sb("eps", [P, 2])
        bank = [ctx.enter_context(nc.psum_tensor(f"bank{i}", [P, 512], F32)) for i in range(8)]
        acc, misc = bank[:4], bank[4:]

        def C(name, rows=slice(0, P), n=None):
            n = dict(_CONST_A)[name] if n is None else n
            return con[rows, CA[name]:CA[name] + n]

        def par_col(name, j):
            return prm[:, bass.ds(PC[name] + j, 1)] if not isinstance(j, int) else prm[:, PC[name] + j:PC[name] + j + 1]

        def flat(t, a, b, n):
            return t[:, a:b, :].rearrange("p a n -> p (a n)")[:, 0:n]

        conv_a = r[:, 0:2, :]
        kbg = flat(r, 4, 8, D).rearrange("p (a n) -> p a n", a=HEADS_A)
        eg_buf = flat(sq, 4, 8, D).rearrange("p (b n) -> p b n", b=2)
        with ExitStack() as gdn:
            kqv = sb("kqv", [P, 24, LP], where=gdn)
            kT = sb("kT", [P, NPAIR, HEADS_A, P], where=gdn)
            uv = sb("uv", [P, NPAIR, HEADS_A, P], where=gdn)
            E = sb("E", [P, NPAIR, HEADS_A, CH], where=gdn)
            X = sb("X", [P, NPAIR, HEADS_A, CH], where=gdn)
            Y = sb("Y", [P, NPAIR, HEADS_A, CH], where=gdn)
            T = sb("T", [P, NPAIR, HEADS_A, CH], where=gdn)
            QK = sb("QK", [P, NPAIR, HEADS_A, CH], where=gdn)
            state = sb("state", [P, HEADS_A, P], where=gdn)
            ba = sb("ba", [P, LP], where=gdn)
            tok = sb("tok", [P, 14, NPAIR, 8], where=gdn)
            z_gate = sb("z_gate", [P, HEADS_A, N_MIX], where=gdn)
            eg_last = sb("eg_last", [P, NCH, 8], where=gdn)
        cv = sb("cv", [P, 2, N_MIX])
        sl = sb("sl", [P, 2, N_MIX])
        av = sb("av", [P, 2, N_MIX])
        con_b = sb("con_b", [P, NCB])
        p_raw = sb("p_raw", [P, 2, 2, SEQ])
        p_hi = sb("p_hi", [P, 2, 2, SEQ], F32R)
        p_lo = sb("p_lo", [P, 2, 2, SEQ], F32R)
        smx = sb("smx", [P, 2, 384])
        prob = sb("prob", [P, 2, 384])
        probT = sb("probT", [P, 2, 384])
        sb_log = sb("sb_log", [P, 2, 384])
        stat = sb("stat", [P, 2, 3, 2])
        with ExitStack() as ffn:
            a_hi = sb("a_hi", [P, FT, N_FFN0], F32R, where=ffn)
            a_lo = sb("a_lo", [P, FT, N_FFN0], F32R, where=ffn)
        with ExitStack() as ple:
            pp = sb("pp", [P, KT, SEQ], where=ple)
        with ExitStack() as att:
            c_hi = sb("c_hi", [P, 4, SEQ], F32R, where=att)
            c_lo = sb("c_lo", [P, 4, SEQ], F32R, where=att)
            q_m = sb("q_m", [P, 8, SEQ], where=att)
            k_m = sb("k_m", [P, 8, SEQ], where=att)
            v_m = sb("v_m", [P, 2, 512], where=att)
            q_s = sb("q_s", [P, 4, SEQ], where=att)
            k_s = sb("k_s", [P, 4, SEQ], where=att)
            v_s = sb("v_s", [P, 2, 512], where=att)
            rope_t = sb("rope_t", [P, 2, SEQ], where=att)
        with ExitStack() as fox:
            q_f = sb("q_f", [P, 8, SEQ], where=fox)
            k_f = sb("k_f", [P, 8, SEQ], where=fox)
            v_f = sb("v_f", [P, 2, 2, 512], where=fox)
            fl = sb("fl", [P, 5, SEQ], where=fox)
            dcum_col = sb("dcum_col", [P, 2, 16], where=fox)
        up_conv = [1, 1, 0, 0]

        def CBv(name, rows=slice(0, P)):
            return con_b[rows, CB[name]:CB[name] + dict(_CONST_B)[name]]

        block = ctx.enter_context(nc.Block())

        def halves(t):
            return [slice(0, 64)] if t == 0 else [slice(0, 64), slice(64, 128)]

        def rows_of(t):
            return slice(0, 64) if t == 0 else slice(0, P)

        PAIR_AT = [0, CH, 3 * CH]

        def chunk_of(c):
            t = (c + 1) // 2
            half = 0 if c == 0 else (c - 1) % 2
            return t, slice(64 * half, 64 * half + 64), slice(CH * c, CH * c + CH)

        @block.sync
        def _(sp):
            sp.dma_start(h[:, :, :], h0).then_inc(S("h0_in"), 16)
            for u in range(RING):
                sp.dma_start(raw[:, u, :], w[u]).then_inc(S(f"raw{u}"), 16)
            n = (NU - RING) // RING
            with sp.Fori(0, n) as i:
                for b in range(RING):
                    sp.wait_ge(S("lo_ready"), i * RING + (b + 1))
                    sp.dma_start(raw[:, b, :], w[bass.ds(i * RING + (RING + b), 1)].rearrange("a p n -> (a p) n")
                                 ).then_inc(S(f"raw{b}"), 16)
            for u in range(RING + n * RING, NU):
                sp.wait_ge(S("lo_ready"), u - RING + 1)
                sp.dma_start(raw[:, u % RING, :], w[u]).then_inc(S(f"raw{u % RING}"), 16)
            for m in range(KT):
                sp.wait_ge(S("ple_h"), KT + m + 1)
                sp.dma_start(out[:, m, :], h[:, m, 0:SEQ]).then_inc(S("stored"), 16)
            sp.wait_ge(S("stored"), 16 * KT)

        def units(eng, u0, n, body):
            pre = RING if u0 < RING < n else 0
            full = (n - pre) // RING
            full = full if full > 1 else 0
            for b in range(pre):
                body(u0 + b, u0 + b, b)
            if full:
                with eng.Fori(0, full) as i:
                    for b in range(RING):
                        body(i * RING + (u0 + pre + b), u0 + pre + b, i * RING + (pre + b))
            for b in range(pre + full * RING, n):
                body(u0 + b, u0 + b, b)

        def at(t, j, cols=slice(None)):
            return t[:, j, cols] if isinstance(j, int) else t[:, bass.ds(j, 1), cols].rearrange("p a n -> p (a n)")

        @block.tensor
        def _(pe):
            x_sets = [0]

            def start_unit(u, s, wait_acc=True):
                pe.wait_ge(S("lo_ready"), u + 1)
                if wait_acc and s >= RING:
                    pe.wait_ge(S("acc_used"), u - (RING - 1))

            def three(o, wh, wl, xh, xl, first, last):
                pe.matmul(o, wh, xh, start=first, stop=False)
                pe.matmul(o, wh, xl, start=False, stop=False)
                return pe.matmul(o, wl, xh, start=False, stop=last)

            def wait_x():
                x_sets[0] += 1
                pe.wait_ge(S("x_ready"), x_sets[0])

            def panels(u0, n, N):
                def body(u, s, j):
                    slot = s % RING
                    start_unit(u, s)
                    for k in range(KT):
                        c = slice(k * P, k * P + P)
                        mm = three(acc[slot][:, 0:N], w_hi[:, slot, c], w_lo[:, slot, c], x_hi[:, k, 0:N],
                                   x_lo[:, k, 0:N], k == 0, k == KT - 1)
                    mm.then_inc(S("unit_done"), 1)
                units(pe, u0, n, body)

            def down(u0, N):
                pe.wait_ge(S("acc_used"), u0)
                pe.wait_ge(S("a_ready"), FT * (downs[0] + 1) + 2)

                def one(u, s, k, first, last):
                    slot = s % RING
                    pe.wait_ge(S("lo_ready"), u + 1)
                    xh, xl = at(a_hi, k, slice(0, N)), at(a_lo, k, slice(0, N))
                    for m in range(KT):
                        c = slice(m * P, m * P + P)
                        mm = three(bank[m][:, 0:N], w_hi[:, slot, c], w_lo[:, slot, c], xh, xl, first, last)
                    mm.then_inc(S("unit_done"), 1)

                for k in range(2):
                    one(u0 + k, u0 + k, k, k == 0, False)
                with pe.Fori(0, (FT - 6) // RING) as i:
                    for b in range(RING):
                        one(i * RING + (u0 + 2 + b), u0 + 2 + b, i * RING + (2 + b), False, False)
                for k in range(FT - 4, FT):
                    one(u0 + k, u0 + k, k, False, k == FT - 1)
                downs[0] += 1

            downs = [0]

            def layer_norm(n, u0, N, from_down):
                order = [4, 5, 6, 7, 0, 1, 2, 3] if from_down else list(range(KT))
                for j, m in enumerate(order):
                    pe.wait_ge(S("acc_used"), u0 + (j + 1 if not from_down or j < KT - 1 else FT))
                    mm = pe.matmul(misc[0][:, 0:N], C("ones"), r[:, m, 0:N], start=(j == 0), stop=(j == KT - 1))
                mm.then_inc(S("ln_sum"), 1)
                for j in range(4):
                    pe.wait_ge(S("ln_sq"), 4 * n + j + 1)
                    for m in (2 * j, 2 * j + 1):
                        mm = pe.matmul(misc[1][:, 0:N], C("ones"), sq[:, m, 0:N], start=(m == 0), stop=(m == KT - 1))
                mm.then_inc(S("ln_var"), 1)

            wait_x()
            panels(U["ba"], 1, L)
            panels(U["kqv"], 24, L)
            panels(U["z"], 8, L)

            pe.wait_ge(S("con_in"), 16)
            pe.wait_ge(S("ba_copied"), 1)
            for t in range(NPAIR):
                mm = pe.transpose(misc[0][:, t * 64:t * 64 + 64], ba[0:64, PAIR_AT[t]:PAIR_AT[t] + P], C("ident", slice(0, 64), 64))
            mm.then_inc(S("ba_turned"), 1)
            for j in range(16):
                pe.wait_ge(S("kq_sq"), j + 1)
                if j >= 2:
                    pe.wait_ge(S("kq_std"), j - 1)
                pe.matmul(misc[1 + j % 2][:, 0:LP], C("ones"), flat(sq, 0, 4, 2 * LP)[:, (j % 2) * LP:(j % 2) * LP + LP],
                          start=True, stop=True).then_inc(S("kq_sum"), 1)
            pe.wait_ge(S("kq_normed"), 16)
            pe.wait_ge(S("g_ready"), 1)
            for t in range(NPAIR):
                pe.matmul(misc[3][:, t * 8:t * 8 + 8], C("half_tri"), tok[:, 1, t, :], start=True, stop=True)
                mm = pe.matmul(misc[3][:, 24 + t * 8:32 + t * 8], C("half_ones"), tok[:, 1, t, :], start=True, stop=True)
            mm.then_inc(S("g_col"), 1)
            for t in range(NPAIR):
                pe.wait_ge(S("g_spread"), t + 1)
                if t:
                    pe.wait_ge(S("g_diff"), t)
                pe.matmul(misc[0][:, :], C("half_ones"), flat(r, 0, 2, 512), start=True, stop=True).then_inc(S("g_row"), 1)
                pe.wait_ge(S("beta_spread"), t + 1)
                if t:
                    pe.wait_ge(S("e_ready"), t)
                pe.matmul(misc[1][:, :], C("half_ones"), flat(r, 2, 4, 512), start=True, stop=True).then_inc(S("beta_row"), 1)
                if t:
                    pe.wait_ge(S("qk_ready"), t)
                for hd in range(HEADS_A):
                    for n, rows in enumerate(halves(t)):
                        cols = slice(PAIR_AT[t] + 64 * n, PAIR_AT[t] + 64 * n + 64)
                        pe.matmul(acc[0][rows, hd * CH:hd * CH + CH], kqv[:, hd, cols], kqv[:, hd, cols], start=True, stop=True)
                        mm = pe.matmul(acc[1][rows, hd * CH:hd * CH + CH], kqv[:, hd, cols], kqv[:, 8 + hd, cols], start=True, stop=True)
                mm.then_inc(S("kk_qk"), 1)
                if t:
                    pe.wait_ge(S("kT_ready"), t)
                    pe.wait_ge(S("v_beta"), t)
                cols = slice(PAIR_AT[t], PAIR_AT[t] + P)
                for hd in range(HEADS_A):
                    q = slice((hd % 4) * P, (hd % 4) * P + P)
                    pe.transpose(bank[2 + hd // 4][:, q], kqv[:, hd, cols], C("ident"))
                    mm = pe.transpose(bank[6 + hd // 4][:, q], kqv[:, 16 + hd, cols], C("ident"))
                mm.then_inc(S("kv_turned"), 1)
            for lv in range(6):
                for t in range(NPAIR):
                    st = lv * NPAIR + t
                    if lv == 0:
                        pe.wait_ge(S("e_ready"), t + 1)
                        pe.wait_ge(S("xy_init"), 1)
                        if t == 0:
                            pe.wait_ge(S("qk_ready"), NPAIR)
                    else:
                        pe.wait_ge(S("xy_ready"), st - NPAIR + 1)
                    if st >= 2:
                        pe.wait_ge(S("t_ready"), st - 1)
                    for hd in range(HEADS_A):
                        for rows in halves(t):
                            c = slice(hd * CH, hd * CH + CH)
                            mm = pe.matmul(acc[st % 2][rows, c], E[rows, t, hd, :], X[rows, t, hd, :], start=True, stop=True)
                    mm.then_inc(S("ax_done"), 1)
                for t in range(NPAIR):
                    st = lv * NPAIR + t
                    pe.wait_ge(S("t_ready"), st + 1)
                    if st >= 2:
                        pe.wait_ge(S("xy_ready"), st - 1)
                    elif st == 0:
                        pe.wait_ge(S("kT_ready"), NPAIR)
                        pe.wait_ge(S("v_beta"), NPAIR)
                    for hd in range(HEADS_A):
                        for rows in halves(t):
                            c = slice(hd * CH, hd * CH + CH)
                            pe.matmul(misc[2 * (st % 2)][rows, c], Y[rows, t, hd, :], T[rows, t, hd, :], start=True, stop=True)
                            mm = pe.matmul(misc[2 * (st % 2) + 1][rows, c], T[rows, t, hd, :], Y[rows, t, hd, :], start=True, stop=True)
                    mm.then_inc(S("xt_done"), 1)
            for t in range(NPAIR):
                pe.wait_ge(S("xy_ready"), 5 * NPAIR + NPAIR)
                pe.wait_ge(S("kbg_ready"), t + 1)
                if t:
                    pe.wait_ge(S("u_ready"), t)
                    pe.wait_ge(S("w_ready"), 2 * t - 1)
                for hd in range(HEADS_A):
                    for rows in halves(t):
                        q = slice((hd % 4) * P, (hd % 4) * P + P)
                        mm = pe.matmul(acc[hd // 4][rows, q], Y[rows, t, hd, :], uv[rows, t, hd, :], start=True, stop=True)
                mm.then_inc(S("u_done"), 1)
                for n, rows in enumerate(halves(t)):
                    for hd in range(HEADS_A):
                        mm = pe.matmul(misc[n][:, hd * CH:hd * CH + CH], kbg[rows, hd, :], Y[rows, t, hd, :], start=True, stop=True)
                    mm.then_inc(S("w_done"), 1)
            for c in range(NCH):
                t, rows, cols = chunk_of(c)
                pe.wait_ge(S("g_spread2"), t + 1)
                if c >= 2:
                    pe.wait_ge(S("eg_exp"), c - 1)
                pe.matmul(misc[2 + c % 2][:, :], C("ones", rows), flat(r, 0, 4, D)[rows, (t % 2) * 512:(t % 2) * 512 + 512],
                          start=True, stop=True).then_inc(S("eg_row"), 1)
            pe.wait_ge(S("eg_exp"), NCH)
            for c in range(NCH):
                t, rows, cols = chunk_of(c)
                if c == 0:
                    pe.wait_ge(S("w_ready"), NCH)
                    pe.wait_ge(S("u_ready"), NPAIR)
                    pe.wait_ge(S("kd_ready"), 1)
                    pe.wait_ge(S("qg_ready"), NCH)
                else:
                    pe.wait_ge(S("state_ready"), c)
                    for hd in range(HEADS_A):
                        mm = pe.matmul(acc[hd // 4][rows, (hd % 4) * P:(hd % 4) * P + P], kqv[:, 16 + hd, cols], state[:, hd, :], start=True, stop=True)
                    mm.then_inc(S("ws_done"), 1)
                    pe.wait_ge(S("v_new"), c)
                if c >= 1:
                    pe.wait_ge(S("o_copied"), c)
                if c < NCH - 1:
                    for hd in range(HEADS_A):
                        mm = pe.matmul(acc[2 + hd // 4][:, (hd % 4) * P:(hd % 4) * P + P], kT[rows, t, hd, :], uv[rows, t, hd, :], start=True, stop=True)
                    mm.then_inc(S("kv_done"), 1)
                for hd in range(HEADS_A):
                    o = misc[0][:, hd * CH:hd * CH + CH]
                    if c:
                        pe.matmul(o, state[:, hd, :], kqv[:, 8 + hd, cols], start=True, stop=False)
                    mm = pe.matmul(o, uv[rows, t, hd, :], QK[rows, t, hd, :], start=(c == 0), stop=True)
                mm.then_inc(S("o_done"), 1)
            for hd in range(HEADS_A):
                pe.wait_ge(S("o_sq"), hd + 1)
                if hd >= 2:
                    pe.wait_ge(S("o_std"), hd - 1)
                pe.matmul(misc[2 + hd % 2][:, 0:N_MIX], C("ones"), sq[:, hd, 0:N_MIX], start=True, stop=True).then_inc(S("o_sum"), 1)

            wait_x()
            panels(U["a_out"], 8, N_MIX)
            layer_norm(0, U["a_out"], N_MIX, False)
            wait_x()
            panels(U["up0"], 2 * FT, N_MIX)
            down(U["down0"], N_FFN0)
            layer_norm(1, U["down0"], N_FFN0, True)
            wait_x()
            panels(U["b_in"], 24, N_FFN0)
            wait_x()
            panels(U["b_out"], 8, N_B)
            layer_norm(2, U["b_out"], N_B, False)
            wait_x()
            panels(U["up1"], 2 * FT, N_B)
            down(U["down1"], N_FFN1)
            layer_norm(3, U["down1"], SEQ, True)

            def tokens(u0, tiles, xh, xl, groups):
                pe.wait_ge(S("acc_used"), u0)
                n = tiles // 2
                for j in range(n):
                    s = u0 + j
                    slot = s % RING
                    pe.wait_ge(S("lo_ready"), s + 1)
                    for i in range(2):
                        for kk in range(2):
                            k = 2 * j + kk
                            wc = slice(kk * 512, kk * 512 + 512)
                            tk = slice(i * P, i * P + P)
                            o = acc[i][:, 0:512]
                            f, l = k == 0, k == tiles - 1
                            pe.matmul(o, xh[:, k, tk], w_hi[:, slot, wc], start=f, stop=False)
                            pe.matmul(o, xl[:, k, tk], w_hi[:, slot, wc], start=False, stop=False)
                            mm = pe.matmul(o, xh[:, k, tk], w_lo[:, slot, wc], start=False, stop=l)
                    mm.then_inc(S("unit_done"), 1)

            def four(u, xh, xl, banks):
                slot = u % RING
                pe.wait_ge(S("acc_used"), u)
                pe.wait_ge(S("lo_ready"), u + 1)
                for m in range(4):
                    for k in range(2):
                        c = slice(k * 512 + m * P, k * 512 + m * P + P)
                        mm = three(banks[m][:, 0:SEQ], w_hi[:, slot, c], w_lo[:, slot, c], xh[:, k, 0:SEQ], xl[:, k, 0:SEQ], k == 0, k == 1)
                mm.then_inc(S("unit_done"), 1)

            wait_x()
            panels(U["m_in"], 5, SEQ)
            panels(U["m_sbqk"], 8, SEQ)
            tokens(U["m_sbv"], KT, x_hi, x_lo, 1)
            for j in range(4):
                pe.wait_ge(S("c_sq"), j + 1)
                mm = pe.matmul(misc[j // 2][:, 0:SEQ], C("ones"), sq[:, j, 0:SEQ], start=(j % 2 == 0), stop=(j % 2 == 1))
                if j % 2:
                    mm.then_inc(S("c_sum"), 1)
            pe.wait_ge(S("c_ready"), 4)
            four(U["m_uq"], c_hi, c_lo, acc)
            four(U["m_uq"] + 1, c_hi, c_lo, acc)
            four(U["m_ukn"], c_hi[:, 2:4, :], c_lo[:, 2:4, :], acc)
            tokens(U["m_ukv"], 2, c_hi[:, 2:4, :], c_lo[:, 2:4, :], 1)

            def scores_mla(hd):
                o = misc[hd % 2]
                kq = (k_m[0:96, hd, :], q_m[0:96, hd, :])
                pe.matmul(o[:, 0:128], kq[1][:, 0:P], kq[0][:, 0:P], start=True, stop=True)
                return pe.matmul(o[:, 128:384], kq[1][:, P:SEQ], kq[0][:, 0:SEQ], start=True, stop=True)

            def scores_fox(hd):
                o = misc[hd % 2]
                rows = slice(64 * (hd % 2), 64 * (hd % 2) + 64)
                k, q = k_f[rows, hd // 2, :], q_f[rows, hd // 2, :]
                sel = con_b[0:16, CB["sel"] + hd * P:CB["sel"] + hd * P + P]
                pe.matmul(o[:, 0:128], q[:, 0:P], k[:, 0:P], start=True, stop=False)
                pe.matmul(o[:, 0:128], sel, fl[0:16, 4, 0:P], start=False, stop=True)
                pe.matmul(o[:, 128:384], q[:, P:SEQ], k[:, 0:SEQ], start=True, stop=False)
                return pe.matmul(o[:, 128:384], sel, fl[0:16, 4, 0:SEQ], start=False, stop=True)

            def softmax_heads(n, base, scores, v):
                def score(hd):
                    if base + hd >= 2:
                        pe.wait_ge(S("sm_masked"), base + hd - 1)
                    scores(hd).then_inc(S("sm_scores"), 1)
                score(0)
                score(1)
                for hd in range(n):
                    g = base + hd
                    pe.wait_ge(S("sm_probs"), g + 1)
                    if g >= 2:
                        pe.wait_ge(S("sm_turned_copied"), g - 1)
                    o = misc[2 + hd % 2]
                    for j in range(3):
                        mm = pe.transpose(o[:, j * P:j * P + P], prob[:, g % 2, j * P:j * P + P], C("ident"))
                    mm.then_inc(S("sm_turned"), 1)
                    if hd + 2 < n:
                        score(hd + 2)
                    pe.wait_ge(S("sm_turned_copied"), g + 1)
                    rows = slice(64 * (hd % 2), 64 * (hd % 2) + 64)
                    ob = acc[(hd // 2) % 4]
                    if hd % 2 == 0 and hd >= 8:
                        pe.wait_ge(S("o_split"), o_base[0] + hd // 2 - 3)
                    pT = probT[:, g % 2, :]
                    pe.matmul(ob[rows, 0:128], v(0, hd), pT[:, 0:128], start=True, stop=True)
                    pe.matmul(ob[rows, 128:256], v(0, hd), pT[:, 128:256], start=True, stop=False)
                    mm = pe.matmul(ob[rows, 128:256], v(1, hd), pT[:, 256:384], start=False, stop=True)
                    mm.then_inc(S("pv_done"), 1)

            o_base = [0]
            pe.wait_ge(S("acc_used"), U["m_out"])
            pe.wait_ge(S("con_b_in"), 16)
            pe.wait_ge(S("m_ready"), 1)
            softmax_heads(8, 0, scores_mla, lambda i, hd: v_m[:, i, hd * 64:hd * 64 + 64])
            o_base[0] = 4

            def sb_ops(hd):
                rows = slice(64 * (hd % 2), 64 * (hd % 2) + 64)
                return k_s[rows, hd // 2, :], q_s[rows, hd // 2, :]

            def sb_z(hd):
                k, q = sb_ops(hd)
                if hd >= 2:
                    pe.wait_ge(S("sb_rem"), hd - 1)
                else:
                    pe.wait_ge(S("sm_masked"), 8)
                o = misc[hd % 2]
                pe.matmul(o[:, 0:256], k[:, 0:P], q[:, 0:SEQ], start=True, stop=True)
                pe.matmul(o[:, 256:384], k[:, P:SEQ], q[:, P:SEQ], start=True, stop=True).then_inc(S("sb_logits"), 1)

            sb_z(0)
            sb_z(1)
            for hd in range(8):
                k, q = sb_ops(hd)
                rem = prob[:, hd % 2, :]
                pe.wait_ge(S("sb_rem"), hd + 1)
                if hd >= 2:
                    pe.wait_ge(S("sb_min"), hd - 1)
                else:
                    pe.wait_ge(S("sm_turned_copied"), 8)
                o = misc[2 + hd % 2]
                pe.matmul(o[:, 0:256], k[:, 0:P], q[:, 0:SEQ], start=True, stop=False)
                pe.matmul(o[:, 0:256], CBv("neg_tri"), rem[:, 0:256], start=False, stop=False)
                pe.matmul(o[:, 128:256], CBv("neg_ones"), rem[:, 256:384], start=False, stop=True)
                pe.matmul(o[:, 256:384], k[:, P:SEQ], q[:, P:SEQ], start=True, stop=False)
                pe.matmul(o[:, 256:384], CBv("neg_tri"), rem[:, 256:384], start=False, stop=True).then_inc(S("sb_sum"), 1)
                if hd + 2 < 8:
                    sb_z(hd + 2)
                pe.wait_ge(S("sb_att"), hd + 1)
                rows = slice(64 * (hd % 2), 64 * (hd % 2) + 64)
                ob = acc[(hd // 2) % 4]
                if hd % 2 == 0:
                    pe.wait_ge(S("o_split"), hd // 2 + 1)
                weights = probT[:, hd % 2, :]
                pe.matmul(ob[rows, 0:256], v_s[:, 0, hd * 64:hd * 64 + 64], weights[:, 0:256], start=True, stop=False)
                pe.matmul(ob[rows, 128:256], v_s[:, 1, hd * 64:hd * 64 + 64], weights[:, 256:384], start=False, stop=True).then_inc(S("pv_done"), 1)
            wait_x()
            panels(U["m_out"], 8, SEQ)
            layer_norm(4, U["m_out"], SEQ, False)

            def ffn_and_ple(i, n, up, dn, proj, gate):
                wait_x()
                panels(up, 2 * FT, SEQ)
                down(dn, SEQ)
                layer_norm(n, dn, SEQ, True)
                pe.wait_ge(S("p_split"), 1)
                for j in range(2):
                    slot = (proj + j) % RING
                    four(proj + j, p_hi[:, i], p_lo[:, i], acc)
                wait_x()
                pe.wait_ge(S("acc_used"), gate)
                panels(gate, 8, SEQ)

            ffn_and_ple(0, 5, U["up2"], U["down2"], U["proj0"], U["gate0"])

            wait_x()
            panels(U["f_f"], 1, SEQ)
            panels(U["f_qk"], 16, SEQ)
            for g in range(2):
                tokens(U["f_v"] + 4 * g, KT, x_hi, x_lo, 1)
            pe.wait_ge(S("dcum"), 1)
            for i in range(2):
                mm = pe.transpose(misc[0][:, i * 16:i * 16 + 16], fl[0:16, 3, i * P:i * P + P], C("ident", slice(0, 16), 16))
            mm.then_inc(S("dcum_turned"), 1)
            pe.wait_ge(S("dcum_copied"), 1)
            pe.wait_ge(S("acc_used"), U["f_out"])
            o_base[0] = 8
            softmax_heads(16, 8, scores_fox, lambda i, hd: v_f[:, i, hd // 8, (hd % 8) * 64:(hd % 8) * 64 + 64])
            wait_x()
            panels(U["f_out"], 8, SEQ)
            layer_norm(6, U["f_out"], SEQ, False)
            ffn_and_ple(1, 7, U["up3"], U["down3"], U["proj1"], U["gate1"])

        @block.scalar
        def _(act):
            A = nc.scalar.activation

            def split(u, s):
                if isinstance(s, int) and s >= NU:
                    return
                slot = s % RING
                act.wait_ge(S(f"raw{slot}"), (u - slot) * 4 + 16 if not isinstance(u, int) else 16 * (u // RING + 1))
                if s >= RING:
                    act.wait_ge(S("unit_done"), u - (RING - 1))
                A(w_hi[:, slot, :], raw[:, slot, :], ACT.Copy).then_inc(S("hi_ready"), 1)

            def ahead(u, s):
                split(u + RING, s + RING)

            x_sets = [0]

            def layer_norm(n, N):
                for j in range(4):
                    act.wait_ge(S("ln_centred"), 4 * n + j + 1)
                    A(sq[:, 2 * j:2 * j + 2, 0:N], r[:, 2 * j:2 * j + 2, 0:N], ACT.Square).then_inc(S("ln_sq"), 1)
                act.wait_ge(S("ln_var"), n + 1)
                A(std[:, 0, 0:N], misc[1][:, 0:N], ACT.Sqrt, bias=eps[:, 0:1], scale=1.0 / D).then_inc(S("ln_std"), 1)
                for k in range(KT):
                    act.wait_ge(S("ln_scaled"), 4 * n + k // 2 + 1)
                    A(x_hi[:, k, 0:N], r[:, k, 0:N], ACT.Identity, bias=par_col(f"ln_b{n}", k), scale=par_col(f"ln_g{n}", k)).then_inc(S("x_hi"), 1)
                x_hi_n[0] += KT

            x_hi_n = [0]

            act.dma_start(prm[:, :], par).then_inc(S("prm_in"), 16)
            act.dma_start(con[:, :], ca).then_inc(S("con_in"), 16)
            act.wait_ge(S("eps_set"), 1)
            act.wait_ge(S("h0_in"), 16)
            for k in range(4):
                A(x_hi[:, 2 * k:2 * k + 2, :], h[:, 2 * k:2 * k + 2, :], ACT.Copy).then_inc(S("x_hi"), 1)
            x_hi_n[0] += 4
            for u in range(RING):
                split(u, u)
            act.wait_ge(S("prm_in"), 16)
            act.wait_ge(S("zeroed"), 1)
            act.wait_ge(S("unit_done"), 1)
            A(ba[:, PAD:LP], acc[U["ba"] % RING][:, 0:L], ACT.Copy).then_inc(S("ba_copied"), 1)
            ahead(U["ba"], U["ba"])

            def kqv_unit(u, s, j):
                c = conv_a[:, (s - U["kqv"]) % 2, :]
                act.wait_ge(S("unit_done"), u + 1)
                A(c, acc[s % RING][:, 0:L], ACT.Copy, scale=par_col("a_conv", j * 4 + 3)).then_inc(S("tap0"), 1)
                ahead(u, s)
                act.wait_ge(S("taps_done"), j + 1)
                A(at(kqv, j, slice(PAD, LP)), c, ACT.Silu).then_inc(S("kqv_silu"), 1)

            units(act, U["kqv"], 24, kqv_unit)

            def z_unit(u, s, j):
                act.wait_ge(S("unit_done"), u + 1)
                A(at(z_gate, j), acc[s % RING][:, OFF_MIX:L], ACT.Silu).then_inc(S("acc_used"), 1)
                ahead(u, s)

            act.wait_ge(S("acc_used"), U["z"])
            units(act, U["z"], 8, z_unit)

            tk = lambda i: tok[:, i, :, :]
            turned = misc[0][:, 0:192].rearrange("p (t c) -> p t c", t=3)
            act.wait_ge(S("ba_turned"), 1)
            A(tk(2), turned[:, :, 0:8], ACT.Exp, scale=-1.0).then_inc(S("tok_act"), 1)
            act.wait_ge(S("tok_dve"), 1)
            A(tk(4), tk(3), ACT.Abs).then_inc(S("tok_act"), 1)
            act.wait_ge(S("tok_act"), 2)
            A(tk(5), tk(4), ACT.Exp, scale=-1.0).then_inc(S("tok_act"), 1)
            act.wait_ge(S("tok_act"), 3)
            A(tk(6), tk(5), ACT.Ln, bias=1.0).then_inc(S("tok_act"), 1)
            A(tok[:, 7, 0, :], prm[:, PC["a_log"]:PC["a_log"] + 8], ACT.Exp).then_inc(S("tok_act"), 1)
            def kq_std(j):
                act.wait_ge(S("kq_sum"), j + 1)
                if j >= 2:
                    act.wait_ge(S("kq_rstd"), j - 1)
                A(std[:, j % 2, :], misc[1 + j % 2][:, 0:LP], ACT.Sqrt, bias=eps[:, 1:2]).then_inc(S("kq_std"), 1)

            def o_std(hd):
                act.wait_ge(S("o_sum"), hd + 1)
                if hd >= 2:
                    act.wait_ge(S("o_gated"), hd - 1)
                A(std[:, hd % 2, 0:N_MIX], misc[2 + hd % 2][:, 0:N_MIX], ACT.Sqrt, bias=eps[:, 1:2], scale=1.0 / P).then_inc(S("o_std"), 1)

            act.wait_ge(S("kqv_silu"), 24)
            sqf = flat(sq, 0, 4, 2 * LP)
            for j in range(16):
                if j >= 2:
                    act.wait_ge(S("kq_sum"), j - 1)
                A(sqf[:, (j % 2) * LP:(j % 2) * LP + LP], kqv[:, j, :], ACT.Square).then_inc(S("kq_sq"), 1)
                if j >= 1:
                    kq_std(j - 1)
            kq_std(15)
            act.wait_ge(S("tok_dve"), 3)
            A(tok[:, 9, :, :], tok[:, 8, :, :], ACT.Exp).then_inc(S("tok_act"), 1)
            A(tok[:, 11, :, :], tok[:, 10, :, :], ACT.Exp).then_inc(S("tok_act"), 1)
            for t in range(NPAIR):
                act.wait_ge(S("g_diff2"), t + 1)
                A(T[:, t], T[:, t], ACT.Exp).then_inc(S("decay"), 1)
                act.wait_ge(S("kv_turned"), t + 1)
                for g in range(2):
                    a = A(kT[:, t, 4 * g:4 * g + 4, :], bank[2 + g][:, :].rearrange("p (a n) -> p a n", a=4), ACT.Copy)
                a.then_inc(S("kT_ready"), 1)
            for t in range(NPAIR):
                for n, rows in enumerate(halves(t)):
                    c = 0 if t == 0 else 2 * t - 1 + n
                    act.wait_ge(S("w_done"), c + 1)
                    A(kqv[:, 16:24, CH * c:CH * c + CH], misc[n][:, :].rearrange("p (a n) -> p a n", a=8), ACT.Copy).then_inc(S("w_ready"), 1)
            for c in range(NCH):
                act.wait_ge(S("eg_row"), c + 1)
                if c >= 2:
                    act.wait_ge(S("qg_ready"), c - 1)
                A(eg_buf[:, c % 2, :], misc[2 + c % 2][:, :], ACT.Exp).then_inc(S("eg_exp"), 1)
            for c in range(NCH):
                t, rows, cols = chunk_of(c)
                act.wait_ge(S("o_done"), c + 1)
                A(kqv[:, 0:8, cols], misc[0][:, :].rearrange("p (a n) -> p a n", a=8), ACT.Copy).then_inc(S("o_copied"), 1)
            act.wait_ge(S("o_copied"), NCH)
            for hd in range(HEADS_A):
                A(sq[:, hd, 0:N_MIX], kqv[:, hd, LP - N_MIX:LP], ACT.Square).then_inc(S("o_sq"), 1)
                if hd >= 1:
                    o_std(hd - 1)
            o_std(HEADS_A - 1)
            for hd in range(HEADS_A):
                act.wait_ge(S("o_gated"), hd + 1)
                A(x_hi[:, hd, 0:N_MIX], r[:, hd, 0:N_MIX], ACT.Copy).then_inc(S("x_hi"), 1)
            x_hi_n[0] += KT
            act.wait_ge(S("x_ready"), 2)
            act.dma_start(con_b[:, :], cb).then_inc(S("con_b_in"), 16)
            act.dma_start(p_raw[:, :, :, :], pin).then_inc(S("p_in"), 16)

            def out_phase(u0, n):
                units(act, u0, n, lambda u, s, j: (act.wait_ge(S("unit_done"), u + 1), ahead(u, s)))

            def down_phase(u0):
                for j in range(2):
                    act.wait_ge(S("unit_done"), u0 + j + 1)
                    ahead(u0 + j, u0 + j)
                with act.Fori(0, (FT - 6) // RING) as i:
                    for b in range(RING):
                        act.wait_ge(S("unit_done"), i * RING + (u0 + 3 + b))
                        ahead(i * RING + (u0 + 2 + b), u0 + 2 + b)
                for j in range(FT - 4, FT):
                    act.wait_ge(S("unit_done"), u0 + j + 1)
                    ahead(u0 + j, u0 + j)

            ups = [0]

            def up_phase(u0, N, conv):
                base = ups[0] * FT
                cbase = sum(up_conv[:ups[0]]) * FT

                def pair(u, s, j):
                    g = s % RING
                    par = (s - u0) // 2 % 2
                    jb = j + base
                    act.wait_ge(S("unit_done"), u + 2)
                    if conv is not None:
                        A(cv[:, par, 0:N - 2], acc[g][:, 0:N - 2], ACT.Copy, scale=par_col(conv, j * 3)).then_inc(S("ffn_tap0"), 1)
                        ahead(u, s)
                        act.wait_ge(S("ffn_taps"), j + (cbase + 1))
                        A(sl[:, par, 0:N - 2], cv[:, par, 0:N - 2], ACT.Silu).then_inc(S("ffn_silu"), 1)
                        M = N - 2
                    else:
                        A(sl[:, par, 0:N], acc[g][:, 0:N], ACT.Silu).then_inc(S("ffn_silu"), 1)
                        ahead(u, s)
                        M = N
                    ahead(u + 1, s + 1)
                    act.wait_ge(S("ffn_product"), jb + 1)
                    A(at(a_hi, j, slice(0, M)), av[:, par, 0:M], ACT.Copy).then_inc(S("a_hi"), 1)

                with act.Fori(0, FT // 2) as i:
                    for b in range(2):
                        pair(i * RING + (u0 + 2 * b), u0 + 2 * b, i * 2 + b)
                ups[0] += 1

            out_phase(U["a_out"], 8)
            layer_norm(0, N_MIX)
            up_phase(U["up0"], N_MIX, "f_conv0")
            down_phase(U["down0"])
            layer_norm(1, N_FFN0)

            def b_tile(u, s, j):
                act.wait_ge(S("unit_done"), u + 1)
                act.wait_ge(S("b_cx"), j)
                A(av[:, 0, 0:N_FFN0], acc[s % RING][:, 0:N_FFN0], ACT.Copy).then_inc(S("b_c"), 1)
                ahead(u, s)
                act.wait_ge(S("unit_done"), u + 2)
                ahead(u + 1, s + 1)
                act.wait_ge(S("unit_done"), u + 3)
                ahead(u + 2, s + 2)

            with act.Fori(0, 2) as i:
                for q in range(4):
                    b_tile(i * 12 + (U["b_in"] + 3 * q), U["b_in"] + 3 * q, i * 4 + q)
            act.wait_ge(S("b_done"), 8)
            for k in range(4):
                A(x_hi[:, 2 * k:2 * k + 2, 0:N_B], r[:, 2 * k:2 * k + 2, 0:N_B], ACT.Copy).then_inc(S("x_hi"), 1)
            x_hi_n[0] += 4
            out_phase(U["b_out"], 8)
            layer_norm(2, N_B)
            up_phase(U["up1"], N_B, "f_conv1")
            down_phase(U["down1"])
            layer_norm(3, SEQ)

            act.wait_ge(S("p_in"), 16)
            A(p_hi[:, :, :, :], p_raw[:, :, :, :], ACT.Copy).then_inc(S("p_hi"), 1)
            for j in range(5):
                u = U["m_in"] + j
                act.wait_ge(S("unit_done"), u + 1)
                if j < 4:
                    A(sq[:, j, 0:SEQ], acc[u % RING][:, 0:SEQ], ACT.Square).then_inc(S("c_sq"), 1)
                ahead(u, u)
            act.wait_ge(S("acc_used"), U["m_sbqk"])
            for j in range(8):
                u = U["m_sbqk"] + j
                act.wait_ge(S("unit_done"), u + 1)
                dst = (q_s if j < 4 else k_s)[:, j % 4, :]
                A(dst, acc[u % RING][:, 0:SEQ], ACT.Copy, scale=0.125 if j < 4 else 1.0).then_inc(S("acc_used"), 1)
                ahead(u, u)
            for j in range(4):
                u = U["m_sbv"] + j
                act.wait_ge(S("unit_done"), u + 1)
                ahead(u, u)
            A(v_s[:, 0, :], acc[0][:, :], ACT.Copy).then_inc(S("acc_used"), 2)
            A(v_s[:, 1, :], acc[1][:, :], ACT.Copy).then_inc(S("acc_used"), 2)
            for j in range(2):
                act.wait_ge(S("c_sum"), j + 1)
                A(std[:, j, 0:SEQ], misc[j][:, 0:SEQ], ACT.Sqrt, bias=eps[:, 1:2], scale=1.0 / 256).then_inc(S("c_std"), 1)
            for j in range(4):
                act.wait_ge(S("c_normed"), j + 1)
                A(c_hi[:, j, :], r[:, 4 + j, 0:SEQ], ACT.Copy).then_inc(S("c_hi"), 1)
            for j in range(2):
                u = U["m_uq"] + j
                act.wait_ge(S("unit_done"), u + 1)
                for m in range(4):
                    A(q_m[0:64, 4 * j + m, :], acc[m][0:64, 0:SEQ], ACT.Copy).then_inc(S("q_nope"), 1)
                ahead(u, u)
            u = U["m_ukn"]
            act.wait_ge(S("unit_done"), u + 1)
            for m in range(4):
                A(k_m[0:64, 2 * m, :], acc[m][0:64, 0:SEQ], ACT.Copy)
                a = A(k_m[0:64, 2 * m + 1, :], acc[m][64:128, 0:SEQ], ACT.Copy)
            a.then_inc(S("acc_used"), 1)
            ahead(u, u)
            u = U["m_ukv"]
            act.wait_ge(S("unit_done"), u + 1)
            A(v_m[:, 0, :], acc[0][:, :], ACT.Copy)
            A(v_m[:, 1, :], acc[1][:, :], ACT.Copy).then_inc(S("acc_used"), 1)
            ahead(u, u)

            def softmax_heads(n, base, ob):
                for hd in range(n):
                    g = base + hd
                    act.wait_ge(S("sm_max"), g + 1)
                    if g >= 2:
                        act.wait_ge(S("sm_turned"), g - 1)
                    pb = g % 2
                    A(prob[:, pb, 0:128], smx[:, pb, 0:128], ACT.Exp, bias=stat[:, pb, 0, 0:1], accum_out=stat[:, pb, 1, 0:1])
                    A(prob[:, pb, 128:384], smx[:, pb, 128:384], ACT.Exp, bias=stat[:, pb, 0, 1:2],
                      accum_out=stat[:, pb, 1, 1:2]).then_inc(S("sm_exp"), 1)
                    if hd >= 1:
                        after(g - 1, hd - 1, ob)
                after(base + n - 1, n - 1, ob)

            def after(g, hd, ob):
                act.wait_ge(S("sm_turned"), g + 1)
                if g >= 2:
                    act.wait_ge(S("pv_done"), pv(g - 1))
                A(probT[:, g % 2, :], misc[2 + hd % 2][:, 0:384], ACT.Copy).then_inc(S("sm_turned_copied"), 1)
                if hd % 2:
                    o_high(hd // 2, ob, pv(g + 1))

            def pv(g):
                return g if g <= 8 else g + 8

            def o_high(m, ob, pvs):
                act.wait_ge(S("pv_done"), pvs)
                A(x_hi[:, ob + m, 0:SEQ], acc[m % 4][:, 0:SEQ], ACT.Copy).then_inc(S("x_hi"), 1)

            softmax_heads(8, 0, 0)
            for hd in range(8):
                pb = hd % 2
                act.wait_ge(S("sb_logits"), hd + 1)
                A(smx[:, pb, :], misc[hd % 2][:, 0:384], ACT.Abs).then_inc(S("sb_act"), 1)
                act.wait_ge(S("sb_act"), 3 * hd + 1)
                A(smx[:, pb, :], smx[:, pb, :], ACT.Exp, scale=-1.0).then_inc(S("sb_act"), 1)
                act.wait_ge(S("sb_act"), 3 * hd + 2)
                A(smx[:, pb, :], smx[:, pb, :], ACT.Ln, bias=1.0).then_inc(S("sb_act"), 1)
                act.wait_ge(S("sb_min"), hd + 1)
                if hd >= 2:
                    act.wait_ge(S("pv_done"), 8 + hd - 1)
                A(probT[:, pb, :], sb_log[:, pb, :], ACT.Exp).then_inc(S("sb_att"), 1)
                if hd % 2:
                    o_high(hd // 2, 4, 8 + hd + 1)
            x_hi_n[0] += 8
            out_phase(U["m_out"], 8)
            layer_norm(4, SEQ)

            def ffn_and_ple(i, n, up, dn, proj, gate):
                up_phase(up, SEQ, None)
                down_phase(dn)
                layer_norm(n, SEQ)
                for j in range(2):
                    u = proj + j
                    act.wait_ge(S("unit_done"), u + 1)
                    if i == 1 and j == 0:
                        act.wait_ge(S("ple_h"), KT)
                    for m in range(4):
                        a = A(pp[:, 4 * j + m, :], acc[m][:, 0:SEQ], ACT.Copy)
                    a.then_inc(S("acc_used"), 1)
                    ahead(u, u)
                for m in range(KT):
                    u = gate + m
                    act.wait_ge(S("unit_done"), u + 1)
                    if m >= 2:
                        act.wait_ge(S("ple_h"), KT * i + m - 1)
                    A(sl[:, m % 2, 0:SEQ], acc[u % RING][:, 0:SEQ], ACT.Sigmoid, bias=par_col(f"ple_b{i}", m)).then_inc(S("acc_used"), 1)
                    ahead(u, u)

            ffn_and_ple(0, 5, U["up2"], U["down2"], U["proj0"], U["gate0"])
            act.wait_ge(S("ple_h"), KT)
            act.wait_ge(S("unit_done"), U["gate0"] + 8)
            for k in range(4):
                A(x_hi[:, 2 * k:2 * k + 2, 0:SEQ], h[:, 2 * k:2 * k + 2, 0:SEQ], ACT.Copy).then_inc(S("x_hi"), 1)
            x_hi_n[0] += 4

            u = U["f_f"]
            act.wait_ge(S("unit_done"), u + 1)
            A(fl[0:16, 0, :], acc[u % RING][0:16, 0:SEQ], ACT.Identity, bias=prm[0:16, PC["b_f"]:PC["b_f"] + 1]).then_inc(S("acc_used"), 1)
            ahead(u, u)
            for j in range(16):
                u = U["f_qk"] + j
                act.wait_ge(S("unit_done"), u + 1)
                dst = (q_f if j < 8 else k_f)[:, j % 8, :]
                A(dst, acc[u % RING][:, 0:SEQ], ACT.Copy, scale=0.125 if j < 8 else 1.0).then_inc(S("acc_used"), 1)
                ahead(u, u)
            act.wait_ge(S("acc_used"), U["f_f"] + 1)
            A(fl[0:16, 1, :], fl[0:16, 0, :], ACT.Abs).then_inc(S("f_act"), 1)
            act.wait_ge(S("f_act"), 1)
            A(fl[0:16, 1, :], fl[0:16, 1, :], ACT.Exp, scale=-1.0).then_inc(S("f_act"), 1)
            act.wait_ge(S("f_act"), 2)
            A(fl[0:16, 1, :], fl[0:16, 1, :], ACT.Ln, bias=1.0).then_inc(S("f_act"), 1)
            for g in range(2):
                for j in range(4):
                    u = U["f_v"] + 4 * g + j
                    act.wait_ge(S("unit_done"), u + 1)
                    ahead(u, u)
                A(v_f[:, 0, g, :], acc[0][:, :], ACT.Copy).then_inc(S("acc_used"), 2)
                A(v_f[:, 1, g, :], acc[1][:, :], ACT.Copy).then_inc(S("acc_used"), 2)
            act.wait_ge(S("dcum_turned"), 1)
            A(dcum_col[:, :, :], misc[0][:, 0:32].rearrange("p (a n) -> p a n", a=2), ACT.Copy).then_inc(S("dcum_copied"), 1)
            softmax_heads(16, 8, 0)
            x_hi_n[0] += 8
            out_phase(U["f_out"], 8)
            layer_norm(6, SEQ)
            ffn_and_ple(1, 7, U["up3"], U["down3"], U["proj1"], U["gate1"])

        @block.vector
        def _(dve):
            V = nc.vector
            x_hi_n = [0]
            x_sets = [0]

            def split(u, s):
                if s >= NU:
                    return
                slot = s % RING
                dve.wait_ge(S("hi_ready"), u + 1)
                V.tensor_tensor(w_lo[:, slot, :], raw[:, slot, :], w_hi[:, slot, :].bitcast(F32), ALU.subtract).then_inc(S("lo_ready"), 1)

            def ahead(u, s):
                split(u + RING, s + RING)

            def x_low(src, N, step):
                for k in range(0, KT, step):
                    x_hi_n[0] += 1
                    dve.wait_ge(S("x_hi"), x_hi_n[0] + 0)
                    a = V.tensor_tensor(x_lo[:, k:k + step, 0:N], src[:, k:k + step, 0:N], x_hi[:, k:k + step, 0:N].bitcast(F32), ALU.subtract)
                a.then_inc(S("x_ready"), 1)

            def layer_norm(n, N):
                dve.wait_ge(S("ln_sum"), n + 1)
                mean = misc[0][:, 0:N].unsqueeze(1).to_broadcast([P, 2, N])
                for j in range(4):
                    t = r[:, 2 * j:2 * j + 2, 0:N]
                    V.scalar_tensor_tensor(out=t, in0=mean, scalar=-1.0 / D, in1=t, op0=ALU.mult, op1=ALU.add).then_inc(S("ln_centred"), 1)
                dve.wait_ge(S("ln_std"), n + 1)
                V.reciprocal(rstd[:, 0, 0:N], std[:, 0, 0:N]).then_inc(S("ln_rstd"), 1)
                dve.wait_ge(S("ln_rstd"), n + 1)
                rs = rstd[:, 0, 0:N].unsqueeze(1).to_broadcast([P, 2, N])
                for j in range(4):
                    t = r[:, 2 * j:2 * j + 2, 0:N]
                    dve.wait_ge(S("ln_sq"), 4 * n + j + 1)
                    V.tensor_tensor(t, t, rs, ALU.mult).then_inc(S("ln_scaled"), 1)
                for k in range(KT):
                    dve.wait_ge(S("ln_scaled"), 4 * n + k // 2 + 1)
                    a = V.tensor_scalar(h[:, k, 0:N], r[:, k, 0:N], par_col(f"ln_g{n}", k), par_col(f"ln_b{n}", k), ALU.mult, ALU.add)
                    a.then_inc(S("ln_h"), 1)
                for k in range(KT):
                    x_hi_n[0] += 1
                    dve.wait_ge(S("x_hi"), x_hi_n[0])
                    dve.wait_ge(S("ln_h"), 8 * n + k + 1)
                    a = V.tensor_tensor(x_lo[:, k, 0:N], h[:, k, 0:N], x_hi[:, k, 0:N].bitcast(F32), ALU.subtract)
                a.then_inc(S("x_ready"), 1)

            V.memset(eps[:, 0:1], 1e-5)
            V.memset(eps[:, 1:2], 1e-6).then_inc(S("eps_set"), 1)
            V.memset(ba[:, 0:PAD], 0.0)
            V.memset(kqv[:, :, 0:PAD], 0.0).then_inc(S("zeroed"), 1)
            dve.wait_ge(S("h0_in"), 16)
            x_low(h, L, 2)
            for u in range(RING):
                split(u, u)
            dve.wait_ge(S("prm_in"), 16)
            dve.wait_ge(S("con_in"), 16)
            dve.wait_ge(S("ba_copied"), 1)
            dve.sem_inc(S("acc_used"), 1)
            ahead(U["ba"], U["ba"])

            def kqv_unit(u, s, j):
                a, c = acc[s % RING], conv_a[:, (s - U["kqv"]) % 2, :]
                dve.wait_ge(S("tap0"), j + 1)
                for n in range(1, 4):
                    if n > 1:
                        dve.wait_ge(S("taps"), j * 2 + (n - 1))
                    v = V.scalar_tensor_tensor(out=c[:, n:L], in0=a[:, 0:L - n], scalar=par_col("a_conv", j * 4 + (3 - n)), in1=c[:, n:L], op0=ALU.mult, op1=ALU.add)
                    v.then_inc(S("taps" if n < 3 else "taps_done"), 1)
                dve.wait_ge(S("taps_done"), j + 1)
                dve.sem_inc(S("acc_used"), 1)
                ahead(u, s)

            units(dve, U["kqv"], 24, kqv_unit)
            units(dve, U["z"], 8, lambda u, s, j: ahead(u, s))

            tk = lambda i: tok[:, i, :, :]
            turned = misc[0][:, 0:192].rearrange("p (t c) -> p t c", t=3)
            chain = [0]

            def link(ins):
                chain[0] += 1
                ins.then_inc(S("gate_chain"), 1)
                dve.wait_ge(S("gate_chain"), chain[0])

            dtb = prm[:, PC["dt_bias"]:PC["dt_bias"] + 8].unsqueeze(1).to_broadcast([P, 3, 8])
            dve.wait_ge(S("tok_act"), 1)
            V.tensor_tensor(tk(3), turned[:, :, 32:40], dtb, ALU.add).then_inc(S("tok_dve"), 1)
            link(V.tensor_scalar(tk(2), tk(2), 1.0, None, ALU.add))
            link(V.reciprocal(tk(0), tk(2)))
            link(V.tensor_scalar(tok[:, 0, 0, :], tok[:, 0, 0, :], C("live0"), None, ALU.mult))
            dve.wait_ge(S("tok_act"), 5)
            dve.wait_ge(S("tok_dve"), 1)
            link(V.scalar_tensor_tensor(out=tk(1), in0=tk(3), scalar=0.0, in1=tk(6), op0=ALU.max, op1=ALU.add))
            link(V.scalar_tensor_tensor(out=tk(1), in0=tk(1), scalar=-1.0, in1=tok[:, 7, 0, :].unsqueeze(1).to_broadcast([P, 3, 8]), op0=ALU.mult, op1=ALU.mult))
            V.tensor_scalar(tok[:, 1, 0, :], tok[:, 1, 0, :], C("live0"), None, ALU.mult).then_inc(S("g_ready"), 1)
            dve.wait_ge(S("g_ready"), 1)
            for j in range(16):
                dve.wait_ge(S("kq_std"), j + 1)
                V.reciprocal(rstd[:, j % 2, :], std[:, j % 2, :]).then_inc(S("kq_rstd"), 1)
                dve.wait_ge(S("kq_rstd"), j + 1)
                V.scalar_tensor_tensor(out=kqv[:, j, :], in0=kqv[:, j, :], scalar=1.0 if j < 8 else float(P) ** -0.5, in1=rstd[:, j % 2, :], op0=ALU.mult, op1=ALU.mult).then_inc(S("kq_normed"), 1)
            dve.wait_ge(S("g_col"), 1)
            gc = misc[3][:, 0:24].rearrange("p (t c) -> p t c", t=3)
            gl = misc[3][:, 24:48].rearrange("p (t c) -> p t c", t=3)
            link(V.tensor_copy(tk(8), gc))
            V.tensor_copy(tk(13), gl).then_inc(S("tok_dve"), 1)
            dve.wait_ge(S("tok_dve"), 2)
            V.tensor_tensor(tk(10), tk(13), tk(8), ALU.subtract).then_inc(S("tok_dve"), 1)
            dve.wait_ge(S("tok_dve"), 3)
            dve.wait_ge(S("tok_act"), 7)
            link(V.tensor_tensor(tk(12), tk(0), tk(9), ALU.mult))
            spread = flat(r, 0, 2, 512).rearrange("p (a n) -> p a n", a=8)
            spread_b = flat(r, 2, 4, 512).rearrange("p (a n) -> p a n", a=8)

            def over_chunk(x):
                return x.unsqueeze(2).to_broadcast([P, HEADS_A, CH])

            def over_heads(x):
                return x.unsqueeze(1).to_broadcast([P, HEADS_A, CH])

            bk = lambda a, rows=slice(0, P): a[rows, :].rearrange("p (a n) -> p a n", a=8)
            for t in range(NPAIR):
                pr = rows_of(t)
                if t:
                    dve.wait_ge(S("g_row"), t)
                V.tensor_tensor(spread, over_chunk(tok[:, 1, t, :]), over_heads(C("tri64")), ALU.mult).then_inc(S("g_spread"), 1)
                if t:
                    dve.wait_ge(S("beta_row"), t)
                V.tensor_tensor(spread_b, over_chunk(tok[:, 0, t, :]), over_heads(C("eye64")), ALU.mult).then_inc(S("beta_spread"), 1)
                dve.wait_ge(S("g_row"), t + 1)
                V.tensor_tensor(T[:, t], bk(misc[0]), over_chunk(tok[:, 8, t, :]), ALU.subtract).then_inc(S("g_diff"), 1)
                dve.wait_ge(S("g_diff"), t + 1)
                V.tensor_scalar(T[:, t], T[:, t], 0.0, None, ALU.min).then_inc(S("g_diff2"), 1)
                dve.wait_ge(S("decay"), t + 1)
                link(V.tensor_tensor(T[:, t], T[:, t], over_heads(C("incl")), ALU.mult))
                dve.wait_ge(S("kk_qk"), t + 1)
                V.tensor_tensor(QK[pr, t], bk(acc[1], pr), T[pr, t], ALU.mult).then_inc(S("qk_kept"), 1)
                link(V.tensor_tensor(E[pr, t], bk(acc[0], pr), T[pr, t], ALU.mult))
                dve.wait_ge(S("qk_kept"), t + 1)
                dve.sem_inc(S("qk_ready"), 1)
                dve.wait_ge(S("beta_row"), t + 1)
                link(V.tensor_tensor(E[pr, t], bk(misc[1], pr), E[pr, t], ALU.mult))
                V.tensor_tensor(E[pr, t], E[pr, t], C("strict", pr).unsqueeze(1).to_broadcast([pr.stop, HEADS_A, CH]), ALU.mult).then_inc(S("e_ready"), 1)
                dve.wait_ge(S("kv_turned"), t + 1)
                for g in range(2):
                    a = V.tensor_tensor(uv[:, t, 4 * g:4 * g + 4, :], bank[6 + g][:, :].rearrange("p (a n) -> p a n", a=4), tok[:, 0, t, 4 * g:4 * g + 4].unsqueeze(2).to_broadcast([P, 4, P]), ALU.mult)
                a.then_inc(S("v_beta"), 1)
            for t in range(NPAIR):
                V.tensor_copy(X[:, t], over_heads(C("eye64")))
                a = V.tensor_copy(Y[:, t], over_heads(C("eye64")))
            a.then_inc(S("xy_init"), 1)
            for lv in range(6):
                for t in range(NPAIR):
                    st, pr = lv * NPAIR + t, rows_of(t)
                    dve.wait_ge(S("ax_done"), st + 1)
                    if lv:
                        dve.wait_ge(S("xt_done"), st - NPAIR + 1)
                    mask = con[pr, CA["levels"] + lv * CH:CA["levels"] + lv * CH + CH].unsqueeze(1).to_broadcast([pr.stop, HEADS_A, CH])
                    V.tensor_tensor(T[pr, t], bk(acc[st % 2], pr), mask, ALU.mult).then_inc(S("t_ready"), 1)
                for t in range(NPAIR):
                    st, pr = lv * NPAIR + t, rows_of(t)
                    dve.wait_ge(S("xt_done"), st + 1)
                    if st == 0:
                        dve.wait_ge(S("xy_init"), 1)
                    V.tensor_tensor(X[pr, t], X[pr, t], bk(misc[2 * (st % 2)], pr), ALU.subtract)
                    V.tensor_tensor(Y[pr, t], Y[pr, t], bk(misc[2 * (st % 2) + 1], pr), ALU.subtract).then_inc(S("xy_ready"), 1)
            for t in range(NPAIR):
                pr = rows_of(t)
                if t:
                    dve.wait_ge(S("w_done"), 2 * t - 1)
                dve.wait_ge(S("kT_ready"), NPAIR)
                V.tensor_tensor(kbg[pr], kT[pr, t], tok[pr, 12, t, :].unsqueeze(2).to_broadcast([pr.stop, HEADS_A, P]), ALU.mult).then_inc(S("kbg_ready"), 1)
                dve.wait_ge(S("u_done"), t + 1)
                for g in range(2):
                    a = V.tensor_copy(uv[pr, t, 4 * g:4 * g + 4, :], acc[g][pr, :].rearrange("p (a n) -> p a n", a=4))
                a.then_inc(S("u_ready"), 1)
            dve.wait_ge(S("kbg_ready"), NPAIR)
            for t in range(NPAIR):
                pr = rows_of(t)
                a = V.tensor_tensor(kT[pr, t], kT[pr, t], tok[pr, 11, t, :].unsqueeze(2).to_broadcast([pr.stop, HEADS_A, P]), ALU.mult)
            a.then_inc(S("kd_ready"), 1)
            for t in range(NPAIR):
                if t == 0:
                    dve.wait_ge(S("g_row"), NPAIR)
                    dve.wait_ge(S("beta_row"), NPAIR)
                if t == 2:
                    dve.wait_ge(S("eg_row"), 1)
                sp2 = flat(r, 0, 4, D)[:, (t % 2) * 512:(t % 2) * 512 + 512].rearrange("p (a n) -> p a n", a=8)
                V.tensor_tensor(sp2, over_chunk(tok[:, 1, t, :]), over_heads(C("tri64")), ALU.mult).then_inc(S("g_spread2"), 1)
            for c in range(NCH):
                t, rows, cols = chunk_of(c)
                dve.wait_ge(S("eg_exp"), c + 1)
                eg = eg_buf[:, c % 2, :].rearrange("p (a n) -> p a n", a=8)
                V.tensor_copy(eg_last[:, c, :], eg[:, :, CH - 1])
                V.tensor_tensor(kqv[:, 8:16, cols], kqv[:, 8:16, cols], eg, ALU.mult).then_inc(S("qg_ready"), 1)
            for c in range(NCH):
                t, rows, cols = chunk_of(c)
                if c:
                    dve.wait_ge(S("ws_done"), c)
                    for g in range(2):
                        a = V.tensor_tensor(uv[rows, t, 4 * g:4 * g + 4, :], uv[rows, t, 4 * g:4 * g + 4, :], acc[g][rows, :].rearrange("p (a n) -> p a n", a=4), ALU.subtract)
                    a.then_inc(S("v_new"), 1)
                if c < NCH - 1:
                    dve.wait_ge(S("kv_done"), c + 1)
                    dve.wait_ge(S("o_done"), c + 1)
                    if c == 0:
                        for g in range(2):
                            a = V.tensor_copy(state[:, 4 * g:4 * g + 4, :], acc[2 + g][:, :].rearrange("p (a n) -> p a n", a=4))
                    else:
                        link(V.tensor_tensor(state[:, :, :], state[:, :, :], eg_last[:, c, :].unsqueeze(2).to_broadcast([P, HEADS_A, P]), ALU.mult))
                        for g in range(2):
                            a = V.tensor_tensor(state[:, 4 * g:4 * g + 4, :], state[:, 4 * g:4 * g + 4, :], acc[2 + g][:, :].rearrange("p (a n) -> p a n", a=4), ALU.add)
                    a.then_inc(S("state_ready"), 1)
                    dve.wait_ge(S("state_ready"), c + 1)
            for hd in range(HEADS_A):
                dve.wait_ge(S("o_std"), hd + 1)
                rs = rstd[:, hd % 2, 0:N_MIX]
                link(V.reciprocal(rs, std[:, hd % 2, 0:N_MIX]))
                link(V.scalar_tensor_tensor(out=rs, in0=rs, scalar=par_col("a_norm", 0), in1=kqv[:, hd, LP - N_MIX:LP], op0=ALU.mult, op1=ALU.mult))
                V.tensor_tensor(r[:, hd, 0:N_MIX], rs, z_gate[:, hd, :], ALU.mult).then_inc(S("o_gated"), 1)
            dve.wait_ge(S("o_gated"), HEADS_A)
            x_low(r, N_MIX, 1)

            def residual(u0, N, off):
                def body(u, s, m):
                    dve.wait_ge(S("unit_done"), u + 1)
                    V.scalar_tensor_tensor(out=at(r, m, slice(0, N)), in0=at(h, m, slice(off, off + N)),
                                           scalar=ALPHA, in1=acc[s % RING][:, 0:N], op0=ALU.mult, op1=ALU.add).then_inc(S("acc_used"), 1)
                    ahead(u, s)
                units(dve, u0, 8, body)

            def down_phase(u0, N, off):
                for j in range(2):
                    ahead(u0 + j, u0 + j)
                with dve.Fori(0, (FT - 6) // RING) as i:
                    for b in range(RING):
                        ahead(i * RING + (u0 + 2 + b), u0 + 2 + b)
                for j in range(FT - 4, FT):
                    ahead(u0 + j, u0 + j)
                dve.wait_ge(S("unit_done"), u0 + FT)
                for j, m in enumerate([4, 5, 6, 7, 0, 1, 2, 3]):
                    V.scalar_tensor_tensor(out=r[:, m, 0:N], in0=h[:, m, off:off + N], scalar=ALPHA, in1=bank[m][:, 0:N], op0=ALU.mult, op1=ALU.add
                                           ).then_inc(S("acc_used"), 1 if j < KT - 1 else FT - KT + 1)

            ups = [0]

            def up_phase(u0, N, conv):
                base = ups[0] * FT
                cbase = sum(up_conv[:ups[0]]) * FT

                def pair(u, s, j):
                    g, sg = s % RING, (s + 1) % RING
                    par = (s - u0) // 2 % 2
                    M = N - 2 if conv is not None else N
                    if conv is not None:
                        dve.wait_ge(S("ffn_tap0"), j + (cbase + 1))
                        c = cv[:, par, 0:M]
                        V.scalar_tensor_tensor(out=c, in0=acc[g][:, 1:N - 1], scalar=par_col(conv, j * 3 + 1), in1=c, op0=ALU.mult, op1=ALU.add).then_inc(S("ffn_tap1"), 1)
                        dve.wait_ge(S("ffn_tap1"), j + (cbase + 1))
                        V.scalar_tensor_tensor(out=c, in0=acc[g][:, 2:N], scalar=par_col(conv, j * 3 + 2), in1=c, op0=ALU.mult, op1=ALU.add).then_inc(S("ffn_taps"), 1)
                    ahead(u, s)
                    dve.wait_ge(S("ffn_silu"), j + (base + 1))
                    dve.wait_ge(S("a_ready"), j + (base + 1))
                    dve.wait_ge(S("unit_done"), u + 2)
                    V.tensor_tensor(av[:, par, 0:M], sl[:, par, 0:M], acc[sg][:, N - M:N], ALU.mult).then_inc(S("ffn_product"), 1)
                    dve.wait_ge(S("ffn_product"), j + (base + 1))
                    dve.sem_inc(S("acc_used"), 2)
                    ahead(u + 1, s + 1)

                with dve.Fori(0, FT // 2) as i:
                    for b in range(2):
                        pair(i * RING + (u0 + 2 * b), u0 + 2 * b, i * 2 + b)
                ups[0] += 1

            residual(U["a_out"], N_MIX, OFF_MIX)
            layer_norm(0, N_MIX)
            up_phase(U["up0"], N_MIX, "f_conv0")
            down_phase(U["down0"], N_FFN0, 2)
            layer_norm(1, N_FFN0)

            def b_tile(u, s, j):
                c, y = cv[:, 0, 0:N_FFN0], cv[:, 1, 0:N_B]
                dve.wait_ge(S("b_c"), j + 1)
                ahead(u, s)
                dve.wait_ge(S("unit_done"), u + 2)
                V.tensor_tensor(c, av[:, 0, 0:N_FFN0], acc[(s + 1) % RING][:, 0:N_FFN0], ALU.mult).then_inc(S("b_cx"), 1)
                dve.wait_ge(S("b_cx"), j + 1)
                V.tensor_scalar(y, c[:, 0:N_B], par_col("b_conv", j * 3), None, ALU.mult).then_inc(S("b_taps"), 1)
                for n in (1, 2):
                    dve.wait_ge(S("b_taps"), j * 3 + n)
                    V.scalar_tensor_tensor(out=y, in0=c[:, n:n + N_B], scalar=par_col("b_conv", j * 3 + n), in1=y, op0=ALU.mult, op1=ALU.add).then_inc(S("b_taps"), 1)
                ahead(u + 1, s + 1)
                dve.wait_ge(S("unit_done"), u + 3)
                dve.wait_ge(S("b_taps"), j * 3 + 3)
                V.tensor_tensor(at(r, j, slice(0, N_B)), y, acc[(s + 2) % RING][:, 2:N_FFN0], ALU.mult).then_inc(S("b_done"), 1)
                dve.wait_ge(S("b_done"), j + 1)
                dve.sem_inc(S("acc_used"), 3)
                ahead(u + 2, s + 2)

            with dve.Fori(0, 2) as i:
                for q in range(4):
                    b_tile(i * 12 + (U["b_in"] + 3 * q), U["b_in"] + 3 * q, i * 4 + q)
            x_low(r, N_B, 2)
            residual(U["b_out"], N_B, 2)
            layer_norm(2, N_B)
            up_phase(U["up1"], N_B, "f_conv1")
            down_phase(U["down1"], SEQ, 2)
            layer_norm(3, SEQ)

            dve.wait_ge(S("p_hi"), 1)
            V.tensor_tensor(p_lo[:, :, :, :], p_raw[:, :, :, :], p_hi[:, :, :, :].bitcast(F32), ALU.subtract).then_inc(S("p_split"), 1)
            rope_rows, swap_rows = slice(64, 96), slice(96, 128)
            ropes = [0]

            def rope(dst, ps):
                n = ropes[0]
                a, b = rope_t[rope_rows, 0, :], rope_t[rope_rows, 1, :]
                V.tensor_tensor(a, ps[swap_rows, 0:SEQ], CBv("rope", swap_rows), ALU.mult)
                V.tensor_tensor(b, ps[rope_rows, 0:SEQ], CBv("rope", rope_rows), ALU.mult).then_inc(S("rope_parts"), 1)
                dve.wait_ge(S("rope_parts"), n + 1)
                ropes[0] += 1
                return V.tensor_tensor(dst, a, b, ALU.add)

            dve.wait_ge(S("con_b_in"), 16)
            for j in range(5):
                u = U["m_in"] + j
                dve.wait_ge(S("unit_done"), u + 1)
                if j < 4:
                    dve.wait_ge(S("c_sq"), j + 1)
                    V.tensor_copy(r[:, j, 0:SEQ], acc[u % RING][:, 0:SEQ]).then_inc(S("acc_used"), 1)
                else:
                    rope(rope_t[rope_rows, 0, :], acc[u % RING]).then_inc(S("acc_used"), 1)
                    dve.wait_ge(S("acc_used"), u + 1)
                    V.tensor_copy(k_m[rope_rows, :, :], rope_t[rope_rows, 0, :].unsqueeze(1).to_broadcast([32, 8, SEQ])).then_inc(S("k_rope"), 1)
                ahead(u, u)
            for j in range(12):
                ahead(U["m_sbqk"] + j, U["m_sbqk"] + j)
            for j in range(2):
                dve.wait_ge(S("c_std"), j + 1)
                sd = std[:, j, 0:SEQ]
                V.reciprocal(sd, sd).then_inc(S("c_rstd"), 1)
                dve.wait_ge(S("c_rstd"), j + 1)
                for m in range(2):
                    V.scalar_tensor_tensor(out=r[:, 4 + 2 * j + m, 0:SEQ], in0=r[:, 2 * j + m, 0:SEQ], scalar=par_col("q_norm" if j == 0 else "kv_norm", m), in1=sd, op0=ALU.mult, op1=ALU.mult).then_inc(S("c_normed"), 1)
            for j in range(4):
                dve.wait_ge(S("c_hi"), j + 1)
                dve.wait_ge(S("c_normed"), j + 1)
                V.tensor_tensor(c_lo[:, j, :], r[:, 4 + j, 0:SEQ], c_hi[:, j, :].bitcast(F32), ALU.subtract).then_inc(S("c_ready"), 1)
            for j in range(2):
                u = U["m_uq"] + j
                dve.wait_ge(S("unit_done"), u + 1)
                for m in range(4):
                    a = rope(q_m[rope_rows, 4 * j + m, :], acc[m])
                    a.then_inc(S("q_rope"), 1)
                    dve.wait_ge(S("q_rope"), 4 * j + m + 1)
                dve.wait_ge(S("q_nope"), 4 * j + 4)
                dve.sem_inc(S("acc_used"), 1)
                ahead(u, u)
            ahead(U["m_ukn"], U["m_ukn"])
            ahead(U["m_ukv"], U["m_ukv"])
            dve.wait_ge(S("k_rope"), 1)
            dve.sem_inc(S("m_ready"), 1)

            def softmax_heads(n, base, scale, mask, ob, dcum):
                for hd in range(n + 1):
                    g = base + hd
                    pb = g % 2
                    if hd < n:
                        dve.wait_ge(S("sm_scores"), g + 1)
                        if g >= 2:
                            dve.wait_ge(S("sm_exp"), g - 1)
                        s = smx[:, pb, :]
                        if dcum is None:
                            V.scalar_tensor_tensor(out=s, in0=misc[hd % 2][:, 0:384], scalar=scale, in1=mask, op0=ALU.mult, op1=ALU.add).then_inc(S("sm_masked"), 1)
                        else:
                            V.scalar_tensor_tensor(out=s[:, 0:128], in0=misc[hd % 2][:, 0:128], scalar=dcum[:, 0, hd:hd + 1], in1=mask[:, 0:128], op0=ALU.add, op1=ALU.add)
                            V.scalar_tensor_tensor(out=s[:, 128:384], in0=misc[hd % 2][:, 128:384], scalar=dcum[:, 1, hd:hd + 1], in1=mask[:, 128:384], op0=ALU.add, op1=ALU.add).then_inc(S("sm_masked"), 1)
                        dve.wait_ge(S("sm_masked"), g + 1)
                        V.tensor_reduce(stat[:, pb, 2, 0:1], s[:, 0:128], AX, ALU.max)
                        V.tensor_reduce(stat[:, pb, 2, 1:2], s[:, 128:384], AX, ALU.max).then_inc(S("sm_top"), 1)
                        dve.wait_ge(S("sm_top"), g + 1)
                        V.tensor_scalar(stat[:, pb, 0, :], stat[:, pb, 2, :], -1.0, None, ALU.mult).then_inc(S("sm_max"), 1)
                    if hd >= 1:
                        g, pb = g - 1, (g - 1) % 2
                        dve.wait_ge(S("sm_exp"), g + 1)
                        V.reciprocal(stat[:, pb, 1, :], stat[:, pb, 1, :]).then_inc(S("sm_recip"), 1)
                        dve.wait_ge(S("sm_recip"), g + 1)
                        V.tensor_scalar(prob[:, pb, 0:128], prob[:, pb, 0:128], stat[:, pb, 1, 0:1], None, ALU.mult)
                        V.tensor_scalar(prob[:, pb, 128:384], prob[:, pb, 128:384], stat[:, pb, 1, 1:2], None, ALU.mult).then_inc(S("sm_probs"), 1)
                    if hd >= 3 and hd % 2 == 1:
                        o_low(hd // 2 - 1, ob)
                o_low(n // 2 - 1, ob)

            def o_low(m, ob):
                x_hi_n[0] += 1
                dve.wait_ge(S("x_hi"), x_hi_n[0])
                V.tensor_tensor(x_lo[:, ob + m, 0:SEQ], acc[m % 4][:, 0:SEQ], x_hi[:, ob + m, 0:SEQ].bitcast(F32), ALU.subtract).then_inc(S("o_split"), 1)

            softmax_heads(8, 0, 96.0 ** -0.5, CBv("mla_mask"), 0, None)
            for hd in range(8):
                pb = hd % 2
                dve.wait_ge(S("sb_act"), 3 * hd + 3)
                rem = prob[:, pb, :]
                if hd >= 2:
                    dve.wait_ge(S("sb_sum"), hd - 1)
                V.scalar_tensor_tensor(out=rem, in0=misc[hd % 2][:, 0:384], scalar=0.0, in1=smx[:, pb, :], op0=ALU.max, op1=ALU.add).then_inc(S("sb_soft"), 1)
                dve.wait_ge(S("sb_soft"), hd + 1)
                V.tensor_tensor(rem, rem, CBv("sb_past"), ALU.mult).then_inc(S("sb_rem"), 1)
                dve.wait_ge(S("sb_sum"), hd + 1)
                if hd >= 2:
                    dve.wait_ge(S("sb_att"), hd - 1)
                V.scalar_tensor_tensor(out=sb_log[:, pb, :], in0=misc[2 + hd % 2][:, 0:384], scalar=0.0, in1=CBv("sb_mask"), op0=ALU.min, op1=ALU.add).then_inc(S("sb_min"), 1)
                if hd % 2:
                    o_low(hd // 2, 4)
            dve.wait_ge(S("o_split"), 8)
            dve.sem_inc(S("x_ready"), 1)
            residual(U["m_out"], SEQ, 0)
            layer_norm(4, SEQ)

            def ffn_and_ple(i, n, up, dn, proj, gate):
                up_phase(up, SEQ, None)
                down_phase(dn, SEQ, 0)
                layer_norm(n, SEQ)
                for j in range(2):
                    ahead(proj + j, proj + j)
                for m in range(KT):
                    u = gate + m
                    dve.wait_ge(S("acc_used"), u + 1)
                    g = sl[:, m % 2, 0:SEQ]
                    link(V.tensor_tensor(g, g, pp[:, m, :], ALU.mult))
                    V.tensor_tensor(h[:, m, 0:SEQ], h[:, m, 0:SEQ], g, ALU.add).then_inc(S("ple_h"), 1)
                    ahead(u, u)
                dve.wait_ge(S("ple_h"), KT * (i + 1))

            ffn_and_ple(0, 5, U["up2"], U["down2"], U["proj0"], U["gate0"])
            x_low(h, SEQ, 2)

            ahead(U["f_f"], U["f_f"])
            for j in range(16):
                ahead(U["f_qk"] + j, U["f_qk"] + j)
            dve.wait_ge(S("f_act"), 3)
            link(V.scalar_tensor_tensor(out=fl[0:16, 2, :], in0=fl[0:16, 0, :], scalar=0.0, in1=fl[0:16, 1, :], op0=ALU.min, op1=ALU.subtract))
            link(V.memset(fl[0:16, 0, :], 1.0))
            link(V.tensor_tensor_scan(fl[0:16, 3, :], fl[0:16, 0, :], fl[0:16, 2, :], 0.0, ALU.mult, ALU.add))
            V.tensor_scalar(fl[0:16, 4, :], fl[0:16, 3, :], -1.0, None, ALU.mult).then_inc(S("dcum"), 1)
            for j in range(8):
                ahead(U["f_v"] + j, U["f_v"] + j)
            dve.wait_ge(S("dcum_copied"), 1)
            softmax_heads(16, 8, 1.0, CBv("fox_mask"), 0, dcum_col)
            dve.wait_ge(S("o_split"), 16)
            dve.sem_inc(S("x_ready"), 1)
            residual(U["f_out"], SEQ, 0)
            layer_norm(6, SEQ)
            ffn_and_ple(1, 7, U["up3"], U["down3"], U["proj1"], U["gate1"])

        @block.gpsimd
        def _(pool):
            pool.sem_inc(S("a_ready"), 2)
            for n, N in enumerate([N_FFN0, SEQ, SEQ, SEQ]):
                with pool.Fori(0, FT // 2) as i:
                    for b in range(2):
                        j = i * 2 + b
                        pool.wait_ge(S("a_hi"), j + (n * FT + 1))
                        nc.gpsimd.tensor_tensor(at(a_lo, j, slice(0, N)), av[:, b, 0:N],
                                                at(a_hi, j, slice(0, N)).bitcast(F32), ALU.subtract).then_inc(S("a_ready"), 1)


def _constants():
    p, f = np.arange(P)[:, None], np.arange(CH)[None, :]
    pc = p % CH
    a = np.zeros((P, NCA), np.float32)

    def put(into, cols, name, value):
        into[:, cols[name]:cols[name] + value.shape[1]] = value

    full = np.arange(P)[None, :]
    same = p // CH == full // CH
    put(a, CA, "ident", np.eye(P))
    put(a, CA, "ones", np.ones((P, P)))
    put(a, CA, "half_ones", same * 1.0)
    put(a, CA, "half_tri", (same & (p <= full)) * 1.0)
    put(a, CA, "tri64", (pc <= f) * 1.0)
    put(a, CA, "eye64", (pc == f) * 1.0)
    put(a, CA, "incl", (f >= pc) * 1.0)
    put(a, CA, "strict", (f > pc) * 1.0)
    levels = [(pc // (2 * s) == f // (2 * s)) & (pc // s % 2 == 1) & (f // s % 2 == 0) for s in (1, 2, 4, 8, 16, 32)]
    put(a, CA, "levels", np.concatenate(levels, 1) * 1.0)
    put(a, CA, "live0", ((p >= PAD) & (p < CH)) * 1.0)
    b = np.zeros((P, NCB), np.float32)
    zero = np.zeros((P, P))
    blocks = np.where(p // CH >= full // CH, 0.0, NEG)
    put(b, CB, "mla_mask", np.concatenate([blocks, zero, blocks], 1))
    causal = np.where(p >= full, 0.0, NEG)
    put(b, CB, "fox_mask", np.concatenate([causal, zero, causal], 1))
    past = np.where(p < full, 0.0, NEG)
    put(b, CB, "sb_mask", np.concatenate([past, zero, past], 1))
    put(b, CB, "sb_past", np.concatenate([p < full, zero == 0, p < full], 1) * 1.0)
    put(b, CB, "neg_tri", -1.0 * (p >= full))
    put(b, CB, "neg_ones", -np.ones((P, P)))
    dim = 32
    inv = (1.0 / (np.float32(10000.0) ** (np.arange(0, dim, 2, dtype=np.float32) / np.float32(dim)))).astype(np.float32)
    ang = np.arange(SEQ, dtype=np.float32)[None, :] * inv[:, None]
    cos, sin = np.cos(ang).astype(np.float32), np.sin(ang).astype(np.float32)
    rope = np.zeros((P, SEQ), np.float32)
    rope[64:96] = np.concatenate([cos, cos])
    rope[96:128] = np.concatenate([-sin, sin])
    put(b, CB, "rope", rope)
    sel = np.zeros((P, 16, P))
    for hd in range(16):
        sel[hd, hd] = 1.0
    put(b, CB, "sel", sel.reshape(P, 16 * P))
    return a, b


def _stream(v):
    w = np.zeros((NU, P, D), np.float32)

    def panel(u, m):
        t = np.zeros((D, P), np.float32)
        t[:, :m.shape[1]] = m
        w[u] = t.reshape(KT, P, P).transpose(1, 0, 2).reshape(P, D)

    def panels(name, m, first=0, step=1):
        for j in range(m.shape[1] // P):
            panel(U[name] + first + step * j, m[:, j * P:j * P + P])

    def wide(u, m):
        w[u] = m.reshape(2, P, 512).transpose(1, 0, 2).reshape(P, D)

    ain = v["a_w_in"][0]
    ba = np.zeros((D, 64), np.float32)
    ba[:, 0:8], ba[:, 32:40] = ain[:, 4 * D:4 * D + 8], ain[:, 4 * D + 8:4 * D + 16]
    panel(U["ba"], ba)
    panels("kqv", ain[:, D:2 * D])
    panels("kqv", ain[:, 0:D], 8)
    panels("kqv", ain[:, 2 * D:3 * D], 16)
    panels("z", ain[:, 3 * D:4 * D])
    panels("a_out", v["a_w_out"][0])
    for i in range(2):
        panels(f"up{i}", v["ffn_w_up"][i][:, :FF], 0, 2)
        panels(f"up{i}", v["ffn_w_up"][i][:, FF:], 1, 2)
        w[U[f"down{i}"]:U[f"down{i}"] + FT] = v["ffn_w_down"][i].reshape(FT, P, D)
        panels(f"up{i + 2}", v["ffn_w1_2"][i], 0, 2)
        panels(f"up{i + 2}", v["ffn_w3_2"][i], 1, 2)
        w[U[f"down{i + 2}"]:U[f"down{i + 2}"] + FT] = v["ffn_w2_2"][i].reshape(FT, P, D)
        for j in range(2):
            wide(U[f"proj{i}"] + j, v["ple_w_proj_2"][i][:, j * 512:j * 512 + 512])
        panels(f"gate{i}", v["ple_w_gate_2"][i])
    bin_ = v["b_w_in"][0]
    for place, c in enumerate((1, 2, 0)):
        panels("b_in", bin_[:, c * D:c * D + D], place, 3)
    panels("b_out", v["b_w_out"][0])
    m = v["a_w_in_2"][0]
    panels("m_in", m[:, 0:512])
    rope = np.zeros((D, P), np.float32)
    rope[:, 64:96] = m[:, 512:544]
    rope[:, 96:112], rope[:, 112:128] = m[:, 528:544], m[:, 512:528]
    panel(U["m_in"] + 4, rope)
    panels("m_sbqk", m[:, 544:544 + D])
    for j in range(4):
        wide(U["m_sbv"] + j, m[j * 256:j * 256 + 256, 544 + D:])
    uq = v["a_w_uq_2"][0].reshape(256, 8, 96)
    uq = np.concatenate([uq, uq[:, :, 80:96], uq[:, :, 64:80]], 2).reshape(256, D)
    ukv = v["a_w_ukv_2"][0].reshape(256, 8, P)
    for j in range(2):
        wide(U["m_uq"] + j, uq[:, j * 512:j * 512 + 512])
    wide(U["m_ukn"], ukv[:, :, 0:64].reshape(256, 512))
    wide(U["m_ukv"], ukv[:, :, 64:].reshape(256, 512))
    panels("m_out", v["a_w_out_2"][0])
    f = v["c_w_in_2"][0]
    panel(U["f_f"], f[:, 3 * D:])
    panels("f_qk", f[:, 0:2 * D])
    for g in range(2):
        for j in range(4):
            wide(U["f_v"] + 4 * g + j, f[j * 256:j * 256 + 256, 2 * D + g * 512:2 * D + g * 512 + 512])
    panels("f_out", v["c_w_out_2"][0])
    return w


def _parameters(v):
    par = np.zeros((P, NPC), np.float32)

    def put(name, a):
        t = a.reshape(-1, P, a.shape[1]).transpose(1, 0, 2).reshape(P, -1)
        par[:, PC[name]:PC[name] + t.shape[1]] = t

    conv = v["a_conv"][0]
    put("a_conv", np.concatenate([conv[:, D:2 * D], conv[:, 0:D], conv[:, 2 * D:]], 1).T)
    put("b_conv", v["b_conv"][0].T)
    for i in range(2):
        put(f"f_conv{i}", v["ffn_conv"][i].T)
        put(f"ple_b{i}", v["ple_b_gate_2"][i][:, None])
        for n, name in enumerate(("ln_mix", "ln_ffn")):
            put(f"ln_g{2 * i + n}", v[name + "_g"][i][:, None])
            put(f"ln_b{2 * i + n}", v[name + "_b"][i][:, None])
        for n, name in enumerate(("ln1", "ln2")):
            put(f"ln_g{4 + 2 * i + n}", v[name + "_g_2"][i][:, None])
            put(f"ln_b{4 + 2 * i + n}", v[name + "_b_2"][i][:, None])
    put("a_norm", v["a_norm"][0][:, None])
    put("q_norm", v["a_q_norm_2"][0][:, None])
    put("kv_norm", v["a_kv_norm_2"][0][:, None])
    par[0:16, PC["b_f"]] = v["c_b_f_2"][0]
    par[:, PC["a_log"]:PC["a_log"] + 8] = v["a_log"][0][None, :]
    par[:, PC["dt_bias"]:PC["dt_bias"] + 8] = v["a_dt_bias"][0][None, :]
    return par


def kernel(**inputs):
    import concourse.bacc as bacc
    from concourse.bass_utils import run_bass_kernel_spmd

    v = {k: np.asarray(a) for k, a in inputs.items()}
    tokens = np.concatenate([v["meta"], v["x"][0]], 0)
    ca, cb = _constants()
    arrays = {
        "w": _stream(v),
        "h0": np.ascontiguousarray(tokens.T.reshape(KT, P, L).transpose(1, 0, 2)),
        "par": _parameters(v),
        "ca": ca,
        "cb": cb,
        "pin": np.ascontiguousarray(v["p_2"][:, 0].transpose(0, 2, 1).reshape(2, 2, P, SEQ).transpose(2, 0, 1, 3)),
    }
    nc = bacc.Bacc("TRN2", target_bir_lowering=False, num_devices=1)
    args = {k: nc.dram_tensor(k, a.shape, F32, kind="ExternalInput").ap() for k, a in arrays.items()}
    out = nc.dram_tensor("out", (P, KT, SEQ), F32, kind="ExternalOutput").ap()
    build(nc, **args, out=out)
    got = run_bass_kernel_spmd(nc, [arrays], core_ids=[0]).results[0]["out"]
    return np.ascontiguousarray(np.asarray(got).transpose(2, 1, 0).reshape(1, SEQ, D))
```

```python
from contextlib import ExitStack

import numpy as np

import concourse.bass as bass
from concourse import mybir

F32 = mybir.dt.float32
F32R = mybir.dt.float32r
ALU = mybir.AluOpType
ACT = mybir.ActivationFunctionType
AX = mybir.AxisListType.X

P = 128
D = 1024
KT = D // P
SEQ, META = 256, 16
L = SEQ + META
FF = 2816
FT = FF // P
HEADS_A = 8
CH = 64
PAD = CH - META
LP = L + PAD
NCH = LP // CH
NPAIR = 3
ALPHA = 4.0 ** 0.25
RING = 4
N_MIX, N_FFN0, N_B, N_FFN1 = SEQ + 6, SEQ + 4, SEQ + 2, SEQ
OFF_MIX = L - N_MIX

_SIZES = [("ba", 1), ("kqv", 24), ("z", 8), ("a_out", 8), ("up0", 2 * FT), ("down0", FT), ("b_in", 24), ("b_out", 8),
          ("up1", 2 * FT), ("down1", FT), ("m_in", 5), ("m_sbqk", 8), ("m_sbv", 4), ("m_uq", 2), ("m_ukn", 1), ("m_ukv", 1),
          ("m_out", 8), ("up2", 2 * FT), ("down2", FT), ("proj0", 2), ("gate0", 8), ("f_f", 1), ("f_qk", 16), ("f_v", 8),
          ("f_out", 8), ("up3", 2 * FT), ("down3", FT), ("proj1", 2), ("gate1", 8)]
U = {}
NU = 0
for _n, _c in _SIZES:
    U[_n] = NU
    NU += _c

_PARAMS = [("a_conv", 24 * 4), ("b_conv", 8 * 3), ("f_conv0", FT * 3), ("f_conv1", FT * 3), ("a_norm", 1),
           ("q_norm", 2), ("kv_norm", 2), ("ple_b0", 8), ("ple_b1", 8), ("b_f", 1), ("a_log", 8), ("dt_bias", 8)]
_PARAMS += [(f"ln_g{i}", 8) for i in range(8)] + [(f"ln_b{i}", 8) for i in range(8)]
PC = {}
NPC = 0
for _n, _c in _PARAMS:
    PC[_n] = NPC
    NPC += _c

_CONST_A = [("ident", P), ("ones", P), ("half_ones", P), ("half_tri", P), ("tri64", CH), ("eye64", CH), ("incl", CH),
            ("levels", 6 * CH), ("pair_up", CH), ("one_col", 31), ("live0", 1)]
_CONST_B = [("mla_mask", 384), ("fox_mask", 384), ("sb_mask", 384), ("sb_past", 384), ("neg_tri", P), ("neg_ones", P),
            ("rope", SEQ), ("sel", 16 * P)]


def _columns(names):
    at, n = {}, 0
    for name, c in names:
        at[name] = n
        n += c
    return at, n


CA, NCA = _columns(_CONST_A)
CB, NCB = _columns(_CONST_B)
NEG = -1.0e30
DOWN_ORDER = [4, 5, 6, 7, 0, 1, 2, 3]


def build(nc, w, h0, par, ca, cb, pin, out):
    with ExitStack() as ctx:
        sems = {}

        def S(name):
            if name not in sems:
                sems[name] = ctx.enter_context(nc.semaphore(name))
            return sems[name]

        def sb(name, shape, dt=F32, where=ctx):
            return where.enter_context(nc.sbuf_tensor(name, shape, dt))

        raw = sb("raw", [P, RING, D])
        w_hi = sb("w_hi", [P, RING, D], F32R)
        w_lo = sb("w_lo", [P, RING, D], F32R)
        h = sb("h", [P, KT, L])
        r = sb("r", [P, KT, L])
        sq = sb("sq", [P, KT, L])
        x_hi = sb("x_hi", [P, KT, L], F32R)
        x_lo = sb("x_lo", [P, KT, L], F32R)
        prm = sb("prm", [P, NPC])
        con = sb("con", [P, NCA])
        std = sb("std", [P, 2, LP])
        rstd = sb("rstd", [P, 2, LP])
        eps = sb("eps", [P, 2])
        warm = sb("warm", [P, 8])
        bank = [ctx.enter_context(nc.psum_tensor(f"bank{i}", [P, 512], F32)) for i in range(8)]
        acc, misc = bank[:4], bank[4:]

        def C(name, rows=slice(0, P), n=None):
            n = dict(_CONST_A)[name] if n is None else n
            return con[rows, CA[name]:CA[name] + n]

        def par_col(name, j):
            return prm[:, bass.ds(PC[name] + j, 1)] if not isinstance(j, int) else prm[:, PC[name] + j:PC[name] + j + 1]

        def col_sum(j, n):
            return con[:, CA["one_col"] + 15 - j:CA["one_col"] + 15 - j + n]

        def flat(t, a, b, n):
            return t[:, a:b, :].rearrange("p a n -> p (a n)")[:, 0:n]

        conv_a = r[:, 0:2, :]

        def kq_slot(i):
            return sq[:, :, :].rearrange("p a n -> p (a n)")[:, i * LP:i * LP + LP]

        kbg = flat(r, 4, 8, D).rearrange("p (a n) -> p a n", a=HEADS_A)
        eg_buf = flat(sq, 4, 8, D).rearrange("p (b n) -> p b n", b=2)
        with ExitStack() as gdn:
            kqv = sb("kqv", [P, 24, LP], where=gdn)
            kT = sb("kT", [P, NPAIR, HEADS_A, P], where=gdn)
            uv = sb("uv", [P, NPAIR, HEADS_A, P], where=gdn)
            E = sb("E", [P, NPAIR, HEADS_A, CH], where=gdn)
            X = sb("X", [P, NPAIR, HEADS_A, CH], where=gdn)
            Y = sb("Y", [P, NPAIR, HEADS_A, CH], where=gdn)
            T = sb("T", [P, NPAIR, HEADS_A, CH], where=gdn)
            QK = sb("QK", [P, NPAIR, HEADS_A, CH], where=gdn)
            state = sb("state", [P, HEADS_A, P], where=gdn)
            ba = sb("ba", [P, LP], where=gdn)
            tok = sb("tok", [P, 14, NPAIR, 8], where=gdn)
            z_gate = sb("z_gate", [P, HEADS_A, N_MIX], where=gdn)
            eg_last = sb("eg_last", [P, NCH, 8], where=gdn)
            states = [state, X[:, :, :, :].rearrange("p t a n -> p (t a n)")[:, 0:D].rearrange("p (a n) -> p a n", a=HEADS_A)]
        cv = sb("cv", [P, 2, N_MIX])
        sl = sb("sl", [P, 2, N_MIX])
        av = sb("av", [P, 2, N_MIX])
        con_b = sb("con_b", [P, NCB])
        p_raw = sb("p_raw", [P, 2, 2, SEQ])
        p_hi = sb("p_hi", [P, 2, 2, SEQ], F32R)
        p_lo = sb("p_lo", [P, 2, 2, SEQ], F32R)
        smx = sb("smx", [P, 2, 384])
        prob = sb("prob", [P, 2, 384])
        probT = sb("probT", [P, 2, 384])
        sb_log = sb("sb_log", [P, 2, 384])
        stat = sb("stat", [P, 2, 3, 2])
        with ExitStack() as ffn:
            a_hi = sb("a_hi", [P, FT, N_FFN0], F32R, where=ffn)
            a_lo = sb("a_lo", [P, FT, N_FFN0], F32R, where=ffn)
        with ExitStack() as ple:
            pp = sb("pp", [P, KT, SEQ], where=ple)
        with ExitStack() as att:
            c_hi = sb("c_hi", [P, 4, SEQ], F32R, where=att)
            c_lo = sb("c_lo", [P, 4, SEQ], F32R, where=att)
            q_m = sb("q_m", [P, 8, SEQ], where=att)
            k_m = sb("k_m", [P, 8, SEQ], where=att)
            v_m = sb("v_m", [P, 2, 512], where=att)
            q_s = sb("q_s", [P, 4, SEQ], where=att)
            k_s = sb("k_s", [P, 4, SEQ], where=att)
            v_s = sb("v_s", [P, 2, 512], where=att)
            rope_t = sb("rope_t", [P, 2, SEQ], where=att)
        with ExitStack() as fox:
            q_f = sb("q_f", [P, 8, SEQ], where=fox)
            k_f = sb("k_f", [P, 8, SEQ], where=fox)
            v_f = sb("v_f", [P, 2, 2, 512], where=fox)
            fl = sb("fl", [P, 5, SEQ], where=fox)
            dcum_col = sb("dcum_col", [P, 2, 16], where=fox)
        up_conv = [1, 1, 0, 0]

        def CBv(name, rows=slice(0, P)):
            return con_b[rows, CB[name]:CB[name] + dict(_CONST_B)[name]]

        block = ctx.enter_context(nc.Block())

        def halves(t):
            return [slice(0, 64)] if t == 0 else [slice(0, 64), slice(64, 128)]

        def rows_of(t):
            return slice(0, 64) if t == 0 else slice(0, P)

        PAIR_AT = [0, CH, 3 * CH]

        def proj_out(gate, j):
            pair = (acc[(gate + 2) % RING], acc[(gate + 3) % RING]) if j == 0 else (misc[2], misc[3])
            return [pair[m // 2][:, (m % 2) * SEQ:(m % 2) * SEQ + SEQ] for m in range(4)]

        def blocks(t, lv, side):
            return t.rearrange("p (b two n) -> p b two n", two=2, n=1 << lv)[:, :, side, :]

        def head_blocks(t, lv, side):
            return t.rearrange("p a (b two n) -> p a b two n", two=2, n=1 << lv)[:, :, :, side, :]

        def chunk_of(c):
            t = (c + 1) // 2
            half = 0 if c == 0 else (c - 1) % 2
            return t, slice(64 * half, 64 * half + 64), slice(CH * c, CH * c + CH)

        @block.sync
        def _(sp):
            sp.dma_start(raw[:, 0, :], w[0]).then_inc(S("raw0"), 16)
            for half in range(2):
                sp.dma_start(h[:, 4 * half:4 * half + 4, :], h0[:, 4 * half:4 * half + 4, :]).then_inc(S(f"h0_in{half}"), 16)
            for u in range(1, RING):
                sp.dma_start(raw[:, u, :], w[u]).then_inc(S(f"raw{u}"), 16)
            n = (NU - RING) // RING
            with sp.Fori(0, n) as i:
                for b in range(RING):
                    sp.wait_ge(S("lo_ready"), i * RING + (b + 1))
                    sp.dma_start(raw[:, b, :], w[bass.ds(i * RING + (RING + b), 1)].rearrange("a p n -> (a p) n")
                                 ).then_inc(S(f"raw{b}"), 16)
            for u in range(RING + n * RING, NU):
                sp.wait_ge(S("lo_ready"), u - RING + 1)
                sp.dma_start(raw[:, u % RING, :], w[u]).then_inc(S(f"raw{u % RING}"), 16)
            for m in range(KT):
                sp.wait_ge(S("ple_h"), KT + m + 1)
                sp.dma_start(out[:, m, :], h[:, m, 0:SEQ]).then_inc(S("stored"), 16)
            sp.wait_ge(S("stored"), 16 * KT)

        def units(eng, u0, n, body):
            pre = RING if u0 < RING < n else 0
            full = (n - pre) // RING
            full = full if full > 1 else 0
            for b in range(pre):
                body(u0 + b, u0 + b, b)
            if full:
                with eng.Fori(0, full) as i:
                    for b in range(RING):
                        body(i * RING + (u0 + pre + b), u0 + pre + b, i * RING + (pre + b))
            for b in range(pre + full * RING, n):
                body(u0 + b, u0 + b, b)

        def at(t, j, cols=slice(None)):
            return t[:, j, cols] if isinstance(j, int) else t[:, bass.ds(j, 1), cols].rearrange("p a n -> p (a n)")

        @block.tensor
        def _(pe):
            x_sets = [0]

            def start_unit(u, s, wait_acc=True):
                pe.wait_ge(S("lo_ready"), u + 1)
                if wait_acc and s >= RING:
                    pe.wait_ge(S("acc_used"), u - (RING - 1))

            def three(o, wh, wl, xh, xl, first, last):
                pe.matmul(o, wh, xh, start=first, stop=False)
                pe.matmul(o, wh, xl, start=False, stop=False)
                return pe.matmul(o, wl, xh, start=False, stop=last)

            def panels(u0, n, N, new_x=False):
                def body(u, s, j, x_before=None):
                    slot = s % RING
                    start_unit(u, s)
                    for k in range(KT):
                        if x_before is not None:
                            pe.wait_ge(S("x_ready"), x_before + k + 1)
                        c = slice(k * P, k * P + P)
                        mm = three(acc[slot][:, 0:N], w_hi[:, slot, c], w_lo[:, slot, c], x_hi[:, k, 0:N],
                                   x_lo[:, k, 0:N], k == 0, k == KT - 1)
                    mm.then_inc(S("unit_done"), 1)
                if new_x:
                    body(u0, u0, 0, KT * x_sets[0])
                    x_sets[0] += 1
                units(pe, u0 + new_x, n - new_x, body)

            def down(u0, N):
                a_before = FT * downs[0] + 2

                def one(u, s, k, first, last):
                    slot = s % RING
                    pe.wait_ge(S("lo_ready"), u + 1)
                    pe.wait_ge(S("a_ready"), k + (a_before + 1))
                    xh, xl = at(a_hi, k, slice(0, N)), at(a_lo, k, slice(0, N))
                    for m in DOWN_ORDER:
                        if first and m == 0:
                            pe.wait_ge(S("acc_used"), u0)
                        c = slice(m * P, m * P + P)
                        mm = three(bank[m][:, 0:N], w_hi[:, slot, c], w_lo[:, slot, c], xh, xl, first, last)
                    mm.then_inc(S("unit_done"), 1)

                for k in range(2):
                    one(u0 + k, u0 + k, k, k == 0, False)
                with pe.Fori(0, (FT - 6) // RING) as i:
                    for b in range(RING):
                        one(i * RING + (u0 + 2 + b), u0 + 2 + b, i * RING + (2 + b), False, False)
                for k in range(FT - 4, FT):
                    one(u0 + k, u0 + k, k, False, k == FT - 1)
                downs[0] += 1

            downs = [0]

            def layer_norm(n, u0, N, from_down, between=lambda: None):
                order = DOWN_ORDER if from_down else list(range(KT))
                for j, m in enumerate(order):
                    pe.wait_ge(S("acc_used"), u0 + (j + 1 if not from_down or j < KT - 1 else FT))
                    mm = pe.matmul(misc[0][:, 0:N], C("ones"), r[:, m, 0:N], start=(j == 0), stop=(j == KT - 1))
                mm.then_inc(S("ln_sum"), 1)
                between()
                for j in range(4):
                    pe.wait_ge(S("ln_sq"), 4 * n + j + 1)
                    for m in (2 * j, 2 * j + 1):
                        mm = pe.matmul(misc[1][:, 0:N], C("ones"), sq[:, m, 0:N], start=(m == 0), stop=(m == KT - 1))
                mm.then_inc(S("ln_var"), 1)

            panels(U["ba"], 1, L, True)
            panels(U["kqv"], 24, L)
            pe.wait_ge(S("con_in"), 16)
            pe.wait_ge(S("ba_copied"), 1)
            for t in range(NPAIR):
                mm = pe.transpose(misc[0][:, t * 64:t * 64 + 64], ba[0:64, PAIR_AT[t]:PAIR_AT[t] + P], C("ident", slice(0, 64), 64))
            mm.then_inc(S("ba_turned"), 1)
            panels(U["z"], 2, L)
            for i in range(4):
                if i < 3:
                    panels(U["z"] + 2 + i, 1, L)
                for j in range(4 * i, 4 * i + 4):
                    pe.wait_ge(S("kq_sq"), j + 1)
                    pe.matmul(misc[1][0:16, 0:LP], col_sum(j, 16), kq_slot(j % 6), start=(j == 0), stop=(j == 15)).then_inc(S("kq_sum"), 1)
            pe.wait_ge(S("g_ready"), 1)
            for t in range(NPAIR):
                pe.matmul(misc[3][:, t * 8:t * 8 + 8], C("half_tri"), tok[:, 1, t, :], start=True, stop=True)
                mm = pe.matmul(misc[3][:, 24 + t * 8:32 + t * 8], C("half_ones"), tok[:, 1, t, :], start=True, stop=True)
            mm.then_inc(S("g_col"), 1)
            panels(U["z"] + 5, 3, L)
            for j in range(16):
                pe.wait_ge(S("kq_row"), j + 1)
                if j >= 2:
                    pe.wait_ge(S("kq_normed"), j - 1)
                pe.matmul(misc[1 + j % 2][:, 0:LP], C("ones", slice(0, 16)), kq_slot(2 + j % 4)[0:16, :], start=True, stop=True).then_inc(S("kq_spread"), 1)
            pe.wait_ge(S("kq_normed"), 16)
            for t in range(NPAIR):
                pe.wait_ge(S("g_spread"), t + 1)
                if t:
                    pe.wait_ge(S("g_diff"), t)
                pe.matmul(misc[0][:, :], C("half_ones"), flat(r, 0, 2, 512), start=True, stop=True).then_inc(S("g_row"), 1)
                pe.wait_ge(S("beta_spread"), t + 1)
                if t:
                    pe.wait_ge(S("e_ready"), t)
                pe.matmul(misc[1][:, :], C("half_ones"), flat(r, 2, 4, 512), start=True, stop=True).then_inc(S("beta_row"), 1)
                if t:
                    pe.wait_ge(S("qk_ready"), t)
                for hd in range(HEADS_A):
                    for n, rows in enumerate(halves(t)):
                        cols = slice(PAIR_AT[t] + 64 * n, PAIR_AT[t] + 64 * n + 64)
                        pe.matmul(acc[0][rows, hd * CH:hd * CH + CH], kqv[:, hd, cols], kqv[:, hd, cols], start=True, stop=True)
                        mm = pe.matmul(acc[1][rows, hd * CH:hd * CH + CH], kqv[:, hd, cols], kqv[:, 8 + hd, cols], start=True, stop=True)
                mm.then_inc(S("kk_qk"), 1)
                if t:
                    pe.wait_ge(S("kT_ready"), t)
                    pe.wait_ge(S("v_beta"), t)
                cols = slice(PAIR_AT[t], PAIR_AT[t] + P)
                for hd in range(HEADS_A):
                    q = slice((hd % 4) * P, (hd % 4) * P + P)
                    pe.transpose(bank[2 + hd // 4][:, q], kqv[:, hd, cols], C("ident"))
                    mm = pe.transpose(bank[6 + hd // 4][:, q], kqv[:, 16 + hd, cols], C("ident"))
                mm.then_inc(S("kv_turned"), 1)
            for lv in range(6):
                for t in range(NPAIR):
                    st = lv * NPAIR + t
                    if lv == 0:
                        pe.wait_ge(S("e_ready"), t + 1)
                        if t == 0:
                            pe.wait_ge(S("qk_ready"), NPAIR)
                    else:
                        pe.wait_ge(S("xy_ready"), st - NPAIR + 1)
                    if st >= 2:
                        pe.wait_ge(S("t_ready"), st - 1)
                    for hd in range(HEADS_A):
                        for rows in halves(t):
                            o = acc[st % 2][rows, hd * CH:hd * CH + CH]
                            if lv == 0:
                                mm = pe.matmul(o, E[rows, t, hd, :], C("eye64", rows), start=True, stop=True)
                            else:
                                mm = pe.matmul(blocks(o, lv, 0), E[rows, t, hd, :], blocks(X[rows, t, hd, :], lv, 0), start=True, stop=True)
                    mm.then_inc(S("ax_done"), 1)
                for t in range(NPAIR if lv else 0):
                    st = lv * NPAIR + t
                    product = st - NPAIR
                    pe.wait_ge(S("t_ready"), st + 1)
                    if product >= 2:
                        pe.wait_ge(S("xy_ready"), st - 1)
                    elif product == 0:
                        pe.wait_ge(S("kT_ready"), NPAIR)
                        pe.wait_ge(S("v_beta"), NPAIR)
                    for hd in range(HEADS_A):
                        for rows in halves(t):
                            c = slice(hd * 32, hd * 32 + 32)
                            if lv < 5:
                                pe.matmul(misc[2 * (product % 2)][rows, c], Y[rows, t, hd, :], blocks(T[rows, t, hd, :], lv, 0), start=True, stop=True)
                            mm = pe.matmul(misc[2 * (product % 2) + 1][rows, c], T[rows, t, hd, :], blocks(Y[rows, t, hd, :], lv, 1), start=True, stop=True)
                    mm.then_inc(S("xt_done"), 1)
            for t in range(NPAIR):
                pe.wait_ge(S("xy_ready"), 5 * NPAIR + NPAIR)
                pe.wait_ge(S("kbg_ready"), t + 1)
                if t:
                    pe.wait_ge(S("u_ready"), t)
                    pe.wait_ge(S("w_ready"), 2 * t - 1)
                for hd in range(HEADS_A):
                    for rows in halves(t):
                        q = slice((hd % 4) * P, (hd % 4) * P + P)
                        mm = pe.matmul(acc[hd // 4][rows, q], Y[rows, t, hd, :], uv[rows, t, hd, :], start=True, stop=True)
                mm.then_inc(S("u_done"), 1)
                for n, rows in enumerate(halves(t)):
                    for hd in range(HEADS_A):
                        mm = pe.matmul(misc[n][:, hd * CH:hd * CH + CH], kbg[rows, hd, :], Y[rows, t, hd, :], start=True, stop=True)
                    mm.then_inc(S("w_done"), 1)
            for c in range(NCH):
                t, rows, cols = chunk_of(c)
                pe.wait_ge(S("g_spread2"), t + 1)
                if c >= 2:
                    pe.wait_ge(S("eg_exp"), c - 1)
                pe.matmul(misc[2 + c % 2][:, :], C("ones", rows), flat(r, 0, 4, D)[rows, (t % 2) * 512:(t % 2) * 512 + 512],
                          start=True, stop=True).then_inc(S("eg_row"), 1)
            pe.wait_ge(S("eg_exp"), NCH)
            for c in range(NCH):
                t, rows, cols = chunk_of(c)
                if c == 0:
                    pe.wait_ge(S("w_ready"), NCH)
                    pe.wait_ge(S("u_ready"), NPAIR)
                    pe.wait_ge(S("kd_ready"), 1)
                    pe.wait_ge(S("qg_ready"), NCH)
                else:
                    pe.wait_ge(S("state_ready"), c)
                    for hd in range(HEADS_A):
                        mm = pe.matmul(acc[hd // 4][rows, (hd % 4) * P:(hd % 4) * P + P], kqv[:, 16 + hd, cols], states[(c - 1) % 2][:, hd, :], start=True, stop=True)
                    mm.then_inc(S("ws_done"), 1)
                    pe.wait_ge(S("o_copied"), c)
                    for hd in range(HEADS_A):
                        pe.matmul(misc[0][:, hd * CH:hd * CH + CH], states[(c - 1) % 2][:, hd, :], kqv[:, 8 + hd, cols], start=(hd == 0), stop=False)
                    pe.wait_ge(S("v_new"), c)
                if c < NCH - 1:
                    for hd in range(HEADS_A):
                        mm = pe.matmul(acc[2 + hd // 4][:, (hd % 4) * P:(hd % 4) * P + P], kT[rows, t, hd, :], uv[rows, t, hd, :], start=True, stop=True)
                    mm.then_inc(S("kv_done"), 1)
                for hd in range(HEADS_A):
                    mm = pe.matmul(misc[0][:, hd * CH:hd * CH + CH], uv[rows, t, hd, :], QK[rows, t, hd, :], start=(c == 0), stop=(c == 0 or hd == HEADS_A - 1))
                mm.then_inc(S("o_done"), 1)
            for hd in range(HEADS_A):
                pe.wait_ge(S("o_sq"), hd + 1)
                mm = pe.matmul(misc[2][0:8, 0:N_MIX], col_sum(hd, 8), sq[:, hd, 0:N_MIX], start=(hd == 0), stop=(hd == HEADS_A - 1))
            mm.then_inc(S("o_sum"), 1)
            for hd in range(HEADS_A):
                pe.wait_ge(S("o_row"), hd + 1)
                if hd >= 2:
                    pe.wait_ge(S("o_gated"), hd - 1)
                pe.matmul(misc[2 + hd % 2][:, 0:N_MIX], C("ones", slice(0, 8)), kqv[0:8, 16 + hd, 0:N_MIX], start=True, stop=True).then_inc(S("o_spread"), 1)

            panels(U["a_out"], 8, N_MIX, True)
            layer_norm(0, U["a_out"], N_MIX, False)
            panels(U["up0"], 2 * FT, N_MIX, True)
            down(U["down0"], N_FFN0)
            layer_norm(1, U["down0"], N_FFN0, True)
            panels(U["b_in"], 24, N_FFN0, True)
            panels(U["b_out"], 8, N_B, True)
            layer_norm(2, U["b_out"], N_B, False)
            panels(U["up1"], 2 * FT, N_B, True)
            down(U["down1"], N_FFN1)
            layer_norm(3, U["down1"], SEQ, True)

            def tokens(u0, tiles, xh, xl, banks):
                n = tiles // 2
                for j in range(n):
                    s = u0 + j
                    slot = s % RING
                    pe.wait_ge(S("lo_ready"), s + 1)
                    for i in range(2):
                        for kk in range(2):
                            k = 2 * j + kk
                            wc = slice(kk * 512, kk * 512 + 512)
                            tk = slice(i * P, i * P + P)
                            o = banks[i][:, 0:512]
                            f, l = k == 0, k == tiles - 1
                            pe.matmul(o, xh[:, k, tk], w_hi[:, slot, wc], start=f, stop=False)
                            pe.matmul(o, xl[:, k, tk], w_hi[:, slot, wc], start=False, stop=False)
                            mm = pe.matmul(o, xh[:, k, tk], w_lo[:, slot, wc], start=False, stop=l)
                    mm.then_inc(S("unit_done"), 1)

            def four(u, xh, xl, banks):
                slot = u % RING
                pe.wait_ge(S("lo_ready"), u + 1)
                for m in range(4):
                    for k in range(2):
                        c = slice(k * 512 + m * P, k * 512 + m * P + P)
                        mm = three(banks[m][:, 0:SEQ], w_hi[:, slot, c], w_lo[:, slot, c], xh[:, k, 0:SEQ], xl[:, k, 0:SEQ], k == 0, k == 1)
                mm.then_inc(S("unit_done"), 1)

            panels(U["m_in"], 5, SEQ, True)
            for j in range(4):
                pe.wait_ge(S("c_sq"), j + 1)
                mm = pe.matmul(misc[j // 2][:, 0:SEQ], C("ones"), sq[:, j, 0:SEQ], start=(j % 2 == 0), stop=(j % 2 == 1))
                if j % 2:
                    mm.then_inc(S("c_sum"), 1)
            panels(U["m_sbqk"], 8, SEQ)
            pe.wait_ge(S("acc_used"), U["m_sbv"])
            tokens(U["m_sbv"], KT, x_hi, x_lo, acc)
            pe.wait_ge(S("c_ready"), 4)
            pe.wait_ge(S("acc_used"), U["m_uq"])
            four(U["m_uq"], c_hi, c_lo, acc)
            four(U["m_uq"] + 1, c_hi, c_lo, misc)
            pe.wait_ge(S("uq_read"), 1)
            four(U["m_ukn"], c_hi[:, 2:4, :], c_lo[:, 2:4, :], acc)
            pe.wait_ge(S("uq_read"), 2)
            tokens(U["m_ukv"], 2, c_hi[:, 2:4, :], c_lo[:, 2:4, :], misc)

            def scores_mla(hd):
                o = misc[hd % 2]
                kq = (k_m[0:96, hd, :], q_m[0:96, hd, :])
                pe.matmul(o[:, 0:128], kq[1][:, 0:P], kq[0][:, 0:P], start=True, stop=True)
                return pe.matmul(o[:, 128:384], kq[1][:, P:SEQ], kq[0][:, 0:SEQ], start=True, stop=True)

            def scores_fox(hd):
                o = misc[hd % 2]
                rows = slice(64 * (hd % 2), 64 * (hd % 2) + 64)
                k, q = k_f[rows, hd // 2, :], q_f[rows, hd // 2, :]
                sel = con_b[0:16, CB["sel"] + hd * P:CB["sel"] + hd * P + P]
                pe.matmul(o[:, 0:128], q[:, 0:P], k[:, 0:P], start=True, stop=False)
                pe.matmul(o[:, 0:128], sel, fl[0:16, 4, 0:P], start=False, stop=True)
                pe.matmul(o[:, 128:384], q[:, P:SEQ], k[:, 0:SEQ], start=True, stop=False)
                return pe.matmul(o[:, 128:384], sel, fl[0:16, 4, 0:SEQ], start=False, stop=True)

            def softmax_heads(n, base, scores, v):
                def score(hd):
                    if base + hd >= 2:
                        pe.wait_ge(S("sm_masked"), base + hd - 1)
                    scores(hd).then_inc(S("sm_scores"), 1)
                def turn(hd):
                    g = base + hd
                    pe.wait_ge(S("sm_probs"), g + 1)
                    if g >= 2:
                        pe.wait_ge(S("sm_turned_copied"), g - 1)
                    o = misc[2 + hd % 2]
                    for j in range(3):
                        mm = pe.transpose(o[:, j * P:j * P + P], prob[:, g % 2, j * P:j * P + P], C("ident"))
                    mm.then_inc(S("sm_turned"), 1)

                def times_v(hd):
                    g = base + hd
                    pe.wait_ge(S("sm_turned_copied"), g + 1)
                    rows = slice(64 * (hd % 2), 64 * (hd % 2) + 64)
                    ob = acc[(hd // 2) % 4]
                    if hd % 2 == 0 and hd >= 8:
                        pe.wait_ge(S("o_split"), o_base[0] + hd // 2 - 3)
                    pT = probT[:, g % 2, :]
                    pe.matmul(ob[rows, 0:128], v(0, hd), pT[:, 0:128], start=True, stop=True)
                    pe.matmul(ob[rows, 128:256], v(0, hd), pT[:, 128:256], start=True, stop=False)
                    pe.matmul(ob[rows, 128:256], v(1, hd), pT[:, 256:384], start=False, stop=True).then_inc(S("pv_done"), 1)

                score(0)
                score(1)
                for hd in range(n + 1):
                    if hd + 2 < n:
                        score(hd + 2)
                    if hd < n:
                        turn(hd)
                    if hd >= 1:
                        times_v(hd - 1)

            o_base = [0]
            pe.wait_ge(S("acc_used"), U["m_out"])
            pe.wait_ge(S("con_b_in"), 16)
            pe.wait_ge(S("m_ready"), 1)
            softmax_heads(8, 0, scores_mla, lambda i, hd: v_m[:, i, hd * 64:hd * 64 + 64])
            o_base[0] = 4

            def sb_ops(hd):
                rows = slice(64 * (hd % 2), 64 * (hd % 2) + 64)
                return k_s[rows, hd // 2, :], q_s[rows, hd // 2, :]

            def sb_z(hd):
                k, q = sb_ops(hd)
                if hd >= 2:
                    pe.wait_ge(S("sb_rem"), hd - 1)
                else:
                    pe.wait_ge(S("sm_masked"), 8)
                o = misc[hd % 2]
                pe.matmul(o[:, 0:256], k[:, 0:P], q[:, 0:SEQ], start=True, stop=True)
                pe.matmul(o[:, 256:384], k[:, P:SEQ], q[:, P:SEQ], start=True, stop=True).then_inc(S("sb_logits"), 1)

            def sb_sums(hd):
                k, q = sb_ops(hd)
                rem = prob[:, hd % 2, :]
                pe.wait_ge(S("sb_rem"), hd + 1)
                if hd >= 2:
                    pe.wait_ge(S("sb_min"), hd - 1)
                else:
                    pe.wait_ge(S("sm_turned_copied"), 8)
                o = misc[2 + hd % 2]
                pe.matmul(o[:, 0:256], k[:, 0:P], q[:, 0:SEQ], start=True, stop=False)
                pe.matmul(o[:, 0:256], CBv("neg_tri"), rem[:, 0:256], start=False, stop=False)
                pe.matmul(o[:, 128:256], CBv("neg_ones"), rem[:, 256:384], start=False, stop=True)
                pe.matmul(o[:, 256:384], k[:, P:SEQ], q[:, P:SEQ], start=True, stop=False)
                pe.matmul(o[:, 256:384], CBv("neg_tri"), rem[:, 256:384], start=False, stop=True).then_inc(S("sb_sum"), 1)

            sb_z(0)
            sb_z(1)
            for pair in range(4):
                heads = (2 * pair, 2 * pair + 1)
                for hd in heads:
                    sb_sums(hd)
                    if hd + 2 < 8:
                        sb_z(hd + 2)
                for hd in heads:
                    pe.wait_ge(S("sb_att"), hd + 1)
                    rows = slice(64 * (hd % 2), 64 * (hd % 2) + 64)
                    ob = acc[pair]
                    if hd % 2 == 0:
                        pe.wait_ge(S("o_split"), pair + 1)
                    weights = probT[:, hd % 2, :]
                    pe.matmul(ob[rows, 0:256], v_s[:, 0, hd * 64:hd * 64 + 64], weights[:, 0:256], start=True, stop=False)
                    pe.matmul(ob[rows, 128:256], v_s[:, 1, hd * 64:hd * 64 + 64], weights[:, 256:384], start=False, stop=True).then_inc(S("pv_done"), 1)
            panels(U["m_out"], 8, SEQ, True)
            layer_norm(4, U["m_out"], SEQ, False)

            def ffn_and_ple(i, n, up, dn, proj, gate):
                panels(up, 2 * FT, SEQ, True)
                down(dn, SEQ)

                def project(j):
                    if j == 0:
                        pe.wait_ge(S("p_split"), 1)
                        pe.wait_ge(S("acc_used"), proj)
                    four(proj + j, p_hi[:, i], p_lo[:, i], proj_out(gate, j))

                layer_norm(n, dn, SEQ, True, lambda: project(0))
                project(1)
                panels(gate, 8, SEQ, True)

            ffn_and_ple(0, 5, U["up2"], U["down2"], U["proj0"], U["gate0"])

            panels(U["f_f"], 1, SEQ, True)
            panels(U["f_qk"], 16, SEQ)
            for g in range(2):
                pe.wait_ge(S("acc_used"), U["f_v"] + 4 * g)
                tokens(U["f_v"] + 4 * g, KT, x_hi, x_lo, acc)
            pe.wait_ge(S("dcum"), 1)
            for i in range(2):
                mm = pe.transpose(misc[0][:, i * 16:i * 16 + 16], fl[0:16, 3, i * P:i * P + P], C("ident", slice(0, 16), 16))
            mm.then_inc(S("dcum_turned"), 1)
            pe.wait_ge(S("dcum_copied"), 1)
            pe.wait_ge(S("acc_used"), U["f_out"])
            o_base[0] = 8
            softmax_heads(16, 8, scores_fox, lambda i, hd: v_f[:, i, hd // 8, (hd % 8) * 64:(hd % 8) * 64 + 64])
            panels(U["f_out"], 8, SEQ, True)
            layer_norm(6, U["f_out"], SEQ, False)
            ffn_and_ple(1, 7, U["up3"], U["down3"], U["proj1"], U["gate1"])

        @block.scalar
        def _(act):
            A = nc.scalar.activation

            def split(u, s):
                if isinstance(s, int) and s >= NU:
                    return
                slot = s % RING
                act.wait_ge(S(f"raw{slot}"), (u - slot) * 4 + 16 if not isinstance(u, int) else 16 * (u // RING + 1))
                if s >= RING:
                    act.wait_ge(S("unit_done"), u - (RING - 1))
                A(w_hi[:, slot, :], raw[:, slot, :], ACT.Copy).then_inc(S("hi_ready"), 1)

            def ahead(u, s):
                split(u + RING, s + RING)

            x_sets = [0]

            def layer_norm(n, N):
                A(warm[:, n:n + 1], eps[:, 0:1], ACT.Sqrt)
                for j in range(4):
                    act.wait_ge(S("ln_centred"), 4 * n + j + 1)
                    A(sq[:, 2 * j:2 * j + 2, 0:N], r[:, 2 * j:2 * j + 2, 0:N], ACT.Square).then_inc(S("ln_sq"), 1)
                act.wait_ge(S("ln_var"), n + 1)
                A(std[:, 0, 0:N], misc[1][:, 0:N], ACT.Sqrt, bias=eps[:, 0:1], scale=1.0 / D).then_inc(S("ln_std"), 1)
                for k in range(KT):
                    act.wait_ge(S("ln_scaled"), KT * n + k + 1)
                    A(x_hi[:, k, 0:N], r[:, k, 0:N], ACT.Identity, bias=par_col(f"ln_b{n}", k)).then_inc(S("x_hi"), 1)
                x_hi_n[0] += KT

            x_hi_n = [0]

            act.dma_start(prm[:, :], par).then_inc(S("prm_in"), 16)
            act.dma_start(con[:, :], ca).then_inc(S("con_in"), 16)
            act.wait_ge(S("eps_set"), 1)
            split(0, 0)
            for k in range(4):
                act.wait_ge(S(f"h0_in{k // 2}"), 16)
                A(x_hi[:, 2 * k:2 * k + 2, :], h[:, 2 * k:2 * k + 2, :], ACT.Copy).then_inc(S("x_hi"), 1)
            x_hi_n[0] += 4
            for u in range(1, RING):
                split(u, u)
            act.wait_ge(S("prm_in"), 16)
            act.wait_ge(S("zeroed"), 1)
            act.wait_ge(S("unit_done"), 1)
            A(ba[:, PAD:LP], acc[U["ba"] % RING][:, 0:L], ACT.Copy).then_inc(S("ba_copied"), 1)
            ahead(U["ba"], U["ba"])

            def kqv_unit(u, s, j):
                c = conv_a[:, (s - U["kqv"]) % 2, :]
                act.wait_ge(S("unit_done"), u + 1)
                A(c, acc[s % RING][:, 0:L], ACT.Copy, scale=par_col("a_conv", j * 4 + 3)).then_inc(S("tap0"), 1)
                ahead(u, s)
                act.wait_ge(S("taps_done"), j + 1)
                A(at(kqv, j, slice(PAD, LP)), c, ACT.Silu).then_inc(S("kqv_silu"), 1)

            units(act, U["kqv"], 24, kqv_unit)

            def z_unit(u, s, j):
                act.wait_ge(S("unit_done"), u + 1)
                A(at(z_gate, j), acc[s % RING][:, OFF_MIX:L], ACT.Silu).then_inc(S("acc_used"), 1)
                ahead(u, s)

            act.wait_ge(S("acc_used"), U["z"])
            tk = lambda i: tok[:, i, :, :]
            turned = misc[0][:, 0:192].rearrange("p (t c) -> p t c", t=3)
            act.wait_ge(S("kqv_silu"), 24)
            for i in range(4):
                for j in range(4 * i, 4 * i + 4):
                    if j >= 6:
                        act.wait_ge(S("kq_sum"), j - 5)
                    A(kq_slot(j % 6), kqv[:, j, :], ACT.Square).then_inc(S("kq_sq"), 1)
                z_unit(U["z"] + i, U["z"] + i, i)
                if i == 1:
                    act.wait_ge(S("ba_turned"), 1)
                    A(tk(2), turned[:, :, 0:8], ACT.Exp, scale=-1.0).then_inc(S("tok_act"), 1)
                    act.wait_ge(S("tok_dve"), 1)
                    A(tk(4), tk(3), ACT.Abs).then_inc(S("tok_act"), 1)
                    act.wait_ge(S("tok_act"), 2)
                    A(tk(5), tk(4), ACT.Exp, scale=-1.0).then_inc(S("tok_act"), 1)
                    act.wait_ge(S("tok_act"), 3)
                    A(tk(6), tk(5), ACT.Ln, bias=1.0).then_inc(S("tok_act"), 1)
                    A(tok[:, 7, 0, :], prm[:, PC["a_log"]:PC["a_log"] + 8], ACT.Exp).then_inc(S("tok_act"), 1)
            act.wait_ge(S("kq_sum"), 16)
            A(std[0:16, 0, :], misc[1][0:16, 0:LP], ACT.Sqrt, bias=eps[0:16, 1:2]).then_inc(S("kq_std"), 1)
            act.wait_ge(S("tok_dve"), 3)
            A(tok[:, 9, :, :], tok[:, 8, :, :], ACT.Exp).then_inc(S("tok_act"), 1)
            A(tok[:, 11, :, :], tok[:, 10, :, :], ACT.Exp).then_inc(S("tok_act"), 1)
            for i in range(4, 8):
                z_unit(U["z"] + i, U["z"] + i, i)
            act.wait_ge(S("kq_rstd"), 1)
            for j in range(16):
                if j >= 4:
                    act.wait_ge(S("kq_spread"), j - 3)
                A(kq_slot(2 + j % 4)[0:16, :], rstd[0:16, 0, :], ACT.Copy, scale=con[0:16, CA["ident"] + j:CA["ident"] + j + 1]).then_inc(S("kq_row"), 1)
            for t in range(NPAIR):
                act.wait_ge(S("g_diff2"), t + 1)
                A(T[:, t], T[:, t], ACT.Exp).then_inc(S("decay"), 1)
                act.wait_ge(S("kv_turned"), t + 1)
                for g in range(2):
                    a = A(kT[:, t, 4 * g:4 * g + 4, :], bank[2 + g][:, :].rearrange("p (a n) -> p a n", a=4), ACT.Copy)
                a.then_inc(S("kT_ready"), 1)
            for t in range(NPAIR):
                for n, rows in enumerate(halves(t)):
                    c = 0 if t == 0 else 2 * t - 1 + n
                    act.wait_ge(S("w_done"), c + 1)
                    A(kqv[:, 16:24, CH * c:CH * c + CH], misc[n][:, :].rearrange("p (a n) -> p a n", a=8), ACT.Copy).then_inc(S("w_ready"), 1)
            for c in range(NCH):
                act.wait_ge(S("eg_row"), c + 1)
                if c >= 2:
                    act.wait_ge(S("qg_ready"), c - 1)
                A(eg_buf[:, c % 2, :], misc[2 + c % 2][:, :], ACT.Exp).then_inc(S("eg_exp"), 1)
            for c in range(NCH):
                t, rows, cols = chunk_of(c)
                act.wait_ge(S("o_done"), c + 1)
                A(kqv[:, 0:8, cols], misc[0][:, :].rearrange("p (a n) -> p a n", a=8), ACT.Copy).then_inc(S("o_copied"), 1)
            act.wait_ge(S("o_copied"), NCH)
            for hd in range(HEADS_A):
                A(sq[:, hd, 0:N_MIX], kqv[:, hd, LP - N_MIX:LP], ACT.Square).then_inc(S("o_sq"), 1)
            act.wait_ge(S("o_sum"), 1)
            A(std[0:8, 0, 0:N_MIX], misc[2][0:8, 0:N_MIX], ACT.Sqrt, bias=eps[0:8, 1:2], scale=1.0 / P).then_inc(S("o_std"), 1)
            act.wait_ge(S("o_rstd"), 1)
            for hd in range(HEADS_A):
                A(kqv[0:8, 16 + hd, 0:N_MIX], rstd[0:8, 0, 0:N_MIX], ACT.Copy, scale=con[0:8, CA["ident"] + hd:CA["ident"] + hd + 1]).then_inc(S("o_row"), 1)
            for hd in range(HEADS_A):
                act.wait_ge(S("o_gated"), hd + 1)
                A(x_hi[:, hd, 0:N_MIX], r[:, hd, 0:N_MIX], ACT.Copy).then_inc(S("x_hi"), 1)
            x_hi_n[0] += KT
            act.wait_ge(S("x_ready"), 2 * KT)
            act.dma_start(con_b[:, :], cb).then_inc(S("con_b_in"), 16)
            act.dma_start(p_raw[:, :, :, :], pin).then_inc(S("p_in"), 16)

            def out_phase(u0, n):
                units(act, u0, n, lambda u, s, j: (act.wait_ge(S("unit_done"), u + 1), ahead(u, s)))

            def down_phase(u0):
                for j in range(2):
                    act.wait_ge(S("unit_done"), u0 + j + 1)
                    ahead(u0 + j, u0 + j)
                with act.Fori(0, (FT - 6) // RING) as i:
                    for b in range(RING):
                        act.wait_ge(S("unit_done"), i * RING + (u0 + 3 + b))
                        ahead(i * RING + (u0 + 2 + b), u0 + 2 + b)
                for j in range(FT - 4, FT):
                    act.wait_ge(S("unit_done"), u0 + j + 1)
                    ahead(u0 + j, u0 + j)

            ups = [0]

            def up_phase(u0, N, conv):
                base = ups[0] * FT
                cbase = sum(up_conv[:ups[0]]) * FT

                def pair(u, s, j):
                    g = s % RING
                    par = (s - u0) // 2 % 2
                    jb = j + base
                    act.wait_ge(S("unit_done"), u + 2)
                    if conv is not None:
                        A(cv[:, par, 0:N - 2], acc[g][:, 0:N - 2], ACT.Copy, scale=par_col(conv, j * 3)).then_inc(S("ffn_tap0"), 1)
                        ahead(u, s)
                        act.wait_ge(S("ffn_taps"), j + (cbase + 1))
                        A(sl[:, par, 0:N - 2], cv[:, par, 0:N - 2], ACT.Silu).then_inc(S("ffn_silu"), 1)
                        M = N - 2
                    else:
                        A(sl[:, par, 0:N], acc[g][:, 0:N], ACT.Silu).then_inc(S("ffn_silu"), 1)
                        ahead(u, s)
                        M = N
                    ahead(u + 1, s + 1)
                    act.wait_ge(S("ffn_product"), jb + 1)
                    A(at(a_hi, j, slice(0, M)), av[:, par, 0:M], ACT.Copy).then_inc(S("a_hi"), 1)

                with act.Fori(0, FT // 2) as i:
                    for b in range(2):
                        pair(i * RING + (u0 + 2 * b), u0 + 2 * b, i * 2 + b)
                ups[0] += 1

            out_phase(U["a_out"], 8)
            layer_norm(0, N_MIX)
            up_phase(U["up0"], N_MIX, "f_conv0")
            down_phase(U["down0"])
            layer_norm(1, N_FFN0)

            def b_tile(u, s, j):
                act.wait_ge(S("unit_done"), u + 1)
                act.wait_ge(S("b_cx"), j)
                A(av[:, 0, 0:N_FFN0], acc[s % RING][:, 0:N_FFN0], ACT.Copy).then_inc(S("b_c"), 1)
                ahead(u, s)
                act.wait_ge(S("unit_done"), u + 2)
                ahead(u + 1, s + 1)
                act.wait_ge(S("unit_done"), u + 3)
                ahead(u + 2, s + 2)

            with act.Fori(0, 2) as i:
                for q in range(4):
                    b_tile(i * 12 + (U["b_in"] + 3 * q), U["b_in"] + 3 * q, i * 4 + q)
            act.wait_ge(S("b_done"), 8)
            for k in range(4):
                A(x_hi[:, 2 * k:2 * k + 2, 0:N_B], r[:, 2 * k:2 * k + 2, 0:N_B], ACT.Copy).then_inc(S("x_hi"), 1)
            x_hi_n[0] += 4
            out_phase(U["b_out"], 8)
            layer_norm(2, N_B)
            up_phase(U["up1"], N_B, "f_conv1")
            down_phase(U["down1"])
            layer_norm(3, SEQ)

            act.wait_ge(S("p_in"), 16)
            A(p_hi[:, :, :, :], p_raw[:, :, :, :], ACT.Copy).then_inc(S("p_hi"), 1)
            for j in range(5):
                u = U["m_in"] + j
                act.wait_ge(S("unit_done"), u + 1)
                if j < 4:
                    A(sq[:, j, 0:SEQ], acc[u % RING][:, 0:SEQ], ACT.Square).then_inc(S("c_sq"), 1)
                ahead(u, u)
            for j in range(2):
                act.wait_ge(S("c_sum"), j + 1)
                A(std[:, j, 0:SEQ], misc[j][:, 0:SEQ], ACT.Sqrt, bias=eps[:, 1:2], scale=1.0 / 256).then_inc(S("c_std"), 1)
            for j in range(4):
                act.wait_ge(S("c_normed"), j + 1)
                A(c_hi[:, j, :], r[:, 4 + j, 0:SEQ], ACT.Copy).then_inc(S("c_hi"), 1)
            act.wait_ge(S("acc_used"), U["m_sbqk"])
            for j in range(8):
                u = U["m_sbqk"] + j
                act.wait_ge(S("unit_done"), u + 1)
                dst = (q_s if j < 4 else k_s)[:, j % 4, :]
                A(dst, acc[u % RING][:, 0:SEQ], ACT.Copy, scale=0.125 if j < 4 else 1.0).then_inc(S("acc_used"), 1)
                ahead(u, u)
            for j in range(4):
                u = U["m_sbv"] + j
                act.wait_ge(S("unit_done"), u + 1)
                ahead(u, u)
            A(v_s[:, 0, :], acc[0][:, :], ACT.Copy).then_inc(S("acc_used"), 2)
            A(v_s[:, 1, :], acc[1][:, :], ACT.Copy).then_inc(S("acc_used"), 2)
            for j in range(2):
                u = U["m_uq"] + j
                act.wait_ge(S("unit_done"), u + 1)
                for m in range(4):
                    A(q_m[0:64, 4 * j + m, :], (acc, misc)[j][m][0:64, 0:SEQ], ACT.Copy).then_inc(S("q_nope"), 1)
                ahead(u, u)
            u = U["m_ukn"]
            act.wait_ge(S("unit_done"), u + 1)
            for m in range(4):
                A(k_m[0:64, 2 * m, :], acc[m][0:64, 0:SEQ], ACT.Copy)
                a = A(k_m[0:64, 2 * m + 1, :], acc[m][64:128, 0:SEQ], ACT.Copy)
            a.then_inc(S("acc_used"), 1)
            ahead(u, u)
            u = U["m_ukv"]
            act.wait_ge(S("unit_done"), u + 1)
            A(v_m[:, 0, :], misc[0][:, :], ACT.Copy)
            A(v_m[:, 1, :], misc[1][:, :], ACT.Copy).then_inc(S("acc_used"), 1)
            ahead(u, u)

            def softmax_heads(n, base, ob):
                for hd in range(n):
                    g = base + hd
                    act.wait_ge(S("sm_max"), g + 1)
                    if g >= 2:
                        act.wait_ge(S("sm_turned"), g - 1)
                    pb = g % 2
                    A(prob[:, pb, 0:128], smx[:, pb, 0:128], ACT.Exp, bias=stat[:, pb, 0, 0:1], accum_out=stat[:, pb, 1, 0:1])
                    A(prob[:, pb, 128:384], smx[:, pb, 128:384], ACT.Exp, bias=stat[:, pb, 0, 1:2],
                      accum_out=stat[:, pb, 1, 1:2]).then_inc(S("sm_exp"), 1)
                    if hd >= 1:
                        after(g - 1, hd - 1, ob)
                after(base + n - 1, n - 1, ob)
                o_high(n // 2 - 1, ob, pv(base + n))

            def after(g, hd, ob):
                act.wait_ge(S("sm_turned"), g + 1)
                if g >= 2:
                    act.wait_ge(S("pv_done"), pv(g - 1))
                A(probT[:, g % 2, :], misc[2 + hd % 2][:, 0:384], ACT.Copy).then_inc(S("sm_turned_copied"), 1)
                if hd % 2 and hd >= 3:
                    o_high(hd // 2 - 1, ob, pv(g - 1))

            def pv(g):
                return g if g <= 8 else g + 8

            def o_high(m, ob, pvs):
                act.wait_ge(S("pv_done"), pvs)
                A(x_hi[:, ob + m, 0:SEQ], acc[m % 4][:, 0:SEQ], ACT.Copy).then_inc(S("x_hi"), 1)

            softmax_heads(8, 0, 0)
            def sb_exp(hd):
                pb = hd % 2
                act.wait_ge(S("sb_logits"), hd + 1)
                A(smx[:, pb, :], misc[pb][:, 0:384], ACT.Abs).then_inc(S("sb_abs"), 1)
                act.wait_ge(S("sb_abs"), hd + 1)
                A(smx[:, pb, :], smx[:, pb, :], ACT.Exp, scale=-1.0).then_inc(S("sb_exp"), 1)

            def sb_ln(hd):
                act.wait_ge(S("sb_exp"), hd + 1)
                A(smx[:, hd % 2, :], smx[:, hd % 2, :], ACT.Ln, bias=1.0).then_inc(S("sb_ln"), 1)

            def sb_att(hd):
                act.wait_ge(S("sb_min"), hd + 1)
                if hd >= 2:
                    act.wait_ge(S("pv_done"), 8 + hd - 1)
                A(probT[:, hd % 2, :], sb_log[:, hd % 2, :], ACT.Exp).then_inc(S("sb_att"), 1)

            sb_exp(0)
            sb_exp(1)
            for pair in range(4):
                heads = (2 * pair, 2 * pair + 1)
                for hd in heads:
                    sb_ln(hd)
                if pair:
                    o_high(pair - 1, 4, 8 + 2 * pair)
                if pair < 3:
                    for hd in heads:
                        sb_exp(hd + 2)
                for hd in heads:
                    sb_att(hd)
            o_high(3, 4, 16)
            x_hi_n[0] += 8
            out_phase(U["m_out"], 8)
            layer_norm(4, SEQ)

            def ffn_and_ple(i, n, up, dn, proj, gate):
                up_phase(up, SEQ, None)
                down_phase(dn)
                layer_norm(n, SEQ)
                for j in range(2):
                    u = proj + j
                    act.wait_ge(S("unit_done"), u + 1)
                    if i == 1 and j == 0:
                        act.wait_ge(S("ple_h"), KT)
                    for m in range(4):
                        a = A(pp[:, 4 * j + m, :], proj_out(gate, j)[m], ACT.Copy)
                    a.then_inc(S("acc_used"), 1)
                    ahead(u, u)
                for m in range(KT):
                    u = gate + m
                    act.wait_ge(S("unit_done"), u + 1)
                    if m >= 2:
                        act.wait_ge(S("ple_h"), KT * i + m - 1)
                    A(sl[:, m % 2, 0:SEQ], acc[u % RING][:, 0:SEQ], ACT.Sigmoid, bias=par_col(f"ple_b{i}", m)).then_inc(S("acc_used"), 1)
                    ahead(u, u)

            ffn_and_ple(0, 5, U["up2"], U["down2"], U["proj0"], U["gate0"])
            act.wait_ge(S("ple_h"), KT)
            act.wait_ge(S("unit_done"), U["gate0"] + 8)
            for k in range(4):
                A(x_hi[:, 2 * k:2 * k + 2, 0:SEQ], h[:, 2 * k:2 * k + 2, 0:SEQ], ACT.Copy).then_inc(S("x_hi"), 1)
            x_hi_n[0] += 4

            u = U["f_f"]
            act.wait_ge(S("unit_done"), u + 1)
            A(fl[0:16, 0, :], acc[u % RING][0:16, 0:SEQ], ACT.Identity, bias=prm[0:16, PC["b_f"]:PC["b_f"] + 1]).then_inc(S("acc_used"), 1)
            ahead(u, u)
            for j in range(16):
                u = U["f_qk"] + j
                act.wait_ge(S("unit_done"), u + 1)
                dst = (q_f if j < 8 else k_f)[:, j % 8, :]
                A(dst, acc[u % RING][:, 0:SEQ], ACT.Copy, scale=0.125 if j < 8 else 1.0).then_inc(S("acc_used"), 1)
                ahead(u, u)
            act.wait_ge(S("acc_used"), U["f_f"] + 1)
            A(fl[0:16, 1, :], fl[0:16, 0, :], ACT.Abs).then_inc(S("f_act"), 1)
            act.wait_ge(S("f_act"), 1)
            A(fl[0:16, 1, :], fl[0:16, 1, :], ACT.Exp, scale=-1.0).then_inc(S("f_act"), 1)
            act.wait_ge(S("f_act"), 2)
            A(fl[0:16, 1, :], fl[0:16, 1, :], ACT.Ln, bias=1.0).then_inc(S("f_act"), 1)
            for g in range(2):
                for j in range(4):
                    u = U["f_v"] + 4 * g + j
                    act.wait_ge(S("unit_done"), u + 1)
                    ahead(u, u)
                A(v_f[:, 0, g, :], acc[0][:, :], ACT.Copy).then_inc(S("acc_used"), 2)
                A(v_f[:, 1, g, :], acc[1][:, :], ACT.Copy).then_inc(S("acc_used"), 2)
            act.wait_ge(S("dcum_turned"), 1)
            A(dcum_col[:, :, :], misc[0][:, 0:32].rearrange("p (a n) -> p a n", a=2), ACT.Copy).then_inc(S("dcum_copied"), 1)
            softmax_heads(16, 8, 0)
            x_hi_n[0] += 8
            out_phase(U["f_out"], 8)
            layer_norm(6, SEQ)
            ffn_and_ple(1, 7, U["up3"], U["down3"], U["proj1"], U["gate1"])

        @block.vector
        def _(dve):
            V = nc.vector
            x_hi_n = [0]
            x_sets = [0]

            def split(u, s):
                if s >= NU:
                    return
                slot = s % RING
                dve.wait_ge(S("hi_ready"), u + 1)
                V.tensor_tensor(w_lo[:, slot, :], raw[:, slot, :], w_hi[:, slot, :].bitcast(F32), ALU.subtract).then_inc(S("lo_ready"), 1)

            def ahead(u, s):
                split(u + RING, s + RING)

            def x_low(src, N, step):
                for k in range(0, KT, step):
                    x_hi_n[0] += 1
                    dve.wait_ge(S("x_hi"), x_hi_n[0] + 0)
                    a = V.tensor_tensor(x_lo[:, k:k + step, 0:N], src[:, k:k + step, 0:N], x_hi[:, k:k + step, 0:N].bitcast(F32), ALU.subtract)
                    a.then_inc(S("x_ready"), step)

            def layer_norm(n, N):
                dve.wait_ge(S("ln_sum"), n + 1)
                mean = misc[0][:, 0:N].unsqueeze(1).to_broadcast([P, 2, N])
                for j in range(4):
                    t = r[:, 2 * j:2 * j + 2, 0:N]
                    V.scalar_tensor_tensor(out=t, in0=mean, scalar=-1.0 / D, in1=t, op0=ALU.mult, op1=ALU.add).then_inc(S("ln_centred"), 1)
                dve.wait_ge(S("ln_std"), n + 1)
                V.reciprocal(rstd[:, 0, 0:N], std[:, 0, 0:N]).then_inc(S("ln_rstd"), 1)
                dve.wait_ge(S("ln_rstd"), n + 1)
                for k in range(KT + 1):
                    if k < KT:
                        dve.wait_ge(S("ln_sq"), 4 * n + k // 2 + 1)
                        V.scalar_tensor_tensor(out=r[:, k, 0:N], in0=r[:, k, 0:N], scalar=par_col(f"ln_g{n}", k), in1=rstd[:, 0, 0:N], op0=ALU.mult, op1=ALU.mult).then_inc(S("ln_scaled"), 1)
                    if k >= 1:
                        m = k - 1
                        x_hi_n[0] += 1
                        dve.wait_ge(S("x_hi"), x_hi_n[0])
                        V.scalar_tensor_tensor(out=x_lo[:, m, 0:N], in0=r[:, m, 0:N], scalar=par_col(f"ln_b{n}", m), in1=x_hi[:, m, 0:N].bitcast(F32), op0=ALU.add, op1=ALU.subtract).then_inc(S("x_ready"), 1)
                dve.wait_ge(S("ln_h"), KT * (n + 1))

            V.memset(eps[:, 0:1], 1e-5)
            V.memset(eps[:, 1:2], 1e-6).then_inc(S("eps_set"), 1)
            V.memset(ba[:, 0:PAD], 0.0)
            V.memset(kqv[:, :, 0:PAD], 0.0).then_inc(S("zeroed"), 1)
            split(0, 0)
            x_low(h, L, 2)
            for u in range(1, RING):
                split(u, u)
            dve.wait_ge(S("prm_in"), 16)
            dve.wait_ge(S("con_in"), 16)
            dve.wait_ge(S("ba_copied"), 1)
            dve.sem_inc(S("acc_used"), 1)
            ahead(U["ba"], U["ba"])

            def kqv_unit(u, s, j):
                a, c = acc[s % RING], conv_a[:, (s - U["kqv"]) % 2, :]
                dve.wait_ge(S("tap0"), j + 1)
                for n in range(1, 4):
                    if n > 1:
                        dve.wait_ge(S("taps"), j * 2 + (n - 1))
                    v = V.scalar_tensor_tensor(out=c[:, n:L], in0=a[:, 0:L - n], scalar=par_col("a_conv", j * 4 + (3 - n)), in1=c[:, n:L], op0=ALU.mult, op1=ALU.add)
                    v.then_inc(S("taps" if n < 3 else "taps_done"), 1)
                dve.wait_ge(S("taps_done"), j + 1)
                dve.sem_inc(S("acc_used"), 1)
                ahead(u, s)

            units(dve, U["kqv"], 24, kqv_unit)
            units(dve, U["z"], 2, lambda u, s, j: ahead(u, s))
            tk = lambda i: tok[:, i, :, :]
            turned = misc[0][:, 0:192].rearrange("p (t c) -> p t c", t=3)
            chain = [0]

            def link(ins):
                chain[0] += 1
                ins.then_inc(S("gate_chain"), 1)
                dve.wait_ge(S("gate_chain"), chain[0])

            dtb = prm[:, PC["dt_bias"]:PC["dt_bias"] + 8].unsqueeze(1).to_broadcast([P, 3, 8])
            dve.wait_ge(S("tok_act"), 1)
            V.tensor_tensor(tk(3), turned[:, :, 32:40], dtb, ALU.add).then_inc(S("tok_dve"), 1)
            link(V.tensor_scalar(tk(2), tk(2), 1.0, None, ALU.add))
            link(V.reciprocal(tk(0), tk(2)))
            link(V.tensor_scalar(tok[:, 0, 0, :], tok[:, 0, 0, :], C("live0"), None, ALU.mult))
            dve.wait_ge(S("tok_act"), 5)
            dve.wait_ge(S("tok_dve"), 1)
            link(V.scalar_tensor_tensor(out=tk(1), in0=tk(3), scalar=0.0, in1=tk(6), op0=ALU.max, op1=ALU.add))
            link(V.scalar_tensor_tensor(out=tk(1), in0=tk(1), scalar=-1.0, in1=tok[:, 7, 0, :].unsqueeze(1).to_broadcast([P, 3, 8]), op0=ALU.mult, op1=ALU.mult))
            V.tensor_scalar(tok[:, 1, 0, :], tok[:, 1, 0, :], C("live0"), None, ALU.mult).then_inc(S("g_ready"), 1)
            dve.wait_ge(S("g_ready"), 1)
            units(dve, U["z"] + 2, 2, lambda u, s, j: ahead(u, s))
            dve.wait_ge(S("kq_std"), 1)
            V.reciprocal(rstd[0:16, 0, :], std[0:16, 0, :]).then_inc(S("kq_rstd"), 1)
            dve.wait_ge(S("g_col"), 1)
            gc = misc[3][:, 0:24].rearrange("p (t c) -> p t c", t=3)
            gl = misc[3][:, 24:48].rearrange("p (t c) -> p t c", t=3)
            link(V.tensor_copy(tk(8), gc))
            V.tensor_copy(tk(13), gl).then_inc(S("tok_dve"), 1)
            dve.wait_ge(S("tok_dve"), 2)
            V.tensor_tensor(tk(10), tk(13), tk(8), ALU.subtract).then_inc(S("tok_dve"), 1)
            dve.wait_ge(S("tok_dve"), 3)
            dve.wait_ge(S("tok_act"), 7)
            link(V.tensor_tensor(tk(12), tk(0), tk(9), ALU.mult))
            units(dve, U["z"] + 4, 4, lambda u, s, j: ahead(u, s))
            spread = flat(r, 0, 2, 512).rearrange("p (a n) -> p a n", a=8)
            spread_b = flat(r, 2, 4, 512).rearrange("p (a n) -> p a n", a=8)

            def over_chunk(x):
                return x.unsqueeze(2).to_broadcast([P, HEADS_A, CH])

            def over_heads(x):
                return x.unsqueeze(1).to_broadcast([P, HEADS_A, CH])

            def spreads(t):
                if t:
                    dve.wait_ge(S("g_row"), t)
                V.tensor_tensor(spread, over_chunk(tok[:, 1, t, :]), over_heads(C("tri64")), ALU.mult).then_inc(S("g_spread"), 1)
                if t:
                    dve.wait_ge(S("beta_row"), t)
                V.tensor_tensor(spread_b, over_chunk(tok[:, 0, t, :]), over_heads(C("eye64")), ALU.mult).then_inc(S("beta_spread"), 1)

            dve.wait_ge(S("kqv_silu"), 24)
            spreads(0)
            for j in range(16):
                dve.wait_ge(S("kq_spread"), j + 1)
                V.scalar_tensor_tensor(out=kqv[:, j, :], in0=kqv[:, j, :], scalar=1.0 if j < 8 else float(P) ** -0.5, in1=misc[1 + j % 2][:, 0:LP], op0=ALU.mult, op1=ALU.mult).then_inc(S("kq_normed"), 1)
            bk = lambda a, rows=slice(0, P): a[rows, :].rearrange("p (a n) -> p a n", a=8)
            for t in range(NPAIR):
                pr = rows_of(t)
                dve.wait_ge(S("g_row"), t + 1)
                V.tensor_tensor(T[:, t], bk(misc[0]), over_chunk(tok[:, 8, t, :]), ALU.subtract).then_inc(S("g_diff"), 1)
                dve.wait_ge(S("g_diff"), t + 1)
                V.tensor_scalar(T[:, t], T[:, t], 0.0, None, ALU.min).then_inc(S("g_diff2"), 1)
                dve.wait_ge(S("decay"), t + 1)
                link(V.tensor_tensor(T[:, t], T[:, t], over_heads(C("incl")), ALU.mult))
                dve.wait_ge(S("kk_qk"), t + 1)
                V.tensor_tensor(QK[pr, t], bk(acc[1], pr), T[pr, t], ALU.mult).then_inc(S("qk_kept"), 1)
                link(V.tensor_tensor(E[pr, t], bk(acc[0], pr), T[pr, t], ALU.mult))
                dve.wait_ge(S("qk_kept"), t + 1)
                dve.sem_inc(S("qk_ready"), 1)
                dve.wait_ge(S("beta_row"), t + 1)
                V.tensor_tensor(E[pr, t], bk(misc[1], pr), E[pr, t], ALU.mult).then_inc(S("e_ready"), 1)
                if t + 1 < NPAIR:
                    spreads(t + 1)
                dve.wait_ge(S("kv_turned"), t + 1)
                for g in range(2):
                    a = V.tensor_tensor(uv[:, t, 4 * g:4 * g + 4, :], bank[6 + g][:, :].rearrange("p (a n) -> p a n", a=4), tok[:, 0, t, 4 * g:4 * g + 4].unsqueeze(2).to_broadcast([P, 4, P]), ALU.mult)
                a.then_inc(S("v_beta"), 1)
            for lv in range(6):
                for t in range(NPAIR):
                    st, pr = lv * NPAIR + t, rows_of(t)
                    dve.wait_ge(S("ax_done"), st + 1)
                    if lv >= 2:
                        dve.wait_ge(S("xt_done"), st - 2 * NPAIR + 1)
                    mask = con[pr, CA["levels"] + lv * CH:CA["levels"] + lv * CH + CH].unsqueeze(1).to_broadcast([pr.stop, HEADS_A, CH])
                    V.tensor_tensor(T[pr, t], bk(acc[st % 2], pr), mask, ALU.mult).then_inc(S("t_ready"), 1)
                for t in range(NPAIR):
                    st, pr = lv * NPAIR + t, rows_of(t)
                    if lv == 0:
                        eye, pair_up = [C(name, pr).unsqueeze(1).to_broadcast([pr.stop, HEADS_A, CH]) for name in ("eye64", "pair_up")]
                        link(V.tensor_tensor(Y[pr, t], E[pr, t], pair_up, ALU.mult))
                        dve.wait_ge(S("t_ready"), st + 1)
                        V.tensor_tensor(X[pr, t], eye, T[pr, t], ALU.subtract)
                        V.tensor_tensor(Y[pr, t], eye, Y[pr, t], ALU.subtract).then_inc(S("xy_ready"), 1)
                        continue
                    product = st - NPAIR
                    dve.wait_ge(S("xt_done"), product + 1)
                    xp, yp = [misc[2 * (product % 2) + n][pr, 0:256].rearrange("p (a b n) -> p a b n", a=HEADS_A, n=1 << lv) for n in range(2)]
                    if lv < 5:
                        x = head_blocks(X[pr, t], lv, 0)
                        V.tensor_tensor(x, x, xp, ALU.subtract)
                    y = head_blocks(Y[pr, t], lv, 1)
                    V.tensor_tensor(y, y, yp, ALU.subtract).then_inc(S("xy_ready"), 1)
            for t in range(NPAIR):
                pr = rows_of(t)
                if t:
                    dve.wait_ge(S("w_done"), 2 * t - 1)
                dve.wait_ge(S("kT_ready"), NPAIR)
                V.tensor_tensor(kbg[pr], kT[pr, t], tok[pr, 12, t, :].unsqueeze(2).to_broadcast([pr.stop, HEADS_A, P]), ALU.mult).then_inc(S("kbg_ready"), 1)
                dve.wait_ge(S("u_done"), t + 1)
                for g in range(2):
                    a = V.tensor_copy(uv[pr, t, 4 * g:4 * g + 4, :], acc[g][pr, :].rearrange("p (a n) -> p a n", a=4))
                a.then_inc(S("u_ready"), 1)
            dve.wait_ge(S("kbg_ready"), NPAIR)
            for t in range(NPAIR):
                pr = rows_of(t)
                a = V.tensor_tensor(kT[pr, t], kT[pr, t], tok[pr, 11, t, :].unsqueeze(2).to_broadcast([pr.stop, HEADS_A, P]), ALU.mult)
            a.then_inc(S("kd_ready"), 1)
            for t in range(NPAIR):
                if t == 0:
                    dve.wait_ge(S("g_row"), NPAIR)
                    dve.wait_ge(S("beta_row"), NPAIR)
                if t == 2:
                    dve.wait_ge(S("eg_row"), 1)
                sp2 = flat(r, 0, 4, D)[:, (t % 2) * 512:(t % 2) * 512 + 512].rearrange("p (a n) -> p a n", a=8)
                V.tensor_tensor(sp2, over_chunk(tok[:, 1, t, :]), over_heads(C("tri64")), ALU.mult).then_inc(S("g_spread2"), 1)
            for c in range(NCH):
                t, rows, cols = chunk_of(c)
                dve.wait_ge(S("eg_exp"), c + 1)
                eg = eg_buf[:, c % 2, :].rearrange("p (a n) -> p a n", a=8)
                V.tensor_copy(eg_last[:, c, :], eg[:, :, CH - 1])
                V.tensor_tensor(kqv[:, 8:16, cols], kqv[:, 8:16, cols], eg, ALU.mult).then_inc(S("qg_ready"), 1)
            for c in range(NCH):
                t, rows, cols = chunk_of(c)
                if c:
                    dve.wait_ge(S("ws_done"), c)
                    for g in range(2):
                        a = V.tensor_tensor(uv[rows, t, 4 * g:4 * g + 4, :], uv[rows, t, 4 * g:4 * g + 4, :], acc[g][rows, :].rearrange("p (a n) -> p a n", a=4), ALU.subtract)
                    a.then_inc(S("v_new"), 1)
                if c < NCH - 1:
                    now, before = states[c % 2], states[(c - 1) % 2]
                    if c:
                        dve.wait_ge(S("o_done"), c)
                        link(V.tensor_tensor(now[:, :, :], before[:, :, :], eg_last[:, c, :].unsqueeze(2).to_broadcast([P, HEADS_A, P]), ALU.mult))
                    dve.wait_ge(S("kv_done"), c + 1)
                    for g in range(2):
                        kv = acc[2 + g][:, :].rearrange("p (a n) -> p a n", a=4)
                        part = now[:, 4 * g:4 * g + 4, :]
                        a = V.tensor_tensor(part, part, kv, ALU.add) if c else V.tensor_copy(part, kv)
                    a.then_inc(S("state_ready"), 1)
                    dve.wait_ge(S("state_ready"), c + 1)
            dve.wait_ge(S("o_copied"), NCH)
            for hd in range(HEADS_A):
                V.scalar_tensor_tensor(out=r[:, hd, 0:N_MIX], in0=kqv[:, hd, LP - N_MIX:LP], scalar=par_col("a_norm", 0), in1=z_gate[:, hd, :], op0=ALU.mult, op1=ALU.mult).then_inc(S("o_times_z"), 1)
            dve.wait_ge(S("o_std"), 1)
            V.reciprocal(rstd[0:8, 0, 0:N_MIX], std[0:8, 0, 0:N_MIX]).then_inc(S("o_rstd"), 1)
            for hd in range(HEADS_A):
                dve.wait_ge(S("o_spread"), hd + 1)
                dve.wait_ge(S("o_times_z"), hd + 1)
                V.tensor_tensor(r[:, hd, 0:N_MIX], r[:, hd, 0:N_MIX], misc[2 + hd % 2][:, 0:N_MIX], ALU.mult).then_inc(S("o_gated"), 1)
            dve.wait_ge(S("o_gated"), HEADS_A)
            x_low(r, N_MIX, 1)

            def residual(u0, N, off):
                def body(u, s, m):
                    dve.wait_ge(S("unit_done"), u + 1)
                    V.scalar_tensor_tensor(out=at(r, m, slice(0, N)), in0=at(h, m, slice(off, off + N)),
                                           scalar=ALPHA, in1=acc[s % RING][:, 0:N], op0=ALU.mult, op1=ALU.add).then_inc(S("acc_used"), 1)
                    ahead(u, s)
                units(dve, u0, 8, body)

            def down_phase(u0, N, off):
                for j in range(2):
                    ahead(u0 + j, u0 + j)
                with dve.Fori(0, (FT - 6) // RING) as i:
                    for b in range(RING):
                        ahead(i * RING + (u0 + 2 + b), u0 + 2 + b)
                for j in range(FT - 4, FT):
                    ahead(u0 + j, u0 + j)
                dve.wait_ge(S("unit_done"), u0 + FT)
                for j, m in enumerate(DOWN_ORDER):
                    V.scalar_tensor_tensor(out=r[:, m, 0:N], in0=h[:, m, off:off + N], scalar=ALPHA, in1=bank[m][:, 0:N], op0=ALU.mult, op1=ALU.add
                                           ).then_inc(S("acc_used"), 1 if j < KT - 1 else FT - KT + 1)

            ups = [0]

            def up_phase(u0, N, conv):
                base = ups[0] * FT
                cbase = sum(up_conv[:ups[0]]) * FT

                def pair(u, s, j):
                    g, sg = s % RING, (s + 1) % RING
                    par = (s - u0) // 2 % 2
                    M = N - 2 if conv is not None else N
                    if conv is not None:
                        dve.wait_ge(S("ffn_tap0"), j + (cbase + 1))
                        c = cv[:, par, 0:M]
                        V.scalar_tensor_tensor(out=c, in0=acc[g][:, 1:N - 1], scalar=par_col(conv, j * 3 + 1), in1=c, op0=ALU.mult, op1=ALU.add).then_inc(S("ffn_tap1"), 1)
                        dve.wait_ge(S("ffn_tap1"), j + (cbase + 1))
                        V.scalar_tensor_tensor(out=c, in0=acc[g][:, 2:N], scalar=par_col(conv, j * 3 + 2), in1=c, op0=ALU.mult, op1=ALU.add).then_inc(S("ffn_taps"), 1)
                    ahead(u, s)
                    dve.wait_ge(S("ffn_silu"), j + (base + 1))
                    dve.wait_ge(S("a_ready"), j + (base + 1))
                    dve.wait_ge(S("unit_done"), u + 2)
                    V.tensor_tensor(av[:, par, 0:M], sl[:, par, 0:M], acc[sg][:, N - M:N], ALU.mult).then_inc(S("ffn_product"), 1)
                    dve.wait_ge(S("ffn_product"), j + (base + 1))
                    dve.sem_inc(S("acc_used"), 2)
                    ahead(u + 1, s + 1)

                with dve.Fori(0, FT // 2) as i:
                    for b in range(2):
                        pair(i * RING + (u0 + 2 * b), u0 + 2 * b, i * 2 + b)
                ups[0] += 1

            residual(U["a_out"], N_MIX, OFF_MIX)
            layer_norm(0, N_MIX)
            up_phase(U["up0"], N_MIX, "f_conv0")
            down_phase(U["down0"], N_FFN0, 2)
            layer_norm(1, N_FFN0)

            def b_tile(u, s, j):
                c, y = cv[:, 0, 0:N_FFN0], cv[:, 1, 0:N_B]
                dve.wait_ge(S("b_c"), j + 1)
                ahead(u, s)
                dve.wait_ge(S("unit_done"), u + 2)
                V.tensor_tensor(c, av[:, 0, 0:N_FFN0], acc[(s + 1) % RING][:, 0:N_FFN0], ALU.mult).then_inc(S("b_cx"), 1)
                dve.wait_ge(S("b_cx"), j + 1)
                V.tensor_scalar(y, c[:, 0:N_B], par_col("b_conv", j * 3), None, ALU.mult).then_inc(S("b_taps"), 1)
                for n in (1, 2):
                    dve.wait_ge(S("b_taps"), j * 3 + n)
                    V.scalar_tensor_tensor(out=y, in0=c[:, n:n + N_B], scalar=par_col("b_conv", j * 3 + n), in1=y, op0=ALU.mult, op1=ALU.add).then_inc(S("b_taps"), 1)
                ahead(u + 1, s + 1)
                dve.wait_ge(S("unit_done"), u + 3)
                dve.wait_ge(S("b_taps"), j * 3 + 3)
                V.tensor_tensor(at(r, j, slice(0, N_B)), y, acc[(s + 2) % RING][:, 2:N_FFN0], ALU.mult).then_inc(S("b_done"), 1)
                dve.wait_ge(S("b_done"), j + 1)
                dve.sem_inc(S("acc_used"), 3)
                ahead(u + 2, s + 2)

            with dve.Fori(0, 2) as i:
                for q in range(4):
                    b_tile(i * 12 + (U["b_in"] + 3 * q), U["b_in"] + 3 * q, i * 4 + q)
            x_low(r, N_B, 2)
            residual(U["b_out"], N_B, 2)
            layer_norm(2, N_B)
            up_phase(U["up1"], N_B, "f_conv1")
            down_phase(U["down1"], SEQ, 2)
            layer_norm(3, SEQ)

            dve.wait_ge(S("p_hi"), 1)
            V.tensor_tensor(p_lo[:, :, :, :], p_raw[:, :, :, :], p_hi[:, :, :, :].bitcast(F32), ALU.subtract).then_inc(S("p_split"), 1)
            rope_rows, swap_rows = slice(64, 96), slice(96, 128)
            ropes = [0]

            def rope(dst, ps):
                n = ropes[0]
                a, b = rope_t[rope_rows, 0, :], rope_t[rope_rows, 1, :]
                V.tensor_tensor(a, ps[swap_rows, 0:SEQ], CBv("rope", swap_rows), ALU.mult)
                V.tensor_tensor(b, ps[rope_rows, 0:SEQ], CBv("rope", rope_rows), ALU.mult).then_inc(S("rope_parts"), 1)
                dve.wait_ge(S("rope_parts"), n + 1)
                ropes[0] += 1
                return V.tensor_tensor(dst, a, b, ALU.add)

            dve.wait_ge(S("con_b_in"), 16)
            for j in range(5):
                u = U["m_in"] + j
                dve.wait_ge(S("unit_done"), u + 1)
                if j < 4:
                    dve.wait_ge(S("c_sq"), j + 1)
                    V.tensor_copy(r[:, j, 0:SEQ], acc[u % RING][:, 0:SEQ]).then_inc(S("acc_used"), 1)
                else:
                    rope(rope_t[rope_rows, 0, :], acc[u % RING]).then_inc(S("acc_used"), 1)
                    dve.wait_ge(S("acc_used"), u + 1)
                    V.tensor_copy(k_m[rope_rows, :, :], rope_t[rope_rows, 0, :].unsqueeze(1).to_broadcast([32, 8, SEQ])).then_inc(S("k_rope"), 1)
                ahead(u, u)
            for j in range(2):
                dve.wait_ge(S("c_std"), j + 1)
                sd = std[:, j, 0:SEQ]
                V.reciprocal(sd, sd).then_inc(S("c_rstd"), 1)
                dve.wait_ge(S("c_rstd"), j + 1)
                for m in range(2):
                    V.scalar_tensor_tensor(out=r[:, 4 + 2 * j + m, 0:SEQ], in0=r[:, 2 * j + m, 0:SEQ], scalar=par_col("q_norm" if j == 0 else "kv_norm", m), in1=sd, op0=ALU.mult, op1=ALU.mult).then_inc(S("c_normed"), 1)
            for j in range(4):
                dve.wait_ge(S("c_hi"), j + 1)
                dve.wait_ge(S("c_normed"), j + 1)
                V.tensor_tensor(c_lo[:, j, :], r[:, 4 + j, 0:SEQ], c_hi[:, j, :].bitcast(F32), ALU.subtract).then_inc(S("c_ready"), 1)
            for j in range(12):
                ahead(U["m_sbqk"] + j, U["m_sbqk"] + j)
            for j in range(2):
                u = U["m_uq"] + j
                dve.wait_ge(S("unit_done"), u + 1)
                for m in range(4):
                    a = rope(q_m[rope_rows, 4 * j + m, :], (acc, misc)[j][m])
                    a.then_inc(S("q_rope"), 1)
                    dve.wait_ge(S("q_rope"), 4 * j + m + 1)
                dve.wait_ge(S("q_nope"), 4 * j + 4)
                dve.sem_inc(S("acc_used"), 1)
                dve.sem_inc(S("uq_read"), 1)
                ahead(u, u)
            ahead(U["m_ukn"], U["m_ukn"])
            ahead(U["m_ukv"], U["m_ukv"])
            dve.wait_ge(S("k_rope"), 1)
            dve.sem_inc(S("m_ready"), 1)

            def softmax_heads(n, base, scale, mask, ob, dcum):
                for hd in range(n + 1):
                    g = base + hd
                    pb = g % 2
                    if hd < n:
                        dve.wait_ge(S("sm_scores"), g + 1)
                        if g >= 2:
                            dve.wait_ge(S("sm_exp"), g - 1)
                        s = smx[:, pb, :]
                        if dcum is None:
                            V.scalar_tensor_tensor(out=s, in0=misc[hd % 2][:, 0:384], scalar=scale, in1=mask, op0=ALU.mult, op1=ALU.add).then_inc(S("sm_masked"), 1)
                        else:
                            V.scalar_tensor_tensor(out=s[:, 0:128], in0=misc[hd % 2][:, 0:128], scalar=dcum[:, 0, hd:hd + 1], in1=mask[:, 0:128], op0=ALU.add, op1=ALU.add)
                            V.scalar_tensor_tensor(out=s[:, 128:384], in0=misc[hd % 2][:, 128:384], scalar=dcum[:, 1, hd:hd + 1], in1=mask[:, 128:384], op0=ALU.add, op1=ALU.add).then_inc(S("sm_masked"), 1)
                        dve.wait_ge(S("sm_masked"), g + 1)
                        V.tensor_reduce(stat[:, pb, 2, 0:1], s[:, 0:128], AX, ALU.max)
                        V.tensor_reduce(stat[:, pb, 2, 1:2], s[:, 128:384], AX, ALU.max).then_inc(S("sm_top"), 1)
                        dve.wait_ge(S("sm_top"), g + 1)
                        V.tensor_scalar(stat[:, pb, 0, :], stat[:, pb, 2, :], -1.0, None, ALU.mult).then_inc(S("sm_max"), 1)
                    if hd >= 1:
                        g, pb = g - 1, (g - 1) % 2
                        dve.wait_ge(S("sm_exp"), g + 1)
                        V.reciprocal(stat[:, pb, 1, :], stat[:, pb, 1, :]).then_inc(S("sm_recip"), 1)
                        dve.wait_ge(S("sm_recip"), g + 1)
                        V.tensor_scalar(prob[:, pb, 0:128], prob[:, pb, 0:128], stat[:, pb, 1, 0:1], None, ALU.mult)
                        V.tensor_scalar(prob[:, pb, 128:384], prob[:, pb, 128:384], stat[:, pb, 1, 1:2], None, ALU.mult).then_inc(S("sm_probs"), 1)
                    if hd >= 5 and hd % 2 == 1:
                        o_low((hd - 5) // 2, ob)
                for m in (n // 2 - 2, n // 2 - 1):
                    o_low(m, ob)

            def o_low(m, ob):
                x_hi_n[0] += 1
                dve.wait_ge(S("x_hi"), x_hi_n[0])
                V.tensor_tensor(x_lo[:, ob + m, 0:SEQ], acc[m % 4][:, 0:SEQ], x_hi[:, ob + m, 0:SEQ].bitcast(F32), ALU.subtract).then_inc(S("o_split"), 1)

            softmax_heads(8, 0, 96.0 ** -0.5, CBv("mla_mask"), 0, None)
            for pair in range(4):
                for hd in (2 * pair, 2 * pair + 1):
                    pb = hd % 2
                    rem = prob[:, pb, :]
                    dve.wait_ge(S("sb_ln"), hd + 1)
                    if hd >= 2:
                        dve.wait_ge(S("sb_sum"), hd - 1)
                    V.scalar_tensor_tensor(out=rem, in0=misc[pb][:, 0:384], scalar=0.0, in1=smx[:, pb, :], op0=ALU.max, op1=ALU.add).then_inc(S("sb_soft"), 1)
                    dve.wait_ge(S("sb_soft"), hd + 1)
                    V.tensor_tensor(rem, rem, CBv("sb_past"), ALU.mult).then_inc(S("sb_rem"), 1)
                if pair:
                    o_low(pair - 1, 4)
                for hd in (2 * pair, 2 * pair + 1):
                    pb = hd % 2
                    dve.wait_ge(S("sb_sum"), hd + 1)
                    if hd >= 2:
                        dve.wait_ge(S("sb_att"), hd - 1)
                    V.scalar_tensor_tensor(out=sb_log[:, pb, :], in0=misc[2 + pb][:, 0:384], scalar=0.0, in1=CBv("sb_mask"), op0=ALU.min, op1=ALU.add).then_inc(S("sb_min"), 1)
            o_low(3, 4)
            dve.wait_ge(S("o_split"), 8)
            dve.sem_inc(S("x_ready"), KT)
            residual(U["m_out"], SEQ, 0)
            layer_norm(4, SEQ)

            def ffn_and_ple(i, n, up, dn, proj, gate):
                up_phase(up, SEQ, None)
                down_phase(dn, SEQ, 0)
                layer_norm(n, SEQ)
                for j in range(2):
                    ahead(proj + j, proj + j)
                for m in range(KT):
                    u = gate + m
                    dve.wait_ge(S("acc_used"), u + 1)
                    g = sl[:, m % 2, 0:SEQ]
                    link(V.tensor_tensor(g, g, pp[:, m, :], ALU.mult))
                    V.tensor_tensor(h[:, m, 0:SEQ], h[:, m, 0:SEQ], g, ALU.add).then_inc(S("ple_h"), 1)
                    ahead(u, u)
                dve.wait_ge(S("ple_h"), KT * (i + 1))

            ffn_and_ple(0, 5, U["up2"], U["down2"], U["proj0"], U["gate0"])
            x_low(h, SEQ, 2)

            ahead(U["f_f"], U["f_f"])
            for j in range(16):
                ahead(U["f_qk"] + j, U["f_qk"] + j)
            dve.wait_ge(S("f_act"), 3)
            link(V.scalar_tensor_tensor(out=fl[0:16, 2, :], in0=fl[0:16, 0, :], scalar=0.0, in1=fl[0:16, 1, :], op0=ALU.min, op1=ALU.subtract))
            link(V.memset(fl[0:16, 0, :], 1.0))
            link(V.tensor_tensor_scan(fl[0:16, 3, :], fl[0:16, 0, :], fl[0:16, 2, :], 0.0, ALU.mult, ALU.add))
            V.tensor_scalar(fl[0:16, 4, :], fl[0:16, 3, :], -1.0, None, ALU.mult).then_inc(S("dcum"), 1)
            for j in range(8):
                ahead(U["f_v"] + j, U["f_v"] + j)
            dve.wait_ge(S("dcum_copied"), 1)
            softmax_heads(16, 8, 1.0, CBv("fox_mask"), 0, dcum_col)
            dve.wait_ge(S("o_split"), 16)
            dve.sem_inc(S("x_ready"), KT)
            residual(U["f_out"], SEQ, 0)
            layer_norm(6, SEQ)
            ffn_and_ple(1, 7, U["up3"], U["down3"], U["proj1"], U["gate1"])

        @block.gpsimd
        def _(pool):
            pool.sem_inc(S("a_ready"), 2)

            def layer_norm(n, N):
                for k in range(KT):
                    pool.wait_ge(S("ln_scaled"), KT * n + k + 1)
                    nc.gpsimd.tensor_scalar(h[:, k, 0:N], r[:, k, 0:N], par_col(f"ln_b{n}", k), None, ALU.add).then_inc(S("ln_h"), 1)

            def low_parts(n, N):
                with pool.Fori(0, FT // 2) as i:
                    for b in range(2):
                        j = i * 2 + b
                        pool.wait_ge(S("a_hi"), j + (n * FT + 1))
                        nc.gpsimd.tensor_tensor(at(a_lo, j, slice(0, N)), av[:, b, 0:N],
                                                at(a_hi, j, slice(0, N)).bitcast(F32), ALU.subtract).then_inc(S("a_ready"), 1)

            layer_norm(0, N_MIX)
            low_parts(0, N_FFN0)
            layer_norm(1, N_FFN0)
            layer_norm(2, N_B)
            low_parts(1, N_FFN1)
            layer_norm(3, SEQ)
            for n in range(2):
                layer_norm(4 + 2 * n, SEQ)
                low_parts(2 + n, SEQ)
                layer_norm(5 + 2 * n, SEQ)


def _constants():
    p, f = np.arange(P)[:, None], np.arange(CH)[None, :]
    pc = p % CH
    a = np.zeros((P, NCA), np.float32)

    def put(into, cols, name, value):
        into[:, cols[name]:cols[name] + value.shape[1]] = value

    full = np.arange(P)[None, :]
    same = p // CH == full // CH
    put(a, CA, "ident", np.eye(P))
    put(a, CA, "ones", np.ones((P, P)))
    put(a, CA, "half_ones", same * 1.0)
    put(a, CA, "half_tri", (same & (p <= full)) * 1.0)
    put(a, CA, "tri64", (pc <= f) * 1.0)
    put(a, CA, "eye64", (pc == f) * 1.0)
    put(a, CA, "incl", (f >= pc) * 1.0)
    levels = [(pc // (2 * s) == f // (2 * s)) & (pc // s % 2 == 1) & (f // s % 2 == 0) for s in (1, 2, 4, 8, 16, 32)]
    put(a, CA, "levels", np.concatenate(levels, 1) * 1.0)
    put(a, CA, "pair_up", ((f == pc + 1) & (pc % 2 == 0)) * 1.0)
    put(a, CA, "one_col", np.repeat(np.arange(31)[None, :] == 15, P, 0) * 1.0)
    put(a, CA, "live0", ((p >= PAD) & (p < CH)) * 1.0)
    b = np.zeros((P, NCB), np.float32)
    zero = np.zeros((P, P))
    blocks = np.where(p // CH >= full // CH, 0.0, NEG)
    put(b, CB, "mla_mask", np.concatenate([blocks, zero, blocks], 1))
    causal = np.where(p >= full, 0.0, NEG)
    put(b, CB, "fox_mask", np.concatenate([causal, zero, causal], 1))
    past = np.where(p < full, 0.0, NEG)
    put(b, CB, "sb_mask", np.concatenate([past, zero, past], 1))
    put(b, CB, "sb_past", np.concatenate([p < full, zero == 0, p < full], 1) * 1.0)
    put(b, CB, "neg_tri", -1.0 * (p >= full))
    put(b, CB, "neg_ones", -np.ones((P, P)))
    dim = 32
    inv = (1.0 / (np.float32(10000.0) ** (np.arange(0, dim, 2, dtype=np.float32) / np.float32(dim)))).astype(np.float32)
    ang = np.arange(SEQ, dtype=np.float32)[None, :] * inv[:, None]
    cos, sin = np.cos(ang).astype(np.float32), np.sin(ang).astype(np.float32)
    rope = np.zeros((P, SEQ), np.float32)
    rope[64:96] = np.concatenate([cos, cos])
    rope[96:128] = np.concatenate([-sin, sin])
    put(b, CB, "rope", rope)
    sel = np.zeros((P, 16, P))
    for hd in range(16):
        sel[hd, hd] = 1.0
    put(b, CB, "sel", sel.reshape(P, 16 * P))
    return a, b


def _stream(v):
    w = np.zeros((NU, P, D), np.float32)

    def panel(u, m):
        t = np.zeros((D, P), np.float32)
        t[:, :m.shape[1]] = m
        w[u] = t.reshape(KT, P, P).transpose(1, 0, 2).reshape(P, D)

    def panels(name, m, first=0, step=1):
        for j in range(m.shape[1] // P):
            panel(U[name] + first + step * j, m[:, j * P:j * P + P])

    def wide(u, m):
        w[u] = m.reshape(2, P, 512).transpose(1, 0, 2).reshape(P, D)

    ain = v["a_w_in"][0]
    ba = np.zeros((D, 64), np.float32)
    ba[:, 0:8], ba[:, 32:40] = ain[:, 4 * D:4 * D + 8], ain[:, 4 * D + 8:4 * D + 16]
    panel(U["ba"], ba)
    panels("kqv", ain[:, D:2 * D])
    panels("kqv", ain[:, 0:D], 8)
    panels("kqv", ain[:, 2 * D:3 * D], 16)
    panels("z", ain[:, 3 * D:4 * D])
    panels("a_out", v["a_w_out"][0])
    for i in range(2):
        panels(f"up{i}", v["ffn_w_up"][i][:, :FF], 0, 2)
        panels(f"up{i}", v["ffn_w_up"][i][:, FF:], 1, 2)
        w[U[f"down{i}"]:U[f"down{i}"] + FT] = v["ffn_w_down"][i].reshape(FT, P, D)
        panels(f"up{i + 2}", v["ffn_w1_2"][i], 0, 2)
        panels(f"up{i + 2}", v["ffn_w3_2"][i], 1, 2)
        w[U[f"down{i + 2}"]:U[f"down{i + 2}"] + FT] = v["ffn_w2_2"][i].reshape(FT, P, D)
        for j in range(2):
            wide(U[f"proj{i}"] + j, v["ple_w_proj_2"][i][:, j * 512:j * 512 + 512])
        panels(f"gate{i}", v["ple_w_gate_2"][i])
    bin_ = v["b_w_in"][0]
    for place, c in enumerate((1, 2, 0)):
        panels("b_in", bin_[:, c * D:c * D + D], place, 3)
    panels("b_out", v["b_w_out"][0])
    m = v["a_w_in_2"][0]
    panels("m_in", m[:, 0:512])
    rope = np.zeros((D, P), np.float32)
    rope[:, 64:96] = m[:, 512:544]
    rope[:, 96:112], rope[:, 112:128] = m[:, 528:544], m[:, 512:528]
    panel(U["m_in"] + 4, rope)
    panels("m_sbqk", m[:, 544:544 + D])
    for j in range(4):
        wide(U["m_sbv"] + j, m[j * 256:j * 256 + 256, 544 + D:])
    uq = v["a_w_uq_2"][0].reshape(256, 8, 96)
    uq = np.concatenate([uq, uq[:, :, 80:96], uq[:, :, 64:80]], 2).reshape(256, D)
    ukv = v["a_w_ukv_2"][0].reshape(256, 8, P)
    for j in range(2):
        wide(U["m_uq"] + j, uq[:, j * 512:j * 512 + 512])
    wide(U["m_ukn"], ukv[:, :, 0:64].reshape(256, 512))
    wide(U["m_ukv"], ukv[:, :, 64:].reshape(256, 512))
    panels("m_out", v["a_w_out_2"][0])
    f = v["c_w_in_2"][0]
    panel(U["f_f"], f[:, 3 * D:])
    panels("f_qk", f[:, 0:2 * D])
    for g in range(2):
        for j in range(4):
            wide(U["f_v"] + 4 * g + j, f[j * 256:j * 256 + 256, 2 * D + g * 512:2 * D + g * 512 + 512])
    panels("f_out", v["c_w_out_2"][0])
    return w


def _parameters(v):
    par = np.zeros((P, NPC), np.float32)

    def put(name, a):
        t = a.reshape(-1, P, a.shape[1]).transpose(1, 0, 2).reshape(P, -1)
        par[:, PC[name]:PC[name] + t.shape[1]] = t

    conv = v["a_conv"][0]
    put("a_conv", np.concatenate([conv[:, D:2 * D], conv[:, 0:D], conv[:, 2 * D:]], 1).T)
    put("b_conv", v["b_conv"][0].T)
    for i in range(2):
        put(f"f_conv{i}", v["ffn_conv"][i].T)
        put(f"ple_b{i}", v["ple_b_gate_2"][i][:, None])
        for n, name in enumerate(("ln_mix", "ln_ffn")):
            put(f"ln_g{2 * i + n}", v[name + "_g"][i][:, None])
            put(f"ln_b{2 * i + n}", v[name + "_b"][i][:, None])
        for n, name in enumerate(("ln1", "ln2")):
            put(f"ln_g{4 + 2 * i + n}", v[name + "_g_2"][i][:, None])
            put(f"ln_b{4 + 2 * i + n}", v[name + "_b_2"][i][:, None])
    put("a_norm", v["a_norm"][0][:, None])
    put("q_norm", v["a_q_norm_2"][0][:, None])
    put("kv_norm", v["a_kv_norm_2"][0][:, None])
    par[0:16, PC["b_f"]] = v["c_b_f_2"][0]
    par[:, PC["a_log"]:PC["a_log"] + 8] = v["a_log"][0][None, :]
    par[:, PC["dt_bias"]:PC["dt_bias"] + 8] = v["a_dt_bias"][0][None, :]
    return par


def kernel(**inputs):
    import concourse.bacc as bacc
    from concourse.bass_utils import run_bass_kernel_spmd

    v = {k: np.asarray(a) for k, a in inputs.items()}
    tokens = np.concatenate([v["meta"], v["x"][0]], 0)
    ca, cb = _constants()
    arrays = {
        "w": _stream(v),
        "h0": np.ascontiguousarray(tokens.T.reshape(KT, P, L).transpose(1, 0, 2)),
        "par": _parameters(v),
        "ca": ca,
        "cb": cb,
        "pin": np.ascontiguousarray(v["p_2"][:, 0].transpose(0, 2, 1).reshape(2, 2, P, SEQ).transpose(2, 0, 1, 3)),
    }
    nc = bacc.Bacc("TRN2", target_bir_lowering=False, num_devices=1)
    args = {k: nc.dram_tensor(k, a.shape, F32, kind="ExternalInput").ap() for k, a in arrays.items()}
    out = nc.dram_tensor("out", (P, KT, SEQ), F32, kind="ExternalOutput").ap()
    build(nc, **args, out=out)
    got = run_bass_kernel_spmd(nc, [arrays], core_ids=[0]).results[0]["out"]
    return np.ascontiguousarray(np.asarray(got).transpose(2, 1, 0).reshape(1, SEQ, D))
```
